# Optimizing a Trainium2 kernel written in Bass

```python
import jax, jax.numpy as jnp
from jax import lax
import numpy as np
import math

D_MODEL = 1024
BATCH = 1
SEQ = 1024
DEPTH = 1

GRID_W = 64
EPS = 1e-6
D_MIX = D_MODEL
NA_HEAD_DIM = 64
NA_WIDTH = D_MIX // 2
NA_HEADS = NA_WIDTH // NA_HEAD_DIM
NA_KH = 8
NA_KW = 16
DN_HEAD_DIM = 128
DN_WIDTH = D_MIX - NA_WIDTH
DN_HEADS = DN_WIDTH // DN_HEAD_DIM
DN_CONV = 5
DN_CHUNK = 64
IN_SIZES = (NA_WIDTH,) * 4 + (DN_WIDTH,) * 4 + (DN_HEADS,) * 4
D_IN = sum(IN_SIZES)


def _rmsnorm(x, w):
    xf = x.astype(jnp.float32)
    y = xf * lax.rsqrt(jnp.mean(xf * xf, axis=-1, keepdims=True) + EPS) * w.astype(jnp.float32)
    return y.astype(x.dtype)

def _l2norm(t):
    return t * lax.rsqrt(jnp.sum(t * t, axis=-1, keepdims=True) + EPS)

def _split_proj(p):
    offsets = [int(o) for o in np.cumsum(IN_SIZES)[:-1]]
    return jnp.split(p, offsets, axis=-1)

def _neighbourhood_attention(q, k, v, rpb):
    B, L, H, Dh = q.shape
    rows = L // GRID_W
    kh = min(NA_KH, rows)
    to_grid = lambda t: t.reshape(B, rows, GRID_W, H, Dh).transpose(0, 3, 1, 2, 4)
    qg, kg, vg = to_grid(q), to_grid(k), to_grid(v)
    cols = np.arange(GRID_W)
    cs = np.clip(cols - NA_KW // 2, 0, GRID_W - NA_KW)
    col_idx = cs[:, None] + np.arange(NA_KW)[None, :]
    col_bias = rpb[:, :, col_idx - cols[:, None] + NA_KW - 1]
    scale = Dh ** -0.5

    def row_fn(r):
        rs = jnp.clip(r - kh // 2, 0, rows - kh)
        q_r = lax.dynamic_index_in_dim(qg, r, axis=2, keepdims=False)
        k_sel = jnp.take(lax.dynamic_slice_in_dim(kg, rs, kh, axis=2), col_idx, axis=3)
        v_sel = jnp.take(lax.dynamic_slice_in_dim(vg, rs, kh, axis=2), col_idx, axis=3)
        dr = rs + jnp.arange(kh) - r + NA_KH - 1
        bias = jnp.take(col_bias, dr, axis=1).transpose(0, 2, 1, 3)
        s = jnp.einsum('bhwd,bhiwjd->bhwij', q_r, k_sel).astype(jnp.float32) * scale + bias.astype(jnp.float32)
        p = jax.nn.softmax(s.reshape(B, H, GRID_W, kh * NA_KW), axis=-1).reshape(s.shape).astype(v.dtype)
        return jnp.einsum('bhwij,bhiwjd->bhwd', p, v_sel)

    o = lax.map(row_fn, jnp.arange(rows))
    return o.transpose(1, 0, 3, 2, 4).reshape(B, L, H * Dh)

def _centred_depthwise_conv(x, w):
    c = x.shape[-1]
    return lax.conv_general_dilated(
        x, w[:, None, :].astype(x.dtype), window_strides=(1,),
        padding=[(DN_CONV // 2, DN_CONV // 2)],
        dimension_numbers=('NWC', 'WIO', 'NWC'), feature_group_count=c)

def _gated_delta_chunked(q, k, v, g, beta):
    B, H, L, Dk = q.shape
    Dv = v.shape[-1]
    C = DN_CHUNK
    N = L // C
    q = q * (Dk ** -0.5)
    ch = lambda t: t.reshape((B, H, N, C) + t.shape[3:])
    q, k, v, g, beta = ch(q), ch(k), ch(v), ch(g), ch(beta)
    g = jnp.cumsum(g, axis=-1)
    tri = np.tril(np.ones((C, C), dtype=bool))
    strict = np.tril(np.ones((C, C), dtype=bool), -1)
    diff = g[..., :, None] - g[..., None, :]
    decay = jnp.where(tri, jnp.exp(jnp.where(tri, diff, 0.0)), 0.0)
    kb = k * beta[..., None]
    a_mat = jnp.where(strict, jnp.einsum('bhncd,bhnsd->bhncs', kb, k) * decay, 0.0) + jnp.eye(C, dtype=jnp.float32)
    rhs = jnp.concatenate([v * beta[..., None], kb * jnp.exp(g)[..., None]], axis=-1)
    sol = lax.linalg.triangular_solve(a_mat, rhs, left_side=True, lower=True, unit_diagonal=True)
    u, w = sol[..., :Dv], sol[..., Dv:]
    intra = jnp.einsum('bhncd,bhnsd->bhncs', q, k) * decay

    def step(S, inp):
        q_c, k_c, u_c, w_c, g_c, a_c = inp
        v_new = u_c - jnp.einsum('bhcd,bhde->bhce', w_c, S)
        o = jnp.einsum('bhcd,bhde->bhce', q_c * jnp.exp(g_c)[..., None], S) + jnp.einsum('bhcs,bhse->bhce', a_c, v_new)
        g_last = g_c[..., -1]
        S = S * jnp.exp(g_last)[..., None, None] + jnp.einsum(
            'bhcd,bhce->bhde', k_c * jnp.exp(g_last[..., None] - g_c)[..., None], v_new)
        return S, o

    xs = tuple(jnp.moveaxis(t, 2, 0) for t in (q, k, u, w, g, intra))
    S0 = jnp.zeros((B, H, Dk, Dv), jnp.float32)
    _, o = lax.scan(step, S0, xs)
    return jnp.moveaxis(o, 0, 2).reshape(B, H, L, Dv)

def _layer(x, norm_w, w_in, qk_gain_q, qk_gain_k, rpb, conv_w, a_log, dt_bias, dn_norm_w, w_out):
    B, L, _ = x.shape
    h = _rmsnorm(x, norm_w)
    proj = jnp.einsum('bld,de->ble', h, w_in)
    aq, ak, av, az, dq, dk, dv, dz, b_f, a_f, b_b, a_b = _split_proj(proj)
    heads = lambda t, n: t.reshape(B, L, n, -1)

    aq = _rmsnorm(heads(aq, NA_HEADS), qk_gain_q)
    ak = _rmsnorm(heads(ak, NA_HEADS), qk_gain_k)
    attn = _neighbourhood_attention(aq, ak, heads(av, NA_HEADS), rpb) * jax.nn.silu(az)

    qkv = jax.nn.silu(_centred_depthwise_conv(jnp.concatenate([dq, dk, dv], axis=-1), conv_w))
    dq, dk, dv = jnp.split(qkv, 3, axis=-1)
    to_bhld = lambda t: heads(t, DN_HEADS).astype(jnp.float32).transpose(0, 2, 1, 3)
    dq, dk, dv = _l2norm(to_bhld(dq)), _l2norm(to_bhld(dk)), to_bhld(dv)

    def gates(b, a, d):
        beta = jax.nn.sigmoid(b.astype(jnp.float32))
        g = -jnp.exp(a_log[d].astype(jnp.float32)) * jax.nn.softplus(a.astype(jnp.float32) + dt_bias[d].astype(jnp.float32))
        return g.transpose(0, 2, 1), beta.transpose(0, 2, 1)

    g_f, beta_f = gates(b_f, a_f, 0)
    g_b, beta_b = gates(b_b, a_b, 1)
    flip = lambda t: jnp.flip(t, axis=2)
    o_f = _gated_delta_chunked(dq, dk, dv, g_f, beta_f)
    o_b = flip(_gated_delta_chunked(flip(dq), flip(dk), flip(dv), flip(g_b), flip(beta_b)))
    o = (o_f + o_b).transpose(0, 2, 1, 3)
    o = o * lax.rsqrt(jnp.mean(o * o, axis=-1, keepdims=True) + EPS) * dn_norm_w.astype(jnp.float32)
    o = o * jax.nn.silu(heads(dz, DN_HEADS).astype(jnp.float32))
    delta = o.reshape(B, L, DN_WIDTH).astype(x.dtype)

    y = jnp.einsum('ble,ed->bld', jnp.concatenate([attn, delta], axis=-1), w_out)
    return x + y

def first_inputs(seed: int = 0) -> dict:
    key = jax.random.key(seed)
    ks = jax.random.split(key, 12)
    f32 = jnp.float32
    x = jax.random.normal(ks[0], (BATCH, SEQ, D_MODEL), f32)
    norm_w = 1.0 + 0.02 * jax.random.normal(ks[1], (DEPTH, D_MODEL), f32)
    w_in = jax.random.normal(ks[2], (DEPTH, D_MODEL, D_IN), f32) * D_MODEL ** -0.5
    qk_gain_q = 1.0 + 0.02 * jax.random.normal(ks[3], (DEPTH, NA_HEAD_DIM), f32)
    qk_gain_k = 1.0 + 0.02 * jax.random.normal(ks[4], (DEPTH, NA_HEAD_DIM), f32)
    rpb = 0.02 * jax.random.normal(ks[5], (DEPTH, NA_HEADS, 2 * NA_KH - 1, 2 * NA_KW - 1), f32)
    conv_w = jax.random.normal(ks[6], (DEPTH, DN_CONV, 3 * DN_WIDTH), f32) * DN_CONV ** -0.5
    a_log = jnp.log(jax.random.uniform(ks[7], (DEPTH, 2, DN_HEADS), f32, 1.0, 16.0))
    u = jax.random.uniform(ks[8], (DEPTH, 2, DN_HEADS), f32)
    dt = jnp.exp(u * (jnp.log(0.1) - jnp.log(0.001)) + jnp.log(0.001))
    dt_bias = dt + jnp.log(-jnp.expm1(-dt))
    dn_norm_w = 1.0 + 0.02 * jax.random.normal(ks[9], (DEPTH, DN_HEAD_DIM), f32)
    w_out = jax.random.normal(ks[10], (DEPTH, D_MIX, D_MODEL), f32) * D_MIX ** -0.5
    return {'x': x, 'norm_w': norm_w, 'w_in': w_in, 'qk_gain_q': qk_gain_q, 'qk_gain_k': qk_gain_k,
            'rpb': rpb, 'conv_w': conv_w, 'a_log': a_log, 'dt_bias': dt_bias,
            'dn_norm_w': dn_norm_w, 'w_out': w_out}

def first_block(x, norm_w, w_in, qk_gain_q, qk_gain_k, rpb, conv_w, a_log, dt_bias, dn_norm_w, w_out):
    for l in range(DEPTH):
        x = _layer(x, norm_w[l], w_in[l], qk_gain_q[l], qk_gain_k[l], rpb[l], conv_w[l],
                   a_log[l], dt_bias[l], dn_norm_w[l], w_out[l])
    return x


MIX_WIDTH = D_MODEL
FNET_WIDTH = MIX_WIDTH // 2
FNET_GROUPS = 4
FNET_GROUP_DIM = FNET_WIDTH // FNET_GROUPS
HEAD_DIM = 64
N_Q_HEADS = (MIX_WIDTH - FNET_WIDTH) // HEAD_DIM
N_KV_HEADS = 2
GQA_GROUP = N_Q_HEADS // N_KV_HEADS
ATTN_WIDTH = N_Q_HEADS * HEAD_DIM
KV_WIDTH = N_KV_HEADS * HEAD_DIM
IN_WIDTH = FNET_WIDTH + ATTN_WIDTH + 2 * KV_WIDTH
D_FF = 2752
AXIS_DIM = HEAD_DIM // 2
ROPE_THETA = 10000.0
Q_BLOCK = 128


def rms_norm(x, g):
    xf = x.astype(jnp.float32)
    y = xf * lax.rsqrt(jnp.mean(xf * xf, axis=-1, keepdims=True) + EPS)
    return (y * g.astype(jnp.float32)).astype(x.dtype)

def swiglu(h, w_gate, w_up, w_down):
    return (jax.nn.silu(h @ w_gate) * (h @ w_up)) @ w_down

def axial_rope_tables(seq):
    rows = seq // GRID_W
    row_idx = jnp.repeat(jnp.arange(rows, dtype=jnp.float32), GRID_W)
    col_idx = jnp.tile(jnp.arange(GRID_W, dtype=jnp.float32), rows)
    inv_freq = ROPE_THETA ** (-jnp.arange(0, AXIS_DIM, 2, dtype=jnp.float32) / AXIS_DIM)
    ang_r = row_idx[:, None] * inv_freq[None, :]
    ang_c = col_idx[:, None] * inv_freq[None, :]
    return jnp.cos(ang_r), jnp.sin(ang_r), jnp.cos(ang_c), jnp.sin(ang_c)

def rotate(x, cos, sin):
    half = x.shape[-1] // 2
    x1, x2 = x[..., :half], x[..., half:]
    c = cos[None, :, None, :].astype(x.dtype)
    s = sin[None, :, None, :].astype(x.dtype)
    return jnp.concatenate([x1 * c - x2 * s, x1 * s + x2 * c], axis=-1)

def apply_axial_rope(x, tables):
    cr, sr, cc, sc = tables
    return jnp.concatenate([rotate(x[..., :AXIS_DIM], cr, sr),
                            rotate(x[..., AXIS_DIM:], cc, sc)], axis=-1)

def fourier_mixer(hf, fnet_w, fnet_b):
    b, s, _ = hf.shape
    g = hf.reshape(b, s, FNET_GROUPS, FNET_GROUP_DIM).astype(jnp.float32)
    mixed = jnp.real(jnp.fft.fft2(g, axes=(1, 3), norm="ortho")).astype(hf.dtype)
    out = jnp.einsum('bsgc,gcd->bsgd', mixed, fnet_w) + fnet_b[None, None]
    return out.reshape(b, s, FNET_WIDTH)

def gqa_attention(q, k, v, q_norm, k_norm):
    b, s, _ = q.shape
    q = rms_norm(q.reshape(b, s, N_Q_HEADS, HEAD_DIM), q_norm)
    k = rms_norm(k.reshape(b, s, N_KV_HEADS, HEAD_DIM), k_norm)
    v = v.reshape(b, s, N_KV_HEADS, HEAD_DIM)
    tables = axial_rope_tables(s)
    q = apply_axial_rope(q, tables)
    k = apply_axial_rope(k, tables)
    scale = 1.0 / math.sqrt(HEAD_DIM)
    n_blocks = s // Q_BLOCK
    qb = q.reshape(b, n_blocks, Q_BLOCK, N_KV_HEADS, GQA_GROUP, HEAD_DIM)
    qb = jnp.moveaxis(qb, 1, 0)

    def attend_block(q_blk):
        scores = jnp.einsum('bqhgd,bkhd->bhgqk', q_blk, k).astype(jnp.float32) * scale
        p = jax.nn.softmax(scores, axis=-1).astype(v.dtype)
        return jnp.einsum('bhgqk,bkhd->bqhgd', p, v)

    o = lax.map(attend_block, qb)
    o = jnp.moveaxis(o, 0, 1)
    return o.reshape(b, s, ATTN_WIDTH)

def second_inputs(seed: int = 0) -> dict:
    key = jax.random.key(seed)
    ks = jax.random.split(key, 20)
    D, F = D_MODEL, D_FF
    nrm = lambda k, shape, fan_in: jax.random.normal(k, shape, jnp.float32) * fan_in ** -0.5
    gain = lambda k, n: 1.0 + 0.05 * jax.random.normal(k, (n,), jnp.float32)
    return {
        "x": jax.random.normal(ks[0], (BATCH, SEQ, D), jnp.float32),
        "ffn1_norm": gain(ks[1], D),
        "ffn1_w_gate": nrm(ks[2], (D, F), D),
        "ffn1_w_up": nrm(ks[3], (D, F), D),
        "ffn1_w_down": nrm(ks[4], (F, D), F),
        "mix_norm": gain(ks[5], D),
        "w_in": nrm(ks[6], (D, IN_WIDTH), D),
        "fnet_w": nrm(ks[7], (FNET_GROUPS, FNET_GROUP_DIM, FNET_GROUP_DIM), FNET_GROUP_DIM),
        "fnet_b": 0.02 * jax.random.normal(ks[8], (FNET_GROUPS, FNET_GROUP_DIM), jnp.float32),
        "q_norm": gain(ks[9], HEAD_DIM),
        "k_norm": gain(ks[10], HEAD_DIM),
        "w_out": nrm(ks[11], (MIX_WIDTH, D), MIX_WIDTH),
        "ffn2_norm": gain(ks[12], D),
        "ffn2_w_gate": nrm(ks[13], (D, F), D),
        "ffn2_w_up": nrm(ks[14], (D, F), D),
        "ffn2_w_down": nrm(ks[15], (F, D), F),
        "final_norm": gain(ks[16], D),
    }

def second_block(x, ffn1_norm, ffn1_w_gate, ffn1_w_up, ffn1_w_down, mix_norm, w_in,
              fnet_w, fnet_b, q_norm, k_norm, w_out, ffn2_norm, ffn2_w_gate,
              ffn2_w_up, ffn2_w_down, final_norm):
    for _ in range(DEPTH):
        x = x + 0.5 * swiglu(rms_norm(x, ffn1_norm), ffn1_w_gate, ffn1_w_up, ffn1_w_down)
        h = rms_norm(x, mix_norm)
        u = h @ w_in
        o0 = FNET_WIDTH
        o1 = o0 + ATTN_WIDTH
        o2 = o1 + KV_WIDTH
        f_out = fourier_mixer(u[..., :o0], fnet_w, fnet_b)
        a_out = gqa_attention(u[..., o0:o1], u[..., o1:o2], u[..., o2:], q_norm, k_norm)
        x = x + jnp.concatenate([f_out, a_out], axis=-1) @ w_out
        x = x + 0.5 * swiglu(rms_norm(x, ffn2_norm), ffn2_w_gate, ffn2_w_up, ffn2_w_down)
    return rms_norm(x, final_norm)


def setup_inputs(seed=0):
    out = dict(first_inputs(seed))
    for name, value in second_inputs(seed + 1).items():
        if name != "x":
            out[name + "_2"] = value
    return out


def reference(
    x, norm_w, w_in, qk_gain_q, qk_gain_k, rpb, conv_w, a_log, dt_bias, dn_norm_w, w_out,
    ffn1_norm_2, ffn1_w_gate_2, ffn1_w_up_2, ffn1_w_down_2, mix_norm_2, w_in_2, fnet_w_2,
    fnet_b_2, q_norm_2, k_norm_2, w_out_2, ffn2_norm_2, ffn2_w_gate_2, ffn2_w_up_2,
    ffn2_w_down_2, final_norm_2,
):
    x = first_block(
        x, norm_w, w_in, qk_gain_q, qk_gain_k, rpb, conv_w, a_log, dt_bias, dn_norm_w, w_out,
    )
    return second_block(
        x, ffn1_norm_2, ffn1_w_gate_2, ffn1_w_up_2, ffn1_w_down_2, mix_norm_2, w_in_2, fnet_w_2,
        fnet_b_2, q_norm_2, k_norm_2, w_out_2, ffn2_norm_2, ffn2_w_gate_2, ffn2_w_up_2,
        ffn2_w_down_2, final_norm_2,
    )


_drawn_inputs = setup_inputs


def setup_inputs(seed=0):
    import zlib

    import numpy as np

    out = dict(_drawn_inputs(seed))
    spreads = {}
    factors = {'norm_w': 4.018,
     'qk_gain_q': 8.0,
     'qk_gain_k': 8.0,
     'rpb': 24.357,
     'dn_norm_w': 6.159,
     'ffn1_norm_2': 2.84,
     'mix_norm_2': 2.731,
     'fnet_b_2': 40.096,
     'q_norm_2': 8.0,
     'k_norm_2': 8.0,
     'ffn2_norm_2': 10.456}
    for name, (base, spread) in spreads.items():
        noise = np.random.default_rng([zlib.crc32(name.encode()), seed]).standard_normal(out[name].shape)
        drawn = base * np.exp(spread * noise) if base else spread * noise
        out[name] = __import__('jax').numpy.asarray(drawn.astype(out[name].dtype))
    for name, factor in factors.items():
        out[name] = (out[name] * factor).astype(out[name].dtype)
    return out
```

```python
import numpy as np
from contextlib import ExitStack

L = 1024
D = 1024
KC = D // 128
FF = 2752
FT = 22
GROUPS = [4, 4, 4, 4, 3, 3]
EPS = 1e-6
N_INPROJ = 33
NEG = -1.0e30


def const_columns():
    cols = {}
    at = 0
    for name, n in [("norm1", 8), ("ffn1", 8), ("mixn", 8), ("ffn2", 8), ("fin", 8), ("gq", 1), ("gk", 1),
                    ("qn", 1), ("kn", 1), ("conv", 60), ("alog", 1), ("dtb", 1), ("dnw", 1), ("fb", 4),
                    ("eps", 1), ("eps64", 1), ("eps128", 1), ("one", 1),
                    ("ident", 128), ("ones", 128), ("bones", 128)]:
        cols[name] = (at, n)
        at += n
    return cols, at


class Mark:
    __slots__ = ("q", "need", "sem", "val")

    def __init__(self, q=None, sem=None, val=0):
        self.q, self.need, self.sem, self.val = q, False, sem, val


class Queue:
    def __init__(self, sem):
        self.sem, self.items = sem, []

    def __call__(self, fn, *after):
        m = Mark(self)
        self.items.append((flat(after), fn, m))
        return m

    def last(self):
        for _, fn, m in reversed(self.items):
            if fn is not None and m.q is not None:
                return m
        return None

    def number(self):
        n = 0
        for _, _, m in self.items:
            if m.q is not None and m.need:
                n += 1
                m.sem, m.val = self.sem, n

    def emit(self, eng):
        seen = {}
        for after, fn, m in self.items:
            want = {}
            for a in after:
                k = id(a.sem)
                if a.val > seen.get(k, 0) and a.val > want.get(k, (0, None))[0]:
                    want[k] = (a.val, a.sem)
            for k, (v, s) in want.items():
                eng.wait_ge(s, v)
                seen[k] = v
            if fn is None:
                continue
            ins = fn(eng)
            if m.q is None:
                ins.then_inc(m.sem, 16)
            elif m.need:
                ins.then_inc(self.sem, 1)


def flat(after):
    out = []
    for a in after:
        if a is None:
            continue
        if isinstance(a, (list, tuple)):
            out += flat(a)
        else:
            a.need = True
            out.append(a)
    return out


class DmaSem:

    def __init__(self, sem):
        self.sem, self.n = sem, 0

    def start(self, q, fn, *after):
        self.n += 16
        m = Mark(None, self.sem, self.n)
        q.items.append((flat(after), fn, m))
        return m


class Ring:

    def __init__(self, bufs):
        self.bufs, self.free, self.busy, self.i = bufs, [[] for _ in bufs], [False] * len(bufs), 0

    def take(self):
        i = self.i
        assert not self.busy[i], "taken before it was given back"
        self.i = (i + 1) % len(self.bufs)
        self.busy[i] = True
        return i, self.bufs[i], self.free[i]

    def give(self, i, *marks):
        assert self.busy[i]
        self.busy[i], self.free[i] = False, list(marks)


def build(nc, A):
    import concourse.bass as bass
    from concourse import mybir

    F = mybir.dt.float32
    R = mybir.dt.float32r
    ACT = mybir.ActivationFunctionType
    ALU = mybir.AluOpType
    AX = mybir.AxisListType.X
    MUL, ADD, SUB = ALU.mult, ALU.add, ALU.subtract

    cols, ncst = const_columns()
    top = ExitStack()
    sem = lambda n: top.enter_context(nc.semaphore(n))
    pe, act, dve, pool, sp = (Queue(sem("s_" + n)) for n in ("pe", "act", "dve", "pool", "sp"))
    engines = [pe, act, dve, pool]
    dsems = {}

    def dsem(name):
        if name not in dsems:
            dsems[name] = DmaSem(sem("d_" + name))
        return dsems[name]

    out_marks = []
    phase_dmas = []

    def load(name, dst, src, *after):
        m = dsem(name).start(sp, lambda e: e.dma_start(dst, src), *after)
        phase_dmas.append(m)
        return m

    def store(name, dst, src, *after):
        m = load(name, dst, src, *after)
        out_marks.append(m)
        return m

    def fence():
        marks = [q.last() for q in engines] + list(phase_dmas)
        phase_dmas.clear()
        for q in engines + [sp]:
            q.items.append((flat(marks), None, Mark(q)))

    names = [0]

    def sb(stack, shape, dt=F):
        names[0] += 1
        return stack.enter_context(nc.sbuf_tensor(f"t{names[0]}", shape, dt))

    scr = lambda n, shape: nc.dram_tensor(n, shape, F, kind="Internal").ap()
    pj = scr("pj", (N_INPROJ, 128, L))
    mixd = scr("mixd", (8, 128, L))
    mixd2 = scr("mixd2", (8, 128, L))

    ps = top.enter_context(nc.psum_tensor("ps", [128, 8, 512], F))
    slot = lambda s: ps[:, 2 * s:2 * s + 2, :].rearrange("p a n -> p (a n)")
    slots = Ring([slot(s) for s in range(4)])

    cst = sb(top, [128, ncst])
    cm = load("cst", cst[:], A["cst"])
    C = lambda n, i=0, w=1: cst[:, cols[n][0] + i:cols[n][0] + i + w]
    IDENT = C("ident", 0, 128)
    ONES = C("ones", 0, 128)
    BONES = C("bones", 0, 128)
    for q in engines:
        q.items.append((flat([cm]), None, Mark(q)))

    def mm(out, lhsT, rhs, start, stop, *after):
        return pe(lambda e: e.matmul(out, lhsT, rhs, start=start, stop=stop), *after)

    def tr(out, in_, *after, n=128, ident=None):
        idn = IDENT[0:n, 0:n] if ident is None else ident
        return pe(lambda e: e.transpose(out, in_, idn), *after)

    def mm3(out, A_, B_, start, stop, *after):
        (ah, al), (bh, bl) = A_, B_
        mm(out, ah, bh, start, False, *after)
        mm(out, ah, bl, False, False)
        return mm(out, al, bh, False, stop)

    def actf(out, in_, fn, *after, scale=1.0, bias=None, accum=None):
        kw = {}
        if bias is not None:
            kw["bias"] = bias
        if accum is not None:
            kw["accum_out"] = accum
        return act(lambda e: e.activation(out, in_, fn, scale=scale, **kw), *after)

    def tt(q, out, a, b, op, *after):
        return q(lambda e: e.tensor_tensor(out, a, b, op), *after)

    def ts(q, out, a, s1, s2, op0, op1, *after):
        if op1 is None:
            return q(lambda e: e.tensor_scalar(out, a, s1, None, op0), *after)
        return q(lambda e: e.tensor_scalar(out, a, s1, s2, op0, op1), *after)

    def stt(out, a, s, b, op0, op1, *after):
        return dve(lambda e: e.scalar_tensor_tensor(out, a, s, b, op0, op1), *after)

    def recip(out, a, *after):
        return dve(lambda e: e.reciprocal(out, a), *after)

    def copy(q, out, a, *after):
        if q is act:
            return actf(out, a, ACT.Copy, *after)
        return q(lambda e: e.tensor_copy(out, a), *after)

    def memset(q, out, v, *after):
        return q(lambda e: e.memset(out, v), *after)

    def split(hi, lo, src, *after, q=pool):
        a = actf(hi, src, ACT.Copy, *after)
        b = tt(q, lo, src, hi.bitcast(F), SUB, a, *after)
        return [a, b]

    def split_psum(parts, *after):
        for hi, lo, src in parts:
            a = actf(hi, src, ACT.Copy, *after)
        for hi, lo, src in parts:
            b = tt(dve, lo, src, hi.bitcast(F), SUB, a, *after)
        return [a, b]

    class Weights:
        NR, NS, AHEAD = 4, 3, 2

        def __init__(self):
            self.next = self.raws = self.splits = 0

        def open(self, stack, limit):
            self.limit = limit
            self.raw = Ring([sb(stack, [128, 1024]) for _ in range(self.NR)])
            self.sp = Ring([(sb(stack, [128, 1024], R), sb(stack, [128, 1024], R)) for _ in range(self.NS)])
            self.rawq, self.spq = [], []
            self.pump()

        def pump(self):
            while self.raws < min(self.next + self.NR, self.limit) and self.raws < self.splits + self.NR:
                n = self.raws
                i, buf, free = self.raw.take()
                m = dsem(f"w{i}").start(sp, lambda e, b=buf, n=n: e.dma_start(b[:], A["wts"][n]), *free)
                self.rawq.append((i, buf, m))
                self.raws += 1

        def split_one(self):
            i, buf, m = self.rawq.pop(0)
            k, (hi, lo), free = self.sp.take()
            marks = split(hi[:], lo[:], buf[:], m, free)
            self.raw.give(i, *marks)
            self.spq.append((k, hi, lo, marks))
            self.splits += 1
            self.pump()

        def get(self):
            while self.splits <= min(self.next + self.AHEAD, self.limit - 1):
                self.split_one()
            k, hi, lo, marks = self.spq.pop(0)
            self.next += 1
            self.k = k
            return hi, lo, marks

        def done(self, m):
            self.sp.give(self.k, m)

    W = Weights()

    def linear_tile(H, Lo, hready):
        wh, wl, wm = W.get()
        s, p, free = slots.take()
        for half in range(2):
            o = p[:, half * 512:half * 512 + 512]
            b = slice(half * 512, half * 512 + 512)
            for k in range(KC):
                a = slice(k * 128, k * 128 + 128)
                last = mm3(o, (wh[:, a], wl[:, a]), (H[:, k, b], Lo[:, k, b]), k == 0, k == KC - 1,
                           wm, free, hready[k])
        W.done(last)
        return s, p, last

    def rmsnorm(x, wname, xready, sink, stack):
        sq = Ring([sb(stack, [128, L]) for _ in range(2)])
        rs = sb(stack, [128, L])
        tmp = Ring([sb(stack, [128, L]) for _ in range(2)])
        s, p, free = slots.take()
        for k in range(KC):
            i, b, f = sq.take()
            a = actf(b[:], x[:, k, :], ACT.Square, xready[k], f)
            for half in range(2):
                c = slice(half * 512, half * 512 + 512)
                m = mm(p[:, c], ONES, b[:, c], k == 0, k == KC - 1, a, free)
            sq.give(i, m)
        a = actf(rs[:], p, ACT.Sqrt, m, scale=1.0 / D, bias=C("eps"))
        slots.give(s, a)
        r = recip(rs[:], rs[:], a)
        for k in range(KC):
            i, b, f = tmp.take()
            m = stt(b[:], x[:, k, :], C(wname, k), rs[:], MUL, MUL, r, xready[k], f)
            tmp.give(i, *sink(k, b, m))

    def norm_split(x, wname, xready, H, Lo, stack):
        ready = [None] * KC

        def sink(k, b, m):
            ready[k] = split(H[:, k, :], Lo[:, k, :], b[:], m)
            return ready[k]

        rmsnorm(x, wname, xready, sink, stack)
        return ready

    def phase_inproj():
        with ExitStack() as st:
            W.open(st, N_INPROJ)
            H, Lo = sb(st, [128, KC, L], R), sb(st, [128, KC, L], R)
            with ExitStack() as s2:
                x = sb(s2, [128, KC, L])
                xm = [load(f"x{k}", x[:, k, :], A["xT"][k]) for k in range(KC)]
                ready = norm_split(x, "norm1", xm, H, Lo, s2)
                ev = Ring([sb(s2, [128, L]) for _ in range(3)])
                for m in range(N_INPROJ):
                    s, p, done = linear_tile(H, Lo, ready)
                    i, b, f = ev.take()
                    c = copy(dve if m % 2 else act, b[:], p, done, f)
                    slots.give(s, c)
                    ev.give(i, store(f"ev{i}", pj[m], b[:], c))
            fence()

    def head_norm(st_rings, raw, gain, epsname, scale, mraw, hi, lo, free, rope=None):
        big, = st_rings
        i1, sqb, f1 = big.take()
        a = actf(sqb[:], raw, ACT.Square, mraw, f1)
        s, p, fr = slots_s.take()
        for half in range(2):
            c = slice(half * 512, half * 512 + 512)
            m = mm(p[:, c], BONES, sqb[:, c], True, True, a, fr)
        a = actf(sqb[:], p, ACT.Sqrt, m, scale=scale, bias=C(epsname))
        slots_s.give(s, a)
        r = recip(sqb[:], sqb[:], a)
        i2, qn, f2 = big.take()
        m = stt(qn[:], raw, C(gain), sqb[:], MUL, MUL, r, f2)
        if rope is None:
            marks = split(hi[:], lo[:], qn[:], m, free)
            big.give(i1, m)
            big.give(i2, *marks)
            return marks, m
        cos, sin, rp = rope
        s, p, fr = slots_s.take()
        for half in range(2):
            c = slice(half * 512, half * 512 + 512)
            m2 = mm(p[:, c], rp, qn[:, c], True, True, m, fr)
        a1 = tt(dve, sqb[:], p, sin, MUL, m2)
        slots_s.give(s, a1)
        a2 = tt(pool, qn[:], qn[:], cos, MUL, m2)
        a3 = tt(dve, qn[:], qn[:], sqb[:], ADD, a1, a2)
        marks = split(hi[:], lo[:], qn[:], a3, free)
        big.give(i1, a3)
        big.give(i2, *marks)
        return marks, m

    slots_s = None

    def value_tiles(vraw, vm, VH, VL, free):
        s, p, fr = slots_s.take()
        for t in range(8):
            m = tr(p[:, t * 128:t * 128 + 128], vraw[:, t * 128:t * 128 + 128], vm, fr)
        pv = p.rearrange("p (t f) -> p t f", t=8)
        cs = [slice(64 * j, 64 * j + 64) for j in range(2)]
        marks = split_psum([(VH[:, :, j, cs[j]], VL[:, :, j, cs[j]], pv[:, :, cs[j]]) for j in range(2)], m, free)
        slots_s.give(s, *marks)
        return marks

    def value_ones(VH, VL, one, zero, ready):
        marks = []
        for j in range(2):
            c = slice(64 * (1 - j), 64 * (1 - j) + 64)
            marks.append(copy(act, VH[:, :, j, c], one, ready))
            marks.append(copy(act, VL[:, :, j, c], zero, ready))
        return marks

    def attention(units, st, prep_at):
        P = Ring([sb(st, [128, L]) for _ in range(2)])
        PT = Ring([(sb(st, [128, L], R), sb(st, [128, L], R)) for _ in range(2)])
        nmx = Ring([sb(st, [128, 2]) for _ in range(4)])
        rec = sb(st, [128, L])
        tslot, oslot = Ring([slot(2)]), Ring([slot(3)])
        state = {}

        def scores(u):
            s, p, fr = slots_s.take()
            j, t, nk, k0 = u["j"], u["t"], u["nk"], u["k0"]
            r = slice(64 * j, 64 * j + 64)
            qh, ql = u["q"]
            kh, kl = u["k"]
            for c in range(0, nk, 512):
                w = min(512, nk - c)
                m = mm3(p[:, c:c + w], (qh[r, t * 128:t * 128 + 128], ql[r, t * 128:t * 128 + 128]),
                        (kh[r, k0 + c:k0 + c + w], kl[r, k0 + c:k0 + c + w]), True, True, fr, u["ready"]())
            i, pb, f = P.take()
            n, mx, fn_ = nmx.take()
            if u["bias"] is not None:
                b, bm = u["bias"]
                a = dve(lambda e: e.tensor_tensor_reduce(pb[:, 0:nk], p[:, 0:nk], b, 1.0, NEG, ADD, ALU.max,
                                                         mx[:, 1:2]), m, f, fn_, bm)
                a2 = ts(dve, mx[:, 0:1], mx[:, 1:2], -1.0, None, MUL, None, a)
                e_ = actf(pb[:, 0:nk], pb[:, 0:nk], ACT.Exp, a2, bias=mx[:, 0:1])
                slots_s.give(s, a)
                u["bias_done"](a)
            else:
                a2 = dve(lambda e: e.tensor_reduce(mx[:, 0:1], p[:, 0:nk], AX, ALU.max, negate=True), m, fn_)
                e_ = actf(pb[:, 0:nk], p[:, 0:nk], ACT.Exp, a2, f, bias=mx[:, 0:1])
                slots_s.give(s, e_)
            nmx.give(n, e_)
            u["P"] = (i, pb, e_)
            if u["last_scores"]:
                u["last_scores"](m)

        def transposes(u):
            i, pb, e_ = u["P"]
            nk = u["nk"]
            s, p, fr = tslot.take()
            for c in range(0, nk, 128):
                w = min(128, nk - c)
                m = tr(p[0:w, c:c + 128], pb[:, c:c + w], e_, fr)
            P.give(i, m)
            k, (ph, pl), f = PT.take()
            full = nk // 128 * 128
            parts = [(ph[:, 0:full], pl[:, 0:full], p[:, 0:full])]
            if nk > full:
                c = slice(full, full + 128)
                parts.append((ph[0:64, c], pl[0:64, c], p[0:64, c]))
            marks = split_psum(parts, m, f)
            tslot.give(s, *marks)
            u["PT"] = (k, ph, pl, marks)

        def values(u):
            k, ph, pl, marks = u["PT"]
            j, t, nk, k0 = u["j"], u["t"], u["nk"], u["k0"]
            if t == 0:
                state["o"] = oslot.take()
            s, o, fr = state["o"]
            VH, VL = u["v"]
            nt = (nk + 127) // 128
            for i in range(nt):
                w = min(128, nk - 128 * i)
                kt = k0 // 128 + i
                m = mm3(o[:, t * 128:t * 128 + 128], (VH[0:w, kt, j, :], VL[0:w, kt, j, :]),
                        (ph[0:w, i * 128:i * 128 + 128], pl[0:w, i * 128:i * 128 + 128]),
                        i == 0, i == nt - 1, marks, fr, u["ready"]())
            PT.give(k, m)
            if t == 7:
                a, b = slice(64 * j, 64 * j + 64), slice(64 - 64 * j, 128 - 64 * j)
                r = recip(rec[a, :], o[b, :], m, state.get("rec%d" % j))
                out, f = u["out"]()
                z = tt(dve, out[a, :], o[a, :], rec[a, :], MUL, r, f)
                state["rec%d" % j] = z
                oslot.give(s, z)
                u["finish"](z, m)

        n = len(units)
        for i in range(n + 2):
            if i in prep_at:
                prep_at[i]()
            if i < n:
                scores(units[i])
            if 1 <= i <= n:
                transposes(units[i - 1])
            if i >= 2:
                values(units[i - 2])

    def phase_na():
        nonlocal slots_s
        slots_s = Ring([slot(0), slot(1)])
        with ExitStack() as st:
            raws = Ring([tuple(sb(st, [128, L]) for _ in range(4)) for _ in range(2)])
            big = Ring([sb(st, [128, L]) for _ in range(2)])
            QK = Ring([tuple(sb(st, [128, L], R) for _ in range(4)) for _ in range(2)])
            V = Ring([tuple(sb(st, [128, 8, 2, 128], R) for _ in range(2)) for _ in range(2)])
            tab = Ring([sb(st, [128, 23 * 64]) for _ in range(2)])
            outs = Ring([sb(st, [128, L]) for _ in range(1)])
            one, zero = sb(st, [128, 8, 64]), sb(st, [128, 8, 64])
            om = [memset(dve, one[:], 1.0), memset(dve, zero[:], 0.0)]
            vinit = [value_ones(VH, VL, one[:], zero[:], om) for VH, VL in V.bufs]
            loads, chunks, tabs = {}, {}, {}

            def fetch(c):
                i, bufs, f = raws.take()
                ms = [load(f"na{i}{n}", bufs[n][:], pj[4 * n + c], f) for n in range(4)]
                loads[c] = (i, bufs, ms)

            def fetch_tab(h):
                i, b, f = tab.take()
                tabs[h] = (i, b, load(f"tab{i}", b[:], A["rpb"][h], f))

            def prep(c):
                i, (q, k, v, z), ms = loads[c]
                qi, (qh, ql, kh, kl), f = QK.take()
                vi, (VH, VL), fv = V.take()
                m1, _ = head_norm((big,), q[:], "gq", "eps64", 1.0, ms[0], qh, ql, f)
                m2, _ = head_norm((big,), k[:], "gk", "eps", 1.0 / 64, ms[1], kh, kl, f)
                m3 = value_tiles(v, ms[2], VH, VL, fv)
                m4 = actf(z[:], z[:], ACT.Silu, ms[3])
                chunks[c] = dict(i=i, z=z, zm=m4, qi=qi, vi=vi, q=(qh, ql), k=(kh, kl), v=(VH, VL),
                                 ready=m1 + m2 + m3 + vinit[vi])

            units = []
            state = {}
            for c in range(4):
                for j in range(2):
                    h = 2 * c + j
                    for t in range(8):
                        if t < 2:
                            nk, k0, b0 = 512, 0, (7 - 2 * t - 1) * 64
                        elif t >= 6:
                            nk, k0, b0 = 512, 512, (8 - 2 * t + 7 - 1) * 64
                        else:
                            nk, k0, b0 = 576, (2 * t - 4) * 64, 14 * 64
                        u = dict(c=c, j=j, h=h, t=t, nk=nk, k0=k0)
                        units.append(u)

                        class Late:
                            pass
                        u["b0"] = b0

            def bind(c, j):
                ch = chunks[c]
                i, b, bm = tabs[2 * c + j]
                for u in units[(2 * c + j) * 8:(2 * c + j) * 8 + 8]:
                    u["q"], u["k"], u["v"] = ch["q"], ch["k"], ch["v"]
                    u["ready"] = lambda ch=ch: ch["ready"]
                    u["bias"] = (b[:, u["b0"]:u["b0"] + u["nk"]], bm)
                    u["bias_done"] = (lambda a, i=i: tab.give(i, a)) if u["t"] == 7 else (lambda a: None)
                    u["last_scores"] = (lambda m, ch=ch: QK.give(ch["qi"], m)) if (u["t"] == 7 and j == 1) else None

                    def out(j=j):
                        if j == 0:
                            state["out"] = outs.take()
                        return state["out"][1], state["out"][2]
                    u["out"] = out

                    def finish(z, m, ch=ch, j=j, c=c):
                        if j == 0:
                            state["z0"] = z
                            return
                        oi, ob, _ = state["out"]
                        g = tt(dve, ob[:], ob[:], ch["z"][:], MUL, z, state["z0"], ch["zm"])
                        V.give(ch["vi"], m)
                        raws.give(ch["i"], g)
                        outs.give(oi, store(f"nao{oi}", mixd[c], ob[:], g))
                    u["finish"] = finish

            fetch(0)
            fetch(1)
            fetch_tab(0)
            prep_at = {}

            def at(i, *fns):
                old = prep_at.get(i)

                def run():
                    if old:
                        old()
                    for f in fns:
                        f()
                prep_at[i] = run
            at(0, lambda: prep(0))
            for c in range(4):
                for j in range(2):
                    h = 2 * c + j
                    at(8 * h, lambda c=c, j=j: bind(c, j))
                    if h < 7:
                        at(8 * h + 1, lambda h=h: fetch_tab(h + 1))
            for c in range(1, 4):
                at(16 * (c - 1) + 8, lambda c=c: prep(c))
                if c + 1 < 4:
                    at(16 * c + 4, lambda c=c: fetch(c + 1))
            attention(units, st, prep_at)
            fence()

    def phase_delta():
        with ExitStack() as st:
            slots = Ring([slot(s) for s in range(4)])
            dm = sb(st, [128, 14, 128])
            dmm = load("dm", dm[:], A["dmask"])
            TRI = [dm[:, 0, :], dm[:, 1, :]]
            LEV = [[dm[:, 2 + d * 6 + l, :] for l in range(6)] for d in range(2)]

            beta, G, eg, ed, bg = (sb(st, [128, 8, 8]) for _ in range(5))
            gt = sb(st, [128, 8, 64])
            with ExitStack() as s2:
                gr, w1, w2, w3 = (sb(s2, [64, L]) for _ in range(4))
                nA = sb(s2, [64, 1])
                b_, a_ = slice(0, 32), slice(32, 64)
                g0 = load("gate", gr[:], pj[32, 0:64, :])
                x1 = actf(w1[b_, :], gr[b_, :], ACT.Exp, g0, scale=-1.0)
                x1 = ts(dve, w1[b_, :], w1[b_, :], 1.0, None, ADD, None, x1)
                x1 = recip(gr[b_, :], w1[b_, :], x1)
                y0 = ts(dve, w1[a_, :], gr[a_, :], C("dtb")[a_, :], None, ADD, None, g0)
                y1 = actf(w2[a_, :], w1[a_, :], ACT.Abs, y0)
                y1 = actf(w2[a_, :], w2[a_, :], ACT.Exp, y1, scale=-1.0)
                y1 = actf(w2[a_, :], w2[a_, :], ACT.Ln, y1, bias=C("one")[a_, :])
                y2 = ts(dve, w3[a_, :], w1[a_, :], 0.0, None, ALU.max, None, y0)
                y3 = tt(dve, w3[a_, :], w3[a_, :], w2[a_, :], ADD, y1, y2)
                n1 = actf(nA[a_, :], C("alog")[a_, :], ACT.Exp)
                y4 = ts(dve, gr[a_, :], w3[a_, :], nA[a_, :], -1.0, MUL, MUL, y3, n1, y0)
                s, p, fr = slots.take()
                for t in range(8):
                    m = tr(p[:, t * 64:t * 64 + 64], gr[:, t * 128:t * 128 + 128], x1, y4, fr, n=64)
                c1 = copy(dve, gt[:], p[:, 0:512].rearrange("p (t f) -> p t f", t=8), m)
                slots.give(s, c1)
                c2 = copy(dve, beta[:], gt[:, :, 0:8], c1)
                s, p, fr = slots.take()
                pg = p.rearrange("p (a n) -> p a n", a=2)
                for d in range(2):
                    m = mm(pg[:, 0, 32 * d:32 * d + 32], TRI[d], gt[:, :, 32 + 4 * d:36 + 4 * d], True, True,
                           c1, fr, dmm)
                m2 = mm(pg[:, 1, 0:64], BONES, gt[:, :, 32:40], True, True, c1, fr)
                gs = []
                for d in range(2):
                    gs.append(copy(dve, G[:, :, 4 * d:4 * d + 4],
                                   pg[:, 0, 32 * d:32 * d + 32].rearrange("p (t h) -> p t h", t=8), m2))
                c3 = tt(dve, ed[:], pg[:, 1, 0:64].rearrange("p (t h) -> p t h", t=8), G[:], SUB, gs)
                slots.give(s, c3)
                e1 = actf(ed[:], ed[:], ACT.Exp, c3)
                e2 = actf(eg[:], G[:], ACT.Exp, gs)
                e3 = tt(dve, bg[:], eg[:], beta[:], MUL, e2, c2)
                gate_ready = [c1, c2, e1, e2, e3, dmm] + gs
                fence()

            bc8 = lambda a: a.unsqueeze(1).to_broadcast([128, 8, 128])
            bcl = lambda a: a.unsqueeze(2).to_broadcast([128, 8, 128])
            v8 = lambda a: a.rearrange("p (t f) -> p t f", t=8)

            raw = Ring([sb(st, [128, L + 4]) for _ in range(2)])
            rz = [memset(pool, b[:, c:c + 2], 0.0) for b in raw.bufs for c in (0, L + 2)]
            cv = Ring([sb(st, [128, L]) for _ in range(2)])
            sqb = sb(st, [128, L])
            sq_free = [None]
            heads = [dict(q=sb(st, [128, L]), k=sb(st, [128, L]), kt=sb(st, [128, L]), vt=sb(st, [128, L]),
                          O=sb(st, [128, L])) for _ in range(2)]
            hds = [dict(D=sb(st, [128, L]), MT=sb(st, [128, L]), X=sb(st, [128, L]), Y=sb(st, [128, L]),
                        vb=sb(st, [128, L]), kb=sb(st, [128, L]), qg=sb(st, [128, L]), egl=sb(st, [128, 16]),
                        S=sb(st, [128, 128]), vn=sb(st, [128, 128])) for _ in range(4)]
            EB = Ring([sb(st, [128, L]) for _ in range(2)])
            P1 = Ring([sb(st, [128, L]) for _ in range(2)])
            nl = [0]

            def fetch_raw(row):
                i, b, f = raw.take()
                return i, b, load(f"dr{i}", b[:, 2:L + 2], pj[row], f)

            def conv_silu(row, wi, dst, free):
                i, b, lm = fetch_raw(row)
                k, c, f = cv.take()
                m = ts(dve, c[:], b[:, 0:L], C("conv", wi * 5), None, MUL, None, lm, f, rz)
                for tap in range(1, 5):
                    m = stt(c[:], b[:, tap:tap + L], C("conv", wi * 5 + tap), c[:], MUL, ADD, m)
                raw.give(i, m)
                a = actf(dst, c[:], ACT.Silu, m, free)
                cv.give(k, a)
                return a

            def l2norm(buf, mark, scale, epsname):
                a = actf(sqb[:], buf, ACT.Square, mark, sq_free[0])
                s, p, fr = slots.take()
                for half in range(2):
                    c = slice(half * 512, half * 512 + 512)
                    m = mm(p[:, c], ONES, sqb[:, c], True, True, a, fr)
                a = actf(sqb[:], p, ACT.Sqrt, m, scale=scale, bias=C(epsname))
                slots.give(s, a)
                r = recip(sqb[:], sqb[:], a)
                m = tt(dve, buf, buf, sqb[:], MUL, r)
                sq_free[0] = m
                return m

            def to_tokens(src, dst, mark, free, q):
                s, p, fr = slots.take()
                for t in range(8):
                    m = tr(p[:, t * 128:t * 128 + 128], src[:, t * 128:t * 128 + 128], mark, fr)
                c = copy(q, dst, p, m, free)
                slots.give(s, c)
                return c

            def prep_head(h, hb, last):
                hb["qm"] = conv_silu(16 + h, h, hb["q"][:], last)
                hb["qm"] = l2norm(hb["q"][:], hb["qm"], 128.0, "eps128")
                hb["km"] = conv_silu(20 + h, 4 + h, hb["k"][:], last)
                hb["km"] = l2norm(hb["k"][:], hb["km"], 1.0, "eps")
                vm = conv_silu(24 + h, 8 + h, hb["O"][:], last)
                hb["ktm"] = to_tokens(hb["k"], hb["kt"][:], hb["km"], last, act)
                hb["vtm"] = to_tokens(hb["O"], hb["vt"][:], vm, last, dve)

            def gate_rows(g, src, col, rhs):
                s, p, fr = slots.take()
                for t in range(8):
                    m = mm(p[:, t * 128:t * 128 + 128], src[:, t, col:col + 1].to_broadcast([128, 128]), rhs,
                           True, True, fr, gate_ready)
                return s, p, m

            def prep_dir(h, d, hb, g, last):
                hd = h + 4 * d
                s, p, m = gate_rows(g, gt, 32 + hd, TRI[d])
                ei, E, ef = EB.take()
                x = actf(E[:], p, ACT.Exp, m, ef)
                for t in range(8):
                    c = slice(t * 128, t * 128 + 128)
                    y = ts(dve, g["D"][:, c], p[:, c], G[:, t, hd:hd + 1], 0.0, SUB, ALU.min, m, x, last)
                slots.give(s, x, y)
                y = actf(g["D"][:], g["D"][:], ACT.Exp, y)
                y = tt(pool, v8(g["D"][:]), v8(g["D"][:]), bc8(TRI[d]), MUL, y)
                g["eglm"] = copy(dve, g["egl"][:], E[:, (63 if d == 0 else 0)::64], x, last)
                g["qgm"] = tt(pool, g["qg"][:], hb["q"][:], E[:], MUL, x, hb["qm"], last)
                EB.give(ei, g["eglm"], g["qgm"])
                s, p, m = gate_rows(g, gt, hd, IDENT)
                ei, kbT, ef = EB.take()
                b = tt(dve, kbT[:], hb["k"][:], p, MUL, m, hb["km"], ef)
                slots.give(s, b)
                s, p, fr = slots.take()
                for t in range(8):
                    c = slice(t * 128, t * 128 + 128)
                    m = mm(p[:, c], hb["k"][:, c], kbT[:, c], True, True, b, fr)
                EB.give(ei, m)
                mt = tt(dve, g["MT"][:], p, g["D"][:], MUL, m, y, last)
                slots.give(s, mt)
                g["Dm"] = y
                g["MTm"] = mt
                m1 = LEV[1 - d][0]
                a = tt(dve, v8(g["Y"][:]), v8(g["MT"][:]), bc8(m1), MUL, mt, last)
                a = tt(dve, v8(g["Y"][:]), bc8(IDENT), v8(g["Y"][:]), SUB, a)
                g["Ym"] = a
                s, p, fr = slots.take()
                for t in range(8):
                    c = slice(t * 128, t * 128 + 128)
                    m = tr(p[:, c], g["Y"][:, c], a, fr)
                g["Xm"] = copy(act, g["X"][:], p, m, last)
                slots.give(s, g["Xm"])
                g["vbm"] = tt(pool, v8(g["vb"][:]), v8(hb["vt"][:]), bcl(beta[:, :, hd]), MUL, hb["vtm"], last)
                g["kbm"] = tt(pool, v8(g["kb"][:]), v8(hb["kt"][:]), bcl(bg[:, :, hd]), MUL, hb["ktm"], last)

            def prep_intra(hb, pair):
                s, p, fr = slots.take()
                for t in range(8):
                    c = slice(t * 128, t * 128 + 128)
                    m = mm(p[:, c], hb["k"][:, c], hb["q"][:, c], True, True, fr, hb["qm"], hb["km"])
                for g in pair:
                    g["Im"] = tt(dve, g["D"][:], p, g["D"][:], MUL, m, g["Dm"], g["MTm"])
                slots.give(s, *[g["Im"] for g in pair])

            def level(l, gs):
                todo = []

                def first(n):
                    d, g = gs[n]
                    s, p, fr = slots.take()
                    for t in range(8):
                        c = slice(t * 128, t * 128 + 128)
                        m = mm(p[:, c], g["MT"][:, c], g["X"][:, c], True, True, g["MTm"], g["Xm"], fr)
                    i, b, f = P1.take()
                    a = tt(dve, v8(b[:]), v8(p), bc8(LEV[d][l]), MUL, m, f)
                    slots.give(s, a)
                    todo.append((i, b, a))

                def second(n):
                    d, g = gs[n]
                    i, b, a = todo.pop(0)
                    s, p, fr = slots.take()
                    for t in range(8):
                        c = slice(t * 128, t * 128 + 128)
                        m = mm(p[:, c], b[:, c], g["Y"][:, c], True, True, a, g["Ym"], fr)
                    if l < 5:
                        s2, p2, fr2 = slots.take()
                        for t in range(8):
                            c = slice(t * 128, t * 128 + 128)
                            m2 = mm(p2[:, c], g["Y"][:, c], b[:, c], True, True, a, g["Ym"], fr2)
                        g["Ym"] = tt(dve, g["Y"][:], g["Y"][:], p, SUB, m, m2)
                        g["Xm"] = tt(dve, g["X"][:], g["X"][:], p2, SUB, m2)
                        slots.give(s2, g["Xm"])
                        P1.give(i, m2)
                    else:
                        g["Ym"] = tt(dve, g["Y"][:], g["Y"][:], p, SUB, m)
                        P1.give(i, m)
                    slots.give(s, g["Ym"])

                first(0)
                for n in range(4):
                    if n + 1 < 4:
                        first(n + 1)
                    second(n)

            def apply(g, hb, hd):
                s, p, fr = slots.take()
                for t in range(8):
                    c = slice(t * 128, t * 128 + 128)
                    m = mm(p[:, c], g["Y"][:, c], g["vb"][:, c], True, True, g["Ym"], g["vbm"], fr)
                g["um"] = copy(act, g["vb"][:], p, m)
                slots.give(s, g["um"])
                s, p, fr = slots.take()
                for t in range(8):
                    c = slice(t * 128, t * 128 + 128)
                    m = mm(p[:, c], g["kb"][:, c], g["Y"][:, c], True, True, g["kbm"], fr)
                g["wm"] = copy(dve, g["kb"][:], p, m)
                slots.give(s, g["wm"])
                g["kdm"] = tt(pool, v8(g["MT"][:]), v8(hb["kt"][:]), bcl(ed[:, :, hd]), MUL, g["Ym"], hb["ktm"])

            def scan(gs):
                banks = Ring([ps[:, i, :] for i in range(8)])
                for i in range(8):
                    banks.free[i] = list(slots.free[i // 2])
                for _, g, _ in gs:
                    g["Sm"] = memset(pool, g["S"][:], 0.0)
                seen = {}
                for n in range(16):
                    work = []
                    for d, g, hb in gs:
                        ch = n if d == 0 else 15 - n
                        t, j = ch // 2, ch % 2
                        r, c, cc = slice(64 * j, 64 * j + 64), slice(64 * ch, 64 * ch + 64), slice(128 * t, 128 * t + 128)
                        i, p, fr = banks.take()
                        m = mm(p[r, 0:128], g["kb"][:, c], g["S"][:], True, True, g["wm"], g["Sm"], fr)
                        v = tt(dve, g["vn"][r, :], g["vb"][r, cc], p[r, 0:128], SUB, m, g["um"], g.get("vfree"))
                        banks.give(i, v)
                        work.append((d, g, hb, ch, r, c, cc, v))
                    for d, g, hb, ch, r, c, cc, v in work:
                        i, p, fr = banks.take()
                        mm(p[:, 0:64], g["S"][:], g["qg"][:, c], True, False, g["qgm"], fr)
                        mo = mm(p[:, 0:64], g["vn"][r, :], g["D"][r, c], False, True, v, g["Im"])
                        i2, p2, fr2 = banks.take()
                        ms = mm(p2[:, 0:128], g["MT"][r, cc], g["vn"][r, :], True, True, g["kdm"], fr2)
                        g["vfree"] = ms
                        g["Sm"] = stt(g["S"][:], g["S"][:], g["egl"][:, ch:ch + 1], p2[:, 0:128], MUL, ADD, ms,
                                      g["eglm"], g["Sm"])
                        banks.give(i2, g["Sm"])
                        key = (id(hb), ch)
                        if key not in seen:
                            seen[key] = copy(act, hb["O"][:, c], p[:, 0:64], mo, hb["vtm"])
                        else:
                            seen[key] = tt(dve, hb["O"][:, c], hb["O"][:, c], p[:, 0:64], ADD, mo, seen[key])
                        hb["Om"] = [seen[key]] if n == 0 else hb["Om"] + [seen[key]]
                        banks.give(i, seen[key])
                for i in range(4):
                    slots.free[i] = banks.free[2 * i] + banks.free[2 * i + 1]
                return ms

            def finish_head(h, hb):
                zi, z, lm = fetch_raw(28 + h)
                za = actf(z[:, 2:L + 2], z[:, 2:L + 2], ACT.Silu, lm)
                a = actf(sqb[:], hb["O"][:], ACT.Square, hb["Om"], sq_free[0])
                s, p, fr = slots.take()
                for half in range(2):
                    c = slice(half * 512, half * 512 + 512)
                    m = mm(p[:, c], ONES, sqb[:, c], True, True, a, fr)
                a = actf(sqb[:], p, ACT.Sqrt, m, scale=1.0 / 128, bias=C("eps"))
                slots.give(s, a)
                r = recip(sqb[:], sqb[:], a)
                i, c, f = cv.take()
                m = stt(c[:], hb["O"][:], C("dnw"), sqb[:], MUL, MUL, r, f)
                sq_free[0] = m
                m2 = tt(dve, c[:], c[:], z[:, 2:L + 2], MUL, m, za)
                raw.give(zi, m2)
                cv.give(i, store(f"cvo{i}", mixd[4 + h], c[:], m2))
                return m

            last = []
            for grp in range(2):
                hh = [2 * grp, 2 * grp + 1]
                for n, h in enumerate(hh):
                    prep_head(h, heads[n], last)
                    for d in range(2):
                        prep_dir(h, d, heads[n], hds[2 * n + d], last)
                    prep_intra(heads[n], hds[2 * n:2 * n + 2])
                gs = [(g % 2, hds[g]) for g in range(4)]
                for l in range(1, 6):
                    level(l, gs)
                for g in range(4):
                    apply(hds[g], heads[g // 2], hh[g // 2] + 4 * (g % 2))
                m = scan([(g % 2, hds[g], heads[g // 2]) for g in range(4)])
                last = [m] + [finish_head(h, heads[n]) for n, h in enumerate(hh)] + [g["Sm"] for g in hds]
            fence()

    def phase_outproj(x, xready, src, st):
        with ExitStack() as s2:
            H, Lo = sb(s2, [128, KC, L], R), sb(s2, [128, KC, L], R)
            tmp = Ring([sb(s2, [128, L]) for _ in range(2)])
            ready = []
            for k in range(KC):
                i, b, f = tmp.take()
                m = load(f"op{i}", b[:], src[k], f)
                ready.append(split(H[:, k, :], Lo[:, k, :], b[:], m))
                tmp.give(i, *ready[k])
            for m in range(KC):
                s, p, done = linear_tile(H, Lo, ready)
                xready[m] = tt(dve, x[:, m, :], x[:, m, :], p, ADD, done, xready[m])
                slots.give(s, xready[m])
            fence()
        return xready

    def phase_ffn(x, wname, xready):
        with ExitStack() as st:
            H, Lo = sb(st, [128, KC, L], R), sb(st, [128, KC, L], R)
            with ExitStack() as s2:
                ready = norm_split(x, wname, xready, H, Lo, s2)
                fence()
            AB = Ring([(sb(st, [128, L], R), sb(st, [128, L], R)) for _ in range(5)])
            sg = Ring([sb(st, [128, L]) for _ in range(1)])
            ab = Ring([sb(st, [128, L]) for _ in range(2)])
            tiles = []

            def gate_up():
                s1, pg, mg = linear_tile(H, Lo, ready)
                s2_, pu, mu = linear_tile(H, Lo, ready)
                i, g, f = sg.take()
                a = actf(g[:], pg, ACT.Silu, mg, f)
                slots.give(s1, a)
                k, b, f = ab.take()
                m = tt(dve, b[:], pu, g[:], MUL, mu, a, f)
                slots.give(s2_, m)
                sg.give(i, m)
                n, (ah, al), f = AB.take()
                marks = split(ah[:], al[:], b[:], m, f)
                ab.give(k, *marks)
                tiles.append((n, ah, al, marks))

            def down(nk):
                grp = tiles[:nk]
                del tiles[:nk]
                for mp in range(4):
                    wh, wl, wm = W.get()
                    for m in range(2):
                        s, p, fr = slots.take()
                        for half in range(2):
                            c = slice(half * 512, half * 512 + 512)
                            for k, (n, ah, al, marks) in enumerate(grp):
                                a = slice((k * 2 + m) * 128, (k * 2 + m) * 128 + 128)
                                last = mm3(p[:, c], (wh[:, a], wl[:, a]), (ah[:, c], al[:, c]),
                                           k == 0, k == nk - 1, wm, fr, marks)
                        o = 2 * mp + m
                        xready[o] = stt(x[:, o, :], p, 0.5, x[:, o, :], MUL, ADD, last, xready[o])
                        slots.give(s, xready[o])
                    W.done(last)
                for n, _, _, _ in grp:
                    AB.give(n, last)

            for _ in range(GROUPS[0]):
                gate_up()
            for g, nk in enumerate(GROUPS):
                if g + 1 < len(GROUPS):
                    gate_up()
                down(nk)
                if g + 1 < len(GROUPS):
                    for _ in range(GROUPS[g + 1] - 1):
                        gate_up()
            fence()
        return xready

    def phase_mix2(x, xready):
        nonlocal slots_s
        with ExitStack() as st:
            UH, UL = sb(st, [128, 4, L], R), sb(st, [128, 4, L], R)
            qkv = sb(st, [128, 6, L])
            qm = [None] * 6
            um = [None] * 4
            with ExitStack() as s2:
                H, Lo = sb(s2, [128, KC, L], R), sb(s2, [128, KC, L], R)
                with ExitStack() as s3:
                    ready = norm_split_in(x, "mixn", xready, H, Lo, qkv)
                    fence()
                for m in range(10):
                    s, p, done = linear_tile(H, Lo, ready)
                    if m < 4:
                        um[m] = split(UH[:, m, :], UL[:, m, :], p, done, q=dve)
                        slots.give(s, *um[m])
                    else:
                        qm[m - 4] = copy(dve if m % 2 else act, qkv[:, m - 4, :], p, done)
                        slots.give(s, qm[m - 4])
                fence()
            for g in range(6):
                store(f"q2{g}", pj[g], qkv[:, g, :], qm[g])
            with ExitStack() as s2:
                TH, TL = sb(s2, [128, 8, 4, 256], R), sb(s2, [128, 8, 4, 256], R)
                wh, wl, wm = W.get()
                tm = []
                for t in range(8):
                    s, p, fr = slots.take()
                    c = slice(t * 128, t * 128 + 128)
                    for g in range(4):
                        m = mm3(p[:, g * 256:g * 256 + 256], (UH[:, g, c], UL[:, g, c]),
                                (wh[:, 0:256], wl[:, 0:256]), True, True, fr, wm, um[g])
                    marks = split(TH[:, t, :, :].rearrange("p g n -> p (g n)"),
                                  TL[:, t, :, :].rearrange("p g n -> p (g n)"), p, m, q=dve)
                    tm.append(marks)
                    slots.give(s, *marks)
                W.done(m)
                alt = sb(s2, [128, 2], R)
                y5 = sb(s2, [128, 8])
                am = load("alt", y5[:, 0:2], A["alt"])
                am = actf(alt[:], y5[:, 0:2], ACT.Copy, am)
                s, p, fr = slots.take()
                for g in range(4):
                    for t in range(8):
                        mm(p[:, 2 * g:2 * g + 2], TH[:, t, g, 0:128], alt[:], t == 0, False, tm[t], am, fr)
                        m = mm(p[:, 2 * g:2 * g + 2], TL[:, t, g, 0:128], alt[:], False, t == 7)
                y5m = actf(y5[:], p[:, 0:8], ACT.Copy, m, am, scale=float(1.0 / np.sqrt(L * 128.0)))
                slots.give(s, y5m)
                taken = [slots.take() for _ in range(4)]
                for t in range(8):
                    wh, wl, wm = W.get()
                    for g in range(4):
                        s, p, fr = taken[g]
                        for d in range(2):
                            a, b = slice(d * 128, d * 128 + 128), slice(d * 512, d * 512 + 512)
                            m = mm3(p[:, b], (TH[:, t, g, a], TL[:, t, g, a]), (wh[:, b], wl[:, b]),
                                    t == 0, t == 7, fr, wm, tm[t])
                    W.done(m)
                wh, wl, wm = W.get()
                cs = Ring([sb(s2, [128, 512]) for _ in range(2)])
                yb = Ring([sb(s2, [128, L]) for _ in range(2)])
                ym = []
                for g in range(4):
                    s, p, _ = taken[g]
                    i, b, f = cs.take()
                    a = copy(act, b[:], p[:, 0:512], m, f)
                    k, y, f = yb.take()
                    a1 = tt(dve, y[:, 0:512], b[:], p[:, 512:1024], SUB, a, f)
                    a2 = tt(dve, y[:, 1023:512:-1], b[:, 1:512], p[:, 513:1024], ADD, a, f)
                    a3 = copy(dve, y[:, 512:513], y5[:, 2 * g:2 * g + 1], y5m, f)
                    slots.give(s, a1, a2)
                    cs.give(i, a1, a2)
                    ym.append(split(UH[:, g, :], UL[:, g, :], y[:], a1, a2, a3, m))
                    yb.give(k, *ym[g])
                for g in range(4):
                    s, p, fr = slots.take()
                    for half in range(2):
                        c = slice(half * 512, half * 512 + 512)
                        a = slice(g * 128, g * 128 + 128)
                        m = mm3(p[:, c], (wh[:, a], wl[:, a]), (UH[:, g, c], UL[:, g, c]), True, True,
                                fr, wm, ym[g])
                    k, y, f = yb.take()
                    a = ts(dve, y[:], p, C("fb", g), None, ADD, None, m, f)
                    slots.give(s, a)
                    yb.give(k, store(f"yb{k}", mixd2[g], y[:], a))
                W.done(m)
                fence()
        with ExitStack() as st:
            slots_s = Ring([slot(0), slot(1)])
            cs_ = sb(st, [128, 2, L])
            rp = sb(st, [128, 128])
            rm = [load("cs", cs_[:], A["rope"]), load("rp", rp[:], A["rperm"])]
            big = Ring([sb(st, [128, L]) for _ in range(2)])
            raws = Ring([sb(st, [128, L]) for _ in range(2)])
            KV = [sb(st, [128, L], R) for _ in range(2)]
            VH, VL = (sb(st, [128, 8, 2, 128], R) for _ in range(2))
            Q = Ring([tuple(sb(st, [128, L], R) for _ in range(2)) for _ in range(2)])
            outs = Ring([sb(st, [128, L]) for _ in range(2)])
            one, zero = sb(st, [128, 8, 64]), sb(st, [128, 8, 64])
            om = [memset(dve, one[:], 1.0), memset(dve, zero[:], 0.0)]
            vi = value_ones(VH, VL, one[:], zero[:], om)
            rope = (cs_[:, 0, :], cs_[:, 1, :], rp[:])

            def fetch(row):
                i, b, f = raws.take()
                return i, b, load(f"gq{i}", b[:], pj[row], f)

            i, b, lm = fetch(0)
            km, g1 = head_norm((big,), b[:], "kn", "eps", 1.0 / 64, [lm] + rm, KV[0], KV[1], None, rope)
            raws.give(i, g1)
            i, b, lm = fetch(1)
            vm = value_tiles(b, lm, VH, VL, None)
            raws.give(i, *vm)
            chunks = {}

            def prep(c):
                i, b, lm = fetch(2 + c)
                qi, (qh, ql), f = Q.take()
                m, g1 = head_norm((big,), b[:], "qn", "eps64", 1.0, lm, qh, ql, f, rope)
                raws.give(i, g1)
                chunks[c] = dict(qi=qi, q=(qh, ql), ready=m + km + vm + vi)

            units = [dict(c=c, j=j, t=t, nk=1024, k0=0) for c in range(4) for j in range(2) for t in range(8)]
            state = {}

            def bind(c):
                ch = chunks[c]
                for u in units[16 * c:16 * c + 16]:
                    j = u["j"]
                    u["q"], u["k"], u["v"], u["bias"] = ch["q"], tuple(KV), (VH, VL), None
                    u["ready"] = lambda ch=ch: ch["ready"]
                    u["last_scores"] = (lambda m, ch=ch: Q.give(ch["qi"], m)) if (u["t"] == 7 and j == 1) else None

                    def out(j=j):
                        if j == 0:
                            state["out"] = outs.take()
                        return state["out"][1], state["out"][2]
                    u["out"] = out

                    def finish(z, m, j=j, c=c):
                        if j == 0:
                            state["z0"] = z
                            return
                        oi, ob, _ = state["out"]
                        outs.give(oi, store(f"gqo{oi}", mixd2[4 + c], ob[:], z, state["z0"]))
                    u["finish"] = finish

            prep_at = {0: lambda: (prep(0), bind(0))}
            for c in range(1, 4):
                prep_at[16 * c - 8] = lambda c=c: prep(c)
                prep_at[16 * c] = lambda c=c: bind(c)
            attention(units, st, prep_at)
            fence()
        return xready

    def norm_split_in(x, wname, xready, H, Lo, space):
        class Fake:
            pass
        bufs = [space[:, i, :] for i in range(5)]
        sq = Ring(bufs[0:2])
        rs = bufs[2]
        tmp = Ring(bufs[3:5])
        s, p, free = slots.take()
        for k in range(KC):
            i, b, f = sq.take()
            a = actf(b, x[:, k, :], ACT.Square, xready[k], f)
            for half in range(2):
                c = slice(half * 512, half * 512 + 512)
                m = mm(p[:, c], ONES, b[:, c], k == 0, k == KC - 1, a, free)
            sq.give(i, m)
        a = actf(rs, p, ACT.Sqrt, m, scale=1.0 / D, bias=C("eps"))
        slots.give(s, a)
        r = recip(rs, rs, a)
        ready = []
        for k in range(KC):
            i, b, f = tmp.take()
            m = stt(b, x[:, k, :], C(wname, k), rs, MUL, MUL, r, xready[k], f)
            ready.append(split(H[:, k, :], Lo[:, k, :], b, m))
            tmp.give(i, *ready[k])
        return ready

    phase_inproj()
    phase_na()
    phase_delta()
    with ExitStack() as st:
        W.open(st, A["wts"].shape[0])
        x = sb(st, [128, KC, L])
        xr = [load(f"x{k}", x[:, k, :], A["xT"][k]) for k in range(KC)]
        xr = phase_outproj(x, xr, mixd, st)
        xr = phase_ffn(x, "ffn1", xr)
        xr = phase_mix2(x, xr)
        xr = phase_outproj(x, xr, mixd2, st)
        xr = phase_ffn(x, "ffn2", xr)
        with ExitStack() as s2:
            def sink(k, b, m):
                return [store(f"fo{k % 2}", A["out"][k], b[:], m)]
            rmsnorm(x, "fin", xr, sink, s2)
            fence()
    if "dbg" in A:
        for n, (dst, src) in enumerate(((A["dbg"][0], pj), (A["dbg"][1], mixd), (A["dbg"][2], mixd2))):
            store(f"dbg{n}", dst, src)
    assert W.next == A["wts"].shape[0], (W.next, A["wts"].shape)
    sp.items.append((flat(out_marks), None, Mark(sp)))

    for q in engines + [sp]:
        q.number()
    with top:
        block = top.enter_context(nc.Block())

        @block.sync
        def _(e):
            sp.emit(e)

        @block.scalar
        def _(e):
            act.emit(e)

        @block.vector
        def _(e):
            dve.emit(e)

        @block.gpsimd
        def _(e):
            pool.emit(e)

        @block.tensor
        def _(e):
            pe.emit(e)


def _tiles(w, pad_to=None):
    K, M = w.shape
    return np.ascontiguousarray(w.reshape(K // 128, 128, M // 128, 128).transpose(2, 1, 0, 3)).reshape(M // 128, 128, K)


def _layout(inputs):
    f = np.float32
    I = {k: np.asarray(v) for k, v in inputs.items()}
    cols, ncst = const_columns()
    cst = np.zeros((128, ncst), f)

    def put(name, a):
        at, n = cols[name]
        cst[:, at:at + n] = a
    for name, src in (("norm1", I["norm_w"][0]), ("ffn1", I["ffn1_norm_2"]), ("mixn", I["mix_norm_2"]),
                      ("ffn2", I["ffn2_norm_2"]), ("fin", I["final_norm_2"])):
        put(name, src.reshape(8, 128).T)
    two = lambda a: np.concatenate([a, a])[:, None]
    put("gq", two(I["qk_gain_q"][0]))
    put("gk", two(I["qk_gain_k"][0]))
    put("qn", two(I["q_norm_2"]))
    put("kn", two(I["k_norm_2"]))
    put("conv", I["conv_w"][0].reshape(5, 12, 128).transpose(2, 1, 0).reshape(128, 60))
    cst[32:40, cols["alog"][0]] = I["a_log"][0].reshape(8)
    cst[32:40, cols["dtb"][0]] = I["dt_bias"][0].reshape(8)
    put("dnw", I["dn_norm_w"][0][:, None])
    put("fb", I["fnet_b_2"].T)
    put("eps", EPS)
    put("eps64", 64 * EPS)
    put("eps128", 128 * EPS)
    put("one", 1.0)
    put("ident", np.eye(128, dtype=f))
    put("ones", 1.0)
    blk = np.arange(128) // 64
    put("bones", (blk[:, None] == blk[None, :]).astype(f))

    w_in = I["w_in"][0]
    gates = np.zeros((D, 128), f)
    g16 = w_in[:, 4096:4112]
    gates[:, 0:4], gates[:, 4:8] = g16[:, 0:4], g16[:, 8:12]
    gates[:, 32:36], gates[:, 36:40] = g16[:, 4:8], g16[:, 12:16]
    parts = [_tiles(w_in[:, :4096]), _tiles(gates), _tiles(I["w_out"][0])]

    def ffn(g, u, d):
        pad = lambda a: np.concatenate([a, np.zeros((D, FT * 128 - FF), f)], 1)
        tg, tu = _tiles(pad(g)), _tiles(pad(u))
        dp = np.concatenate([d, np.zeros((FT * 128 - FF, D), f)], 0).reshape(FT, 128, 4, 256)
        out = []
        at = 0

        def gu(n):
            for _ in range(n):
                i = sum(1 for o in out if o[1] == "g")
                out.append((tg[i:i + 1], "g"))
                out.append((tu[i:i + 1], "u"))
        gu(GROUPS[0])
        for g_, nk in enumerate(GROUPS):
            if g_ + 1 < len(GROUPS):
                gu(1)
            for mp in range(4):
                t = np.zeros((1, 128, 1024), f)
                t[0, :, :nk * 256] = dp[at:at + nk, :, mp, :].transpose(1, 0, 2).reshape(128, nk * 256)
                out.append((t, "d"))
            at += nk
            if g_ + 1 < len(GROUPS):
                gu(GROUPS[g_ + 1] - 1)
        return [o[0] for o in out]

    parts += ffn(I["ffn1_w_gate_2"], I["ffn1_w_up_2"], I["ffn1_w_down_2"])
    w2 = I["w_in_2"]
    wf, wq, wk, wv = w2[:, :512], w2[:, 512:1024], w2[:, 1024:1152], w2[:, 1152:1280]
    heads = np.array([[c, c + 4] for c in range(4)]).reshape(-1)
    wq = wq.reshape(D, 8, 64)[:, heads].reshape(D, 512)
    parts += [_tiles(wf), _tiles(wk), _tiles(wv), _tiles(wq)]
    n = np.arange(128)
    ang = 2 * np.pi * ((n[:, None] * n[None, :]) % 128) / 128
    x1 = np.zeros((1, 128, 1024), f)
    x1[0, :, 0:128], x1[0, :, 128:256] = np.cos(ang), np.sin(ang)
    t, s = np.arange(L), np.arange(512)
    ang = 2 * np.pi * ((t[:, None] * s[None, :]) % L) / L
    sc = 1.0 / np.sqrt(L * 128.0)
    tab = np.concatenate([np.cos(ang) * sc, np.sin(ang) * sc], 1).astype(f).reshape(8, 128, 1024)
    x2 = np.zeros((1, 128, 1024), f)
    x2[0, :, 0:512] = I["fnet_w_2"].transpose(1, 0, 2).reshape(128, 512)
    wo2 = I["w_out_2"]
    wo2 = np.concatenate([wo2[:512], wo2[512:].reshape(8, 64, D)[heads].reshape(512, D)], 0)
    parts += [x1, tab, x2, _tiles(wo2)]
    parts += ffn(I["ffn2_w_gate_2"], I["ffn2_w_up_2"], I["ffn2_w_down_2"])
    wts = np.concatenate(parts, 0)

    rpb = I["rpb"][0]
    c, kc = np.arange(64), np.arange(64)
    lo = np.clip(c - 8, 0, 48)
    ok = (kc[None, :] >= lo[:, None]) & (kc[None, :] < lo[:, None] + 16)
    dc = np.clip(kc[None, :] - c[:, None] + 15, 0, 30)
    full = rpb[:, :, dc]
    tabs = np.full((8, 128, 23, 64), NEG, f)
    for half in range(2):
        r = slice(64 * half, 64 * half + 64)
        for i in range(14):
            tabs[:, r, i, :] = np.where(ok[None], full[:, i + 1 - half], f(NEG))
        for i in range(9):
            dr = i + 3 - half
            if 3 <= dr <= 10:
                tabs[:, r, 14 + i, :] = np.where(ok[None], full[:, dr], f(NEG))
    i = np.arange(128)
    same = blk[:, None] == blk[None, :]
    dm = np.zeros((128, 14, 128), f)
    dm[:, 0] = same & (i[:, None] <= i[None, :])
    dm[:, 1] = same & (i[:, None] >= i[None, :])
    for l in range(6):
        b = 1 << l
        low = (i[:, None] // (2 * b) == i[None, :] // (2 * b)) & (i[:, None] % (2 * b) >= b) & (i[None, :] % (2 * b) < b)
        dm[:, 2 + l] = low
        dm[:, 8 + l] = low.T
    inv = (np.float32(10000.0) ** (-np.arange(0, 32, 2, dtype=f) / np.float32(32))).astype(f)
    tok = np.arange(L)
    ar = (tok // 64).astype(f)[None, :] * inv[:, None]
    ac = (tok % 64).astype(f)[None, :] * inv[:, None]
    ang = np.concatenate([ar, ar, ac, ac] * 2, 0)
    rope = np.stack([np.cos(ang), np.sin(ang)], 1).astype(f)
    rp = np.zeros((128, 128), f)
    for p in range(128):
        if p % 32 < 16:
            rp[p + 16, p] = -1.0
        else:
            rp[p - 16, p] = 1.0
    alt = np.zeros((128, 2), f)
    alt[:] = (1.0 - 2.0 * (i % 2))[:, None]
    return dict(xT=np.ascontiguousarray(I["x"][0].T).reshape(8, 128, L), cst=cst, wts=wts,
                rpb=tabs.reshape(8, 128, 23 * 64), dmask=dm, rope=rope, rperm=rp, alt=alt)


DBG = False


def kernel(**inputs):
    import concourse.bacc as _bacc
    from concourse import mybir as _mybir
    from concourse.bass_utils import run_bass_kernel_spmd as _run

    nc = _bacc.Bacc("TRN2", target_bir_lowering=False, num_devices=1)
    arrays, A = {}, {}
    for name, a in _layout(inputs).items():
        a = np.ascontiguousarray(a)
        arrays[f"in_{name}_dram"] = a
        A[name] = nc.dram_tensor(f"in_{name}_dram", a.shape, _mybir.dt.from_np(a.dtype), kind="ExternalInput").ap()
    A["out"] = nc.dram_tensor("out_0_dram", (8, 128, L), _mybir.dt.float32, kind="ExternalOutput").ap()
    if DBG:
        A["dbg"] = [nc.dram_tensor(f"dbg{i}", (n, 128, L), _mybir.dt.float32, kind="ExternalOutput").ap()
                    for i, n in enumerate((33, 8, 8))]
    build(nc, A)
    r = _run(nc, [arrays], core_ids=[0])
    out = np.ascontiguousarray(np.asarray(r.results[0]["out_0_dram"]).reshape(D, L).T).reshape(1, L, D)
    if DBG:
        return tuple([out] + [np.asarray(r.results[0][f"dbg{i}"]) for i in range(3)])
    return out
```

```python
import numpy as np
from contextlib import ExitStack

L = 1024
D = 1024
KC = D // 128
FF = 2752
FT = 22
GROUPS = [4, 4, 4, 4, 3, 3]
EPS = 1e-6
N_INPROJ = 33
NEG = -1.0e30


def const_columns():
    cols = {}
    at = 0
    for name, n in [("norm1", 8), ("ffn1", 8), ("mixn", 8), ("ffn2", 8), ("fin", 8), ("gq", 1), ("gk", 1),
                    ("qn", 1), ("kn", 1), ("dnw", 1), ("one", 1), ("conv", 60), ("alog", 1), ("dtb", 1), ("fb", 4),
                    ("eps", 1), ("eps64", 1), ("eps128", 1),
                    ("ident", 128), ("ones", 128), ("bones", 128)]:
        cols[name] = (at, n)
        at += n
    return cols, at


class Mark:
    __slots__ = ("q", "need", "sem", "val")

    def __init__(self, q=None, sem=None, val=0):
        self.q, self.need, self.sem, self.val = q, False, sem, val


class Queue:
    def __init__(self, sem):
        self.sem, self.items = sem, []

    def __call__(self, fn, *after):
        m = Mark(self)
        self.items.append((flat(after), fn, m))
        return m

    def last(self):
        for _, fn, m in reversed(self.items):
            if fn is not None and m.q is not None:
                return m
        return None

    def number(self):
        n = 0
        for _, _, m in self.items:
            if m.q is not None and m.need:
                n += 1
                m.sem, m.val = self.sem, n

    def emit(self, eng):
        seen = {}
        for after, fn, m in self.items:
            want = {}
            for a in after:
                k = id(a.sem)
                if a.val > seen.get(k, 0) and a.val > want.get(k, (0, None))[0]:
                    want[k] = (a.val, a.sem)
            for k, (v, s) in want.items():
                eng.wait_ge(s, v)
                seen[k] = v
            if fn is None:
                continue
            ins = fn(eng)
            if m.q is None:
                ins.then_inc(m.sem, 16)
            elif m.need:
                ins.then_inc(self.sem, 1)


def flat(after):
    out = []
    for a in after:
        if a is None:
            continue
        if isinstance(a, (list, tuple)):
            out += flat(a)
        else:
            a.need = True
            out.append(a)
    return out


class DmaSem:

    def __init__(self, sem):
        self.sem, self.n = sem, 0

    def start(self, q, fn, *after):
        self.n += 16
        m = Mark(None, self.sem, self.n)
        q.items.append((flat(after), fn, m))
        return m


class Ring:

    def __init__(self, bufs):
        self.bufs, self.free, self.busy, self.i = bufs, [[] for _ in bufs], [False] * len(bufs), 0

    def take(self):
        i = self.i
        assert not self.busy[i], "taken before it was given back"
        self.i = (i + 1) % len(self.bufs)
        self.busy[i] = True
        return i, self.bufs[i], self.free[i]

    def give(self, i, *marks):
        assert self.busy[i]
        self.busy[i], self.free[i] = False, list(marks)


def build(nc, A):
    import concourse.bass as bass
    from concourse import mybir

    F = mybir.dt.float32
    R = mybir.dt.float32r
    ACT = mybir.ActivationFunctionType
    ALU = mybir.AluOpType
    AX = mybir.AxisListType.X
    MUL, ADD, SUB = ALU.mult, ALU.add, ALU.subtract

    cols, ncst = const_columns()
    top = ExitStack()
    sem = lambda n: top.enter_context(nc.semaphore(n))
    pe, act, dve, pool, sp = (Queue(sem("s_" + n)) for n in ("pe", "act", "dve", "pool", "sp"))
    engines = [pe, act, dve, pool]
    dsems = {}

    def dsem(name):
        if name not in dsems:
            dsems[name] = DmaSem(sem("d_" + name))
        return dsems[name]

    out_marks = []
    phase_dmas = []

    def load(name, dst, src, *after):
        m = dsem(name).start(sp, lambda e: e.dma_start(dst, src), *after)
        phase_dmas.append(m)
        return m

    def store(name, dst, src, *after):
        m = load(name, dst, src, *after)
        out_marks.append(m)
        return m

    def fence():
        marks = [q.last() for q in engines] + list(phase_dmas)
        phase_dmas.clear()
        for q in engines + [sp]:
            q.items.append((flat(marks), None, Mark(q)))

    names = [0]

    def sb(stack, shape, dt=F):
        names[0] += 1
        return stack.enter_context(nc.sbuf_tensor(f"t{names[0]}", shape, dt))

    scr = lambda n, shape: nc.dram_tensor(n, shape, F, kind="Internal").ap()
    pj = scr("pj", (N_INPROJ, 128, L))
    mixd = scr("mixd", (8, 128, L))
    mixd2 = scr("mixd2", (8, 128, L))

    ps = top.enter_context(nc.psum_tensor("ps", [128, 8, 512], F))
    slot = lambda s: ps[:, 2 * s:2 * s + 2, :].rearrange("p a n -> p (a n)")
    slots = Ring([slot(s) for s in range(4)])

    cst = sb(top, [128, ncst])
    cm = load("cst", cst[:], A["cst"])
    C = lambda n, i=0, w=1: cst[:, cols[n][0] + i:cols[n][0] + i + w]
    nh = sb(top, [128, 46])
    NH = lambda n, i=0: nh[:, cols[n][0] + i:cols[n][0] + i + 1]
    IDENT = C("ident", 0, 128)
    ONES = C("ones", 0, 128)
    BONES = C("bones", 0, 128)
    for q in engines:
        q.items.append((flat([cm]), None, Mark(q)))
    hm = dve(lambda e: e.tensor_scalar(nh[:], cst[:, 0:46], -0.5, None, MUL))
    dve.items.append((flat([hm]), None, Mark(dve)))

    def mm(out, lhsT, rhs, start, stop, *after):
        return pe(lambda e: e.matmul(out, lhsT, rhs, start=start, stop=stop), *after)

    def tr(out, in_, *after, n=128, ident=None):
        idn = IDENT[0:n, 0:n] if ident is None else ident
        return pe(lambda e: e.transpose(out, in_, idn), *after)

    def mm3(out, A_, B_, start, stop, *after):
        (ah, al), (bh, bl) = A_, B_
        mm(out, ah, bh, start, False, *after)
        mm(out, ah, bl, False, False)
        return mm(out, al, bh, False, stop)

    table = [None]

    def actf(out, in_, fn, *after, scale=1.0, bias=None, accum=None):
        if fn in (ACT.Exp, ACT.Ln) and table[0] != "lnexp":
            table[0] = "lnexp"
            act(lambda e: e.preload_act_table_set("natural_log_exp_and_others"))
        elif fn == ACT.Silu:
            table[0] = "silu"
        kw = {}
        if bias is not None:
            kw["bias"] = bias
        if accum is not None:
            kw["accum_out"] = accum
        return act(lambda e: e.activation(out, in_, fn, scale=scale, **kw), *after)

    def tt(q, out, a, b, op, *after):
        return q(lambda e: e.tensor_tensor(out, a, b, op), *after)

    def ts(q, out, a, s1, s2, op0, op1, *after):
        if op1 is None:
            return q(lambda e: e.tensor_scalar(out, a, s1, None, op0), *after)
        return q(lambda e: e.tensor_scalar(out, a, s1, s2, op0, op1), *after)

    def stt(out, a, s, b, op0, op1, *after):
        return dve(lambda e: e.scalar_tensor_tensor(out, a, s, b, op0, op1), *after)

    def recip(out, a, *after):
        return dve(lambda e: e.reciprocal(out, a), *after)

    def copy(q, out, a, *after):
        if q is act:
            return actf(out, a, ACT.Copy, *after)
        return q(lambda e: e.tensor_copy(out, a), *after)

    def memset(q, out, v, *after):
        return q(lambda e: e.memset(out, v), *after)

    def split(hi, lo, src, *after, q=pool):
        a = actf(hi, src, ACT.Copy, *after)
        b = tt(q, lo, src, hi.bitcast(F), SUB, a, *after)
        return [a, b]

    def split_psum(parts, *after):
        for hi, lo, src in parts:
            a = actf(hi, src, ACT.Copy, *after)
        for hi, lo, src in parts:
            b = tt(dve, lo, src, hi.bitcast(F), SUB, a, *after)
        return [a, b]

    def neg2_rsqrt(out, aux, p, scale, epsname, eps, *after):
        a = actf(aux, p, ACT.Ln, *after, scale=scale, bias=C(epsname))
        a = actf(out, aux, ACT.Exp, a, scale=-0.5)
        a = actf(aux, out, ACT.Square, a, scale=float(np.sqrt(scale)))
        d = stt(aux, p, eps / scale, aux, ADD, MUL, a)
        return d, stt(out, aux, -3.0, out, ADD, MUL, d)

    class Weights:
        NR, NS, AHEAD = 4, 3, 2

        def __init__(self):
            self.next = self.raws = self.splits = 0

        def open(self, stack, limit):
            self.limit = limit
            self.raw = Ring([sb(stack, [128, 1024]) for _ in range(self.NR)])
            self.sp = Ring([(sb(stack, [128, 1024], R), sb(stack, [128, 1024], R)) for _ in range(self.NS)])
            self.rawq, self.spq = [], []
            self.pump()

        def pump(self):
            while self.raws < min(self.next + self.NR, self.limit) and self.raws < self.splits + self.NR:
                n = self.raws
                i, buf, free = self.raw.take()
                m = dsem(f"w{i}").start(sp, lambda e, b=buf, n=n: e.dma_start(b[:], A["wts"][n]), *free)
                self.rawq.append((i, buf, m))
                self.raws += 1

        def split_one(self):
            i, buf, m = self.rawq.pop(0)
            k, (hi, lo), free = self.sp.take()
            marks = split(hi[:], lo[:], buf[:], m, free)
            self.raw.give(i, *marks)
            self.spq.append((k, hi, lo, marks))
            self.splits += 1
            self.pump()

        def get(self):
            while self.splits <= min(self.next + self.AHEAD, self.limit - 1):
                self.split_one()
            k, hi, lo, marks = self.spq.pop(0)
            self.next += 1
            self.k = k
            return hi, lo, marks

        def done(self, m):
            self.sp.give(self.k, m)

    W = Weights()

    def linear_tile(H, Lo, hready):
        wh, wl, wm = W.get()
        s, p, free = slots.take()
        for half in range(2):
            o = p[:, half * 512:half * 512 + 512]
            b = slice(half * 512, half * 512 + 512)
            for k in range(KC):
                a = slice(k * 128, k * 128 + 128)
                last = mm3(o, (wh[:, a], wl[:, a]), (H[:, k, b], Lo[:, k, b]), k == 0, k == KC - 1,
                           wm, free, hready[k])
        W.done(last)
        return s, p, last

    def rmsnorm(x, wname, xready, sink, stack):
        sq = Ring([sb(stack, [128, L]) for _ in range(2)])
        rs, aux = sb(stack, [128, L]), sb(stack, [128, L])
        tmp = Ring([sb(stack, [128, L]) for _ in range(2)])
        s, p, free = slots.take()
        for k in range(KC):
            i, b, f = sq.take()
            a = actf(b[:], x[:, k, :], ACT.Square, xready[k], f)
            for half in range(2):
                c = slice(half * 512, half * 512 + 512)
                m = mm(p[:, c], ONES, b[:, c], k == 0, k == KC - 1, a, free)
            sq.give(i, m)
        a, r = neg2_rsqrt(rs[:], aux[:], p, 1.0 / D, "eps", EPS, m)
        slots.give(s, a)
        for k in range(KC):
            i, b, f = tmp.take()
            m = stt(b[:], x[:, k, :], NH(wname, k), rs[:], MUL, MUL, r, xready[k], f)
            tmp.give(i, *sink(k, b, m))

    def norm_split(x, wname, xready, H, Lo, stack):
        ready = [None] * KC

        def sink(k, b, m):
            ready[k] = split(H[:, k, :], Lo[:, k, :], b[:], m)
            return ready[k]

        rmsnorm(x, wname, xready, sink, stack)
        return ready

    def phase_inproj():
        with ExitStack() as st:
            W.open(st, N_INPROJ)
            H, Lo = sb(st, [128, KC, L], R), sb(st, [128, KC, L], R)
            with ExitStack() as s2:
                x = sb(s2, [128, KC, L])
                xm = [load(f"x{k}", x[:, k, :], A["xT"][k]) for k in range(KC)]
                ready = norm_split(x, "norm1", xm, H, Lo, s2)
                ev = Ring([sb(s2, [128, L]) for _ in range(3)])
                for m in range(N_INPROJ):
                    s, p, done = linear_tile(H, Lo, ready)
                    i, b, f = ev.take()
                    c = copy(dve if m % 2 else act, b[:], p, done, f)
                    slots.give(s, c)
                    ev.give(i, store(f"ev{i}", pj[m], b[:], c))
            fence()

    def head_norm(big, raw, gain, epsname, scale, mraw, hi, lo, free, done, rope=None):
        (i1, sqb, f1), (i2, var, f2), (i3, qn, f3) = big.take(), big.take(), big.take()
        a = actf(sqb[:], raw, ACT.Square, mraw, f1)
        yield
        s, p, fr = slots_s.take()
        for half in range(2):
            c = slice(half * 512, half * 512 + 512)
            m = mm(p[:, c], BONES, sqb[:, c], True, True, a, fr)
        d = copy(dve, var[:], p, m, f2)
        slots_s.give(s, d)
        yield
        a = actf(qn[:], var[:], ACT.Ln, d, f3, scale=scale, bias=C(epsname))
        yield
        a = actf(sqb[:], qn[:], ACT.Exp, a, m, scale=-0.5)
        yield
        a = actf(qn[:], sqb[:], ACT.Square, a, scale=float(np.sqrt(scale)))
        yield
        d = stt(qn[:], var[:], {"eps": EPS, "eps64": 64 * EPS}[epsname] / scale, qn[:], ADD, MUL, a)
        yield
        d = stt(sqb[:], qn[:], -3.0, sqb[:], ADD, MUL, d)
        yield
        m = stt(qn[:], raw, NH(gain), sqb[:], MUL, MUL, d)
        last = m
        yield
        if rope is not None:
            cos, sin, rp = rope
            s, p, fr = slots_s.take()
            for half in range(2):
                c = slice(half * 512, half * 512 + 512)
                m2 = mm(p[:, c], rp, qn[:, c], True, True, m, fr)
            a1 = tt(dve, sqb[:], p, sin, MUL, m2)
            slots_s.give(s, a1)
            a2 = tt(pool, var[:], qn[:], cos, MUL, m)
            yield
            m = tt(dve, qn[:], var[:], sqb[:], ADD, a1, a2, m2)
            yield
        marks = split(hi[:], lo[:], qn[:], m, free)
        big.give(i1, m)
        big.give(i2, m)
        big.give(i3, *marks)
        done(marks, last)
        yield

    slots_s = None

    def value_tiles(vraw, vm, VH, VL, free):
        s, p, fr = slots_s.take()
        for t in range(8):
            m = tr(p[:, t * 128:t * 128 + 128], vraw[:, t * 128:t * 128 + 128], vm, fr)
        pv = p.rearrange("p (t f) -> p t f", t=8)
        cs = [slice(64 * j, 64 * j + 64) for j in range(2)]
        marks = split_psum([(VH[:, :, j, cs[j]], VL[:, :, j, cs[j]], pv[:, :, cs[j]]) for j in range(2)], m, free)
        slots_s.give(s, *marks)
        return marks

    def value_ones(VH, VL, one, zero, ready):
        marks = []
        for j in range(2):
            c = slice(64 * (1 - j), 64 * (1 - j) + 64)
            marks.append(copy(act, VH[:, :, j, c], one, ready))
            marks.append(copy(act, VL[:, :, j, c], zero, ready))
        return marks

    def attention(units, st, prep_at, background, pair_keys):
        P = Ring([sb(st, [128, L]) for _ in range(2)])
        PT = Ring([(sb(st, [128, pair_keys, 256], R), sb(st, [128, pair_keys, 256], R)) for _ in range(2)])
        nmx = Ring([sb(st, [128, 2]) for _ in range(4)])
        rec, rec2 = sb(st, [128, L]), sb(st, [128, L])
        tslot, oslot = Ring([ps[:, 4, :], ps[:, 5, :]]), Ring([slot(3)])
        state = {}

        def scores(u):
            s, p, fr = slots_s.take()
            j, t, nk, k0 = u["j"], u["t"], u["nk"], u["k0"]
            r = slice(64 * j, 64 * j + 64)
            qh, ql = u["q"]
            kh, kl = u["k"]
            for c in range(0, nk, 512):
                w = min(512, nk - c)
                m = mm3(p[:, c:c + w], (qh[r, t * 128:t * 128 + 128], ql[r, t * 128:t * 128 + 128]),
                        (kh[r, k0 + c:k0 + c + w], kl[r, k0 + c:k0 + c + w]), True, True, fr, u["ready"]())
            i, pb, f = P.take()
            n, mx, fn_ = nmx.take()
            u["S"] = (s, p, i, pb)
            if u["bias"] is not None:
                b, bm = u["bias"]
                a = dve(lambda e: e.tensor_tensor_reduce(pb[:, 0:nk], p[:, 0:nk], b, 1.0, NEG, ADD, ALU.max,
                                                         mx[:, 1:2]), m, f, fn_, bm)
                a2 = ts(dve, mx[:, 0:1], mx[:, 1:2], -1.0, None, MUL, None, a)
                slots_s.give(s, a)
                u["bias_done"](a)
            else:
                a2 = dve(lambda e: e.tensor_reduce(mx[:, 0:1], p[:, 0:nk], AX, ALU.max, negate=True), m, fn_)
            u["max"] = (n, mx, a2, f)
            if u["last_scores"]:
                u["last_scores"](m)

        def exps(u):
            s, p, i, pb = u["S"]
            n, mx, a2, f = u["max"]
            nk = u["nk"]
            if u["bias"] is not None:
                e_ = actf(pb[:, 0:nk], pb[:, 0:nk], ACT.Exp, a2, bias=mx[:, 0:1])
            else:
                e_ = actf(pb[:, 0:nk], p[:, 0:nk], ACT.Exp, a2, f, bias=mx[:, 0:1])
                slots_s.give(s, e_)
            nmx.give(n, e_)
            u["P"] = (i, pb, e_)

        def transposes(u):
            i, pb, e_ = u["P"]
            nk = u["nk"]
            if u["t"] % 2 == 0:
                state["PT"] = PT.take()
                state["marks"] = []
            k, (ph, pl), f = state["PT"]
            o = 128 * (u["t"] % 2)
            at = (u["k0"] - u["base"]) // 128
            banks = []
            for c0 in range(0, nk, 512):
                s, p, fr = tslot.take()
                for c in range(c0, min(nk, c0 + 512), 128):
                    w = min(128, nk - c)
                    m = tr(p[0:w, c - c0:c - c0 + 128], pb[:, c:c + w], e_, fr)
                n = (min(nk, c0 + 512) - c0) // 128
                kk = at + c0 // 128
                if n:
                    w, src = 128, p[:, 0:n * 128].rearrange("p (k n) -> p k n", k=n)
                    hi, lo = ph[:, kk:kk + n, o:o + 128], pl[:, kk:kk + n, o:o + 128]
                else:
                    src, hi, lo = p[0:64, 0:128], ph[0:64, kk, o:o + 128], pl[0:64, kk, o:o + 128]
                banks.append((s, m, hi, lo, src))
            P.give(i, m)
            his = [actf(hi, src, ACT.Copy, m, f) for s, m, hi, lo, src in banks]
            for (s, m, hi, lo, src), a in zip(banks, his):
                b = tt(dve, lo, src, hi.bitcast(F), SUB, a)
                tslot.give(s, a, b)
                state["marks"] += [a, b]
            u["PT"] = (k, ph, pl, state["marks"])

        def values(u):
            k, ph, pl, marks = u["PT"]
            j, t, nk, base = u["j"], u["t"], u["nk"], u["base"]
            if t == 1:
                state["o"] = oslot.take()
            s, o, fr = state["o"]
            VH, VL = u["v"]
            if nk % 128 == 0:
                steps = [(i, 128, 0, 256) for i in range(nk // 128)]
            else:
                steps = [(1, 128, 0, 256), (2, 128, 0, 256), (3, 128, 0, 256), (0, 128, 0, 128), (4, 64, 0, 128),
                         (4, 128, 128, 256), (5, 64, 128, 256)]
            q0 = (t - 1) * 128
            for n_, (i, w, a, b) in enumerate(steps):
                kt = base // 128 + i
                m = mm3(o[:, q0 + a:q0 + b], (VH[0:w, kt, j, :], VL[0:w, kt, j, :]),
                        (ph[0:w, i, a:b], pl[0:w, i, a:b]), n_ == 0, n_ == len(steps) - 1, marks, fr, u["ready"]())
            PT.give(k, m)
            if t == 7:
                a, b = slice(64 * j, 64 * j + 64), slice(64 - 64 * j, 128 - 64 * j)
                r = actf(rec[a, :], o[b, :], ACT.Ln, m, state.get("rec%d" % j))
                r = actf(rec[a, :], rec[a, :], ACT.Exp, r, scale=-1.0)
                r = tt(dve, rec2[a, :], o[b, :], rec[a, :], MUL, r)
                r = stt(rec[a, :], rec2[a, :], -2.0, rec[a, :], ADD, MUL, r)
                out, f = u["out"]()
                z = stt(out[a, :], o[a, :], -1.0, rec[a, :], MUL, MUL, r, f)
                state["rec%d" % j] = z
                oslot.give(s, z)
                u["finish"](z, m)

        n = len(units)
        for i in range(n + 2):
            if i in prep_at:
                prep_at[i]()
            if i < n:
                scores(units[i])
            if 1 <= i <= n:
                transposes(units[i - 1])
            if i < n:
                exps(units[i])
            if i >= 2 and i % 2 == 1:
                values(units[i - 2])
            for _ in range(2):
                if background:
                    if next(background[0], "end") == "end":
                        background.pop(0)

    def phase_na():
        nonlocal slots_s
        slots_s = Ring([slot(0), slot(1)])
        with ExitStack() as st:
            raws = Ring([tuple(sb(st, [128, L]) for _ in range(4)) for _ in range(2)])
            big = Ring([sb(st, [128, L]) for _ in range(3)])
            QK = Ring([tuple(sb(st, [128, L], R) for _ in range(4)) for _ in range(2)])
            V = Ring([tuple(sb(st, [128, 8, 2, 128], R) for _ in range(2)) for _ in range(2)])
            tab = Ring([sb(st, [128, 23 * 64]) for _ in range(2)])
            outs = Ring([sb(st, [128, L]) for _ in range(1)])
            one, zero = sb(st, [128, 8, 64]), sb(st, [128, 8, 64])
            om = [memset(dve, one[:], 1.0), memset(dve, zero[:], 0.0)]
            vinit = [value_ones(VH, VL, one[:], zero[:], om) for VH, VL in V.bufs]
            loads, chunks, tabs = {}, {}, {}

            def fetch(c):
                i, bufs, f = raws.take()
                ms = [load(f"na{i}{n}", bufs[n][:], pj[4 * n + c], f) for n in range(4)]
                loads[c] = (i, bufs, ms)

            def fetch_tab(h):
                i, b, f = tab.take()
                tabs[h] = (i, b, load(f"tab{i}", b[:], A["rpb"][h], f))

            def prep(c):
                i, (q, k, v, z), ms = loads[c]
                qi, (qh, ql, kh, kl), f = QK.take()
                vi, (VH, VL), fv = V.take()
                ready = []
                done = lambda marks, last: ready.extend(marks)
                yield from head_norm(big, q[:], "gq", "eps64", 1.0, ms[0], qh, ql, f, done)
                yield from head_norm(big, k[:], "gk", "eps", 1.0 / 64, ms[1], kh, kl, f, done)
                ready += value_tiles(v, ms[2], VH, VL, fv)
                yield
                m4 = actf(z[:], z[:], ACT.Silu, ms[3])
                chunks[c] = dict(i=i, z=z, zm=m4, qi=qi, vi=vi, q=(qh, ql), k=(kh, kl), v=(VH, VL),
                                 ready=ready + vinit[vi])

            units = []
            state = {}
            for c in range(4):
                for j in range(2):
                    h = 2 * c + j
                    for t in range(8):
                        if t < 2:
                            nk, k0, b0 = 512, 0, (7 - 2 * t - 1) * 64
                        elif t >= 6:
                            nk, k0, b0 = 512, 512, (8 - 2 * t + 7 - 1) * 64
                        else:
                            nk, k0, b0 = 576, (2 * t - 4) * 64, 14 * 64
                        u = dict(c=c, j=j, h=h, t=t, nk=nk, k0=k0, base=[0, 0, 256, 512][t // 2])
                        units.append(u)

                        class Late:
                            pass
                        u["b0"] = b0

            def bind(c, j):
                ch = chunks[c]
                i, b, bm = tabs[2 * c + j]
                for u in units[(2 * c + j) * 8:(2 * c + j) * 8 + 8]:
                    u["q"], u["k"], u["v"] = ch["q"], ch["k"], ch["v"]
                    u["ready"] = lambda ch=ch: ch["ready"]
                    u["bias"] = (b[:, u["b0"]:u["b0"] + u["nk"]], bm)
                    u["bias_done"] = (lambda a, i=i: tab.give(i, a)) if u["t"] == 7 else (lambda a: None)
                    u["last_scores"] = (lambda m, ch=ch: QK.give(ch["qi"], m)) if (u["t"] == 7 and j == 1) else None

                    def out(j=j):
                        if j == 0:
                            state["out"] = outs.take()
                        return state["out"][1], state["out"][2]
                    u["out"] = out

                    def finish(z, m, ch=ch, j=j, c=c):
                        if j == 0:
                            state["z0"] = z
                            return
                        oi, ob, _ = state["out"]
                        g = tt(dve, ob[:], ob[:], ch["z"][:], MUL, z, state["z0"], ch["zm"])
                        V.give(ch["vi"], m)
                        raws.give(ch["i"], g)
                        outs.give(oi, store(f"nao{oi}", mixd[c], ob[:], g))
                    u["finish"] = finish

            fetch(0)
            fetch(1)
            fetch_tab(0)
            prep_at = {}

            def at(i, *fns):
                old = prep_at.get(i)

                def run():
                    if old:
                        old()
                    for f in fns:
                        f()
                prep_at[i] = run
            background = []

            def drain():
                while background:
                    for _ in background.pop(0):
                        pass
            at(0, lambda: background.append(prep(0)), drain)
            for c in range(4):
                for j in range(2):
                    h = 2 * c + j
                    if j == 0:
                        at(8 * h, drain)
                    at(8 * h, lambda c=c, j=j: bind(c, j))
                    if h < 7:
                        at(8 * h + 1, lambda h=h: fetch_tab(h + 1))
            for c in range(1, 4):
                at(16 * (c - 1) + 5, lambda c=c: background.append(prep(c)))
                if c + 1 < 4:
                    at(16 * c + 2, lambda c=c: fetch(c + 1))
            attention(units, st, prep_at, background, 6)
            fence()

    def phase_delta():
        with ExitStack() as st:
            slots = Ring([slot(s) for s in range(4)])
            dm = sb(st, [128, 14, 128])
            dmm = load("dm", dm[:], A["dmask"])
            TRI = [dm[:, 0, :], dm[:, 1, :]]
            LEV = [[dm[:, 2 + d * 6 + l, :] for l in range(6)] for d in range(2)]

            beta, G, eg, ed, bg = (sb(st, [128, 8, 8]) for _ in range(5))
            gt = sb(st, [128, 8, 64])
            with ExitStack() as s2:
                gr, w1, w2, w3 = (sb(s2, [64, L]) for _ in range(4))
                nA = sb(s2, [64, 1])
                b_, a_ = slice(0, 32), slice(32, 64)
                g0 = load("gate", gr[:], pj[32, 0:64, :])
                x1 = actf(w1[b_, :], gr[b_, :], ACT.Exp, g0, scale=-1.0)
                x1 = ts(dve, w1[b_, :], w1[b_, :], 1.0, None, ADD, None, x1)
                x1 = recip(gr[b_, :], w1[b_, :], x1)
                y0 = ts(dve, w1[a_, :], gr[a_, :], C("dtb")[a_, :], None, ADD, None, g0)
                y1 = actf(w2[a_, :], w1[a_, :], ACT.Abs, y0)
                y1 = actf(w2[a_, :], w2[a_, :], ACT.Exp, y1, scale=-1.0)
                y1 = actf(w2[a_, :], w2[a_, :], ACT.Ln, y1, bias=C("one")[a_, :])
                y2 = ts(dve, w3[a_, :], w1[a_, :], 0.0, None, ALU.max, None, y0)
                y3 = tt(dve, w3[a_, :], w3[a_, :], w2[a_, :], ADD, y1, y2)
                n1 = actf(nA[a_, :], C("alog")[a_, :], ACT.Exp)
                y4 = ts(dve, gr[a_, :], w3[a_, :], nA[a_, :], -1.0, MUL, MUL, y3, n1, y0)
                s, p, fr = slots.take()
                for t in range(8):
                    m = tr(p[:, t * 64:t * 64 + 64], gr[:, t * 128:t * 128 + 128], x1, y4, fr, n=64)
                c1 = copy(dve, gt[:], p[:, 0:512].rearrange("p (t f) -> p t f", t=8), m)
                slots.give(s, c1)
                c2 = copy(dve, beta[:], gt[:, :, 0:8], c1)
                s, p, fr = slots.take()
                pg = p.rearrange("p (a n) -> p a n", a=2)
                for d in range(2):
                    m = mm(pg[:, 0, 32 * d:32 * d + 32], TRI[d], gt[:, :, 32 + 4 * d:36 + 4 * d], True, True,
                           c1, fr, dmm)
                m2 = mm(pg[:, 1, 0:64], BONES, gt[:, :, 32:40], True, True, c1, fr)
                gs = []
                for d in range(2):
                    gs.append(copy(dve, G[:, :, 4 * d:4 * d + 4],
                                   pg[:, 0, 32 * d:32 * d + 32].rearrange("p (t h) -> p t h", t=8), m2))
                c3 = tt(dve, ed[:], pg[:, 1, 0:64].rearrange("p (t h) -> p t h", t=8), G[:], SUB, gs)
                slots.give(s, c3)
                e1 = actf(ed[:], ed[:], ACT.Exp, c3)
                e2 = actf(eg[:], G[:], ACT.Exp, gs)
                e3 = tt(dve, bg[:], eg[:], beta[:], MUL, e2, c2)
                gate_ready = [c1, c2, e1, e2, e3, dmm] + gs
                fence()

            bc8 = lambda a: a.unsqueeze(1).to_broadcast([128, 8, 128])
            bcl = lambda a: a.unsqueeze(2).to_broadcast([128, 8, 128])
            v8 = lambda a: a.rearrange("p (t f) -> p t f", t=8)

            raw = Ring([sb(st, [128, L + 4]) for _ in range(2)])
            rz = [memset(pool, b[:, c:c + 2], 0.0) for b in raw.bufs for c in (0, L + 2)]
            cv = Ring([sb(st, [128, L]) for _ in range(2)])
            sqb = sb(st, [128, L])
            sq_free = [None]
            heads = [dict(q=sb(st, [128, L]), k=sb(st, [128, L]), kt=sb(st, [128, L]), vt=sb(st, [128, L]),
                          O=sb(st, [128, L])) for _ in range(2)]
            hds = [dict(D=sb(st, [128, L]), MT=sb(st, [128, L]), X=sb(st, [128, L]), Y=sb(st, [128, L]),
                        vb=sb(st, [128, L]), kb=sb(st, [128, L]), qg=sb(st, [128, L]), egl=sb(st, [128, 16]),
                        S=sb(st, [128, 128]), vn=sb(st, [128, 128])) for _ in range(4)]
            EB = Ring([sb(st, [128, L]) for _ in range(2)])
            P1 = Ring([sb(st, [128, L]) for _ in range(2)])
            mslots = Ring([slot(i) for i in range(3)])
            mslots.free = [list(slots.free[i]) for i in range(3)]
            last_free = list(slots.free[3])
            slots = Ring([slot(3)])
            slots.free = [last_free]

            def fetch_raw(row):
                i, b, f = raw.take()
                return i, b, load(f"dr{i}", b[:, 2:L + 2], pj[row], f)

            def conv(row, wi, q=dve):
                i, b, lm = fetch_raw(row)
                k, c, f = cv.take()
                if q is dve:
                    m = ts(dve, c[:], b[:, 0:L], C("conv", wi * 5), None, MUL, None, lm, f, rz)
                    for tap in range(1, 5):
                        m = stt(c[:], b[:, tap:tap + L], C("conv", wi * 5 + tap), c[:], MUL, ADD, m)
                        if tap % 2 == 0:
                            yield
                    raw.give(i, m)
                    return k, c, m
                e, E, ef = EB.take()
                m = act(lambda e_: e_.activation(c[:], b[:, 0:L], ACT.Copy, scale=C("conv", wi * 5)), lm, f, rz)
                for tap in range(1, 5):
                    a = act(lambda e_, t=tap: e_.activation(E[:], b[:, t:t + L], ACT.Copy,
                                                            scale=C("conv", wi * 5 + t)), ef)
                    m = tt(pool, c[:], c[:], E[:], ADD, a, m)
                    ef = m
                    yield
                EB.give(e, m)
                raw.give(i, a)
                return k, c, m

            def l2norm(buf, mark, scale, epsname):
                a = actf(sqb[:], buf, ACT.Square, mark, sq_free[0])
                s, p, fr = slots.take()
                for half in range(2):
                    c = slice(half * 512, half * 512 + 512)
                    m = mm(p[:, c], ONES, sqb[:, c], True, True, a, fr)
                i, c, f = cv.take()
                a = actf(c[:], p, ACT.Ln, m, f, scale=scale, bias=C(epsname))
                yield
                a = actf(sqb[:], c[:], ACT.Exp, a, scale=-0.5)
                a = actf(c[:], sqb[:], ACT.Square, a, scale=float(np.sqrt(scale)))
                yield
                a = stt(c[:], p, EPS, c[:], ADD, MUL, a)
                slots.give(s, a)
                yield
                r = stt(sqb[:], c[:], -3.0, sqb[:], ADD, MUL, a)
                cv.give(i, r)
                yield
                m = stt(buf, buf, -0.5, sqb[:], MUL, MUL, r)
                sq_free[0] = m
                return m

            def to_tokens(src, dst, mark, free):
                s, p, fr = slots.take()
                for t in range(8):
                    m = tr(p[:, t * 128:t * 128 + 128], src[:, t * 128:t * 128 + 128], mark, fr)
                c = copy(act, dst, p, m, free)
                slots.give(s, c)
                return c

            def prep_head(h, hb, last):
                marks = []
                for n, (name, q) in enumerate((("q", dve), ("k", pool), ("O", pool))):
                    k, c, m = yield from conv(16 + 4 * n + h, 4 * n + h, q)
                    a = actf(hb[name][:], c[:], ACT.Silu, m, last)
                    cv.give(k, a)
                    marks.append(a)
                    yield
                hb["vtm"] = to_tokens(hb["O"], hb["vt"][:], marks[2], last)
                yield
                hb["qm"] = yield from l2norm(hb["q"][:], marks[0], 128.0, "eps128")
                yield
                hb["km"] = yield from l2norm(hb["k"][:], marks[1], 1.0, "eps")
                yield
                hb["ktm"] = to_tokens(hb["k"], hb["kt"][:], hb["km"], last)
                yield

            def gate_rows(g, src, col, rhs):
                s, p, fr = slots.take()
                for t in range(8):
                    m = mm(p[:, t * 128:t * 128 + 128], src[:, t, col:col + 1].to_broadcast([128, 128]), rhs,
                           True, True, fr, gate_ready)
                return s, p, m

            def prep_dir(h, d, hb, g, last):
                hd = h + 4 * d
                s, p, m = gate_rows(g, gt, 32 + hd, TRI[d])
                ei, E, ef = EB.take()
                x = actf(E[:], p, ACT.Exp, m, ef)
                for t in range(8):
                    c = slice(t * 128, t * 128 + 128)
                    y = ts(dve, g["D"][:, c], p[:, c], G[:, t, hd:hd + 1], 0.0, SUB, ALU.min, m, x, last)
                slots.give(s, x, y)
                yield
                y = actf(g["D"][:], g["D"][:], ACT.Exp, y)
                y = tt(pool, v8(g["D"][:]), v8(g["D"][:]), bc8(TRI[d]), MUL, y)
                g["eglm"] = copy(dve, g["egl"][:], E[:, (63 if d == 0 else 0)::64], x, last)
                g["qgm"] = tt(pool, g["qg"][:], hb["q"][:], E[:], MUL, x, hb["qm"], last)
                EB.give(ei, g["eglm"], g["qgm"])
                yield
                s, p, m = gate_rows(g, gt, hd, IDENT)
                ei, kbT, ef = EB.take()
                b = tt(dve, kbT[:], hb["k"][:], p, MUL, m, hb["km"], ef)
                slots.give(s, b)
                yield
                s, p, fr = slots.take()
                for t in range(8):
                    c = slice(t * 128, t * 128 + 128)
                    m = mm(p[:, c], hb["k"][:, c], kbT[:, c], True, True, b, fr)
                EB.give(ei, m)
                mt = tt(dve, g["MT"][:], p, g["D"][:], MUL, m, y, last)
                slots.give(s, mt)
                yield
                g["Dm"] = y
                g["MTm"] = mt
                m1 = LEV[1 - d][0]
                a = tt(pool, v8(g["Y"][:]), v8(g["MT"][:]), bc8(m1), MUL, mt, last)
                yield
                a = tt(dve, v8(g["Y"][:]), bc8(IDENT), v8(g["Y"][:]), SUB, a)
                g["Ym"] = a
                s, p, fr = slots.take()
                for t in range(8):
                    c = slice(t * 128, t * 128 + 128)
                    m = tr(p[:, c], g["Y"][:, c], a, fr)
                g["Xm"] = copy(act, g["X"][:], p, m, last)
                slots.give(s, g["Xm"])
                yield
                g["vbm"] = tt(pool, v8(g["vb"][:]), v8(hb["vt"][:]), bcl(beta[:, :, hd]), MUL, hb["vtm"], last)
                g["kbm"] = tt(pool, v8(g["kb"][:]), v8(hb["kt"][:]), bcl(bg[:, :, hd]), MUL, hb["ktm"], last)
                yield

            def prep_intra(hb, pair):
                s, p, fr = slots.take()
                for t in range(8):
                    c = slice(t * 128, t * 128 + 128)
                    m = mm(p[:, c], hb["k"][:, c], hb["q"][:, c], True, True, fr, hb["qm"], hb["km"])
                for g in pair:
                    g["Im"] = tt(dve, g["D"][:], p, g["D"][:], MUL, m, g["Dm"], g["MTm"])
                slots.give(s, *[g["Im"] for g in pair])
                yield

            def level(l, gs):
                todo = []
                for d, g in gs:
                    s, p, fr = mslots.take()
                    for t in range(8):
                        c = slice(t * 128, t * 128 + 128)
                        m = mm(p[:, c], g["MT"][:, c], g["X"][:, c], True, True, g["MTm"], g["Xm"], fr)
                    i, b, f = P1.take()
                    a = tt(dve, v8(b[:]), v8(p), bc8(LEV[d][l]), MUL, m, f)
                    mslots.give(s, a)
                    todo.append((i, b, a))
                yield 2
                for (d, g), (i, b, a) in zip(gs, todo):
                    m2 = None
                    if l < 5:
                        s2, p2, fr2 = mslots.take()
                        for t in range(8):
                            c = slice(t * 128, t * 128 + 128)
                            m2 = mm(p2[:, c], g["Y"][:, c], b[:, c], True, True, a, g["Ym"], fr2)
                        g["Xm"] = tt(dve, g["X"][:], g["X"][:], p2, SUB, m2)
                        mslots.give(s2, g["Xm"])
                    s, p, fr = mslots.take()
                    for t in range(8):
                        c = slice(t * 128, t * 128 + 128)
                        m = mm(p[:, c], b[:, c], g["Y"][:, c], True, True, a, g["Ym"], fr)
                    g["Ym"] = tt(dve, g["Y"][:], g["Y"][:], p, SUB, m)
                    P1.give(i, m)
                    mslots.give(s, g["Ym"])
                    yield 1

            def apply(g, hb, hd):
                s, p, fr = mslots.take()
                for t in range(8):
                    c = slice(t * 128, t * 128 + 128)
                    m = mm(p[:, c], g["Y"][:, c], g["vb"][:, c], True, True, g["Ym"], g["vbm"], fr)
                g["um"] = copy(act, g["vb"][:], p, m)
                mslots.give(s, g["um"])
                s, p, fr = mslots.take()
                for t in range(8):
                    c = slice(t * 128, t * 128 + 128)
                    m = mm(p[:, c], g["kb"][:, c], g["Y"][:, c], True, True, g["kbm"], fr)
                g["wm"] = copy(dve, g["kb"][:], p, m)
                mslots.give(s, g["wm"])
                g["kdm"] = tt(pool, v8(g["MT"][:]), v8(hb["kt"][:]), bcl(ed[:, :, hd]), MUL, g["Ym"], hb["ktm"])

            def scan(gs, hb):
                banks = Ring([ps[:, i, :] for i in range(6)])
                for i in range(6):
                    banks.free[i] = list(mslots.free[i // 2])
                for _, g in gs:
                    g["Sm"] = memset(dve, g["S"][:], 0.0, hb["last"])
                    g["vfree"] = hb["last"]
                seen = {}
                hb["Om"] = []
                for n in range(16):
                    work = []
                    for d, g in gs:
                        ch = n if d == 0 else 15 - n
                        t, j = ch // 2, ch % 2
                        r, c, cc = slice(64 * j, 64 * j + 64), slice(64 * ch, 64 * ch + 64), slice(128 * t, 128 * t + 128)
                        i, p, fr = banks.take()
                        m = mm(p[r, 0:128], g["kb"][:, c], g["S"][:], True, True, g["wm"], g["Sm"], fr)
                        v = tt(dve, g["vn"][r, :], g["vb"][r, cc], p[r, 0:128], SUB, m, g["um"], g["vfree"])
                        banks.give(i, v)
                        work.append((d, g, ch, r, c, cc, v))
                    outs = []
                    for d, g, ch, r, c, cc, v in work:
                        i, p, fr = banks.take()
                        mm(p[:, 0:64], g["S"][:], g["qg"][:, c], True, False, g["qgm"], fr)
                        outs.append((i, p))
                    for (d, g, ch, r, c, cc, v), (i, p) in zip(work, outs):
                        i2, p2, fr2 = banks.take()
                        ms = mm(p2[:, 0:128], g["MT"][r, cc], g["vn"][r, :], True, True, v, g["kdm"], fr2)
                        mo = mm(p[:, 0:64], g["vn"][r, :], g["D"][r, c], False, True, v, g["Im"])
                        g["vfree"] = mo
                        g["Sm"] = stt(g["S"][:], g["S"][:], g["egl"][:, ch:ch + 1], p2[:, 0:128], MUL, ADD, ms,
                                      g["eglm"], g["Sm"])
                        banks.give(i2, g["Sm"])
                        if ch not in seen:
                            seen[ch] = copy(act, hb["O"][:, c], p[:, 0:64], mo, hb["vtm"])
                        else:
                            seen[ch] = tt(dve, hb["O"][:, c], hb["O"][:, c], p[:, 0:64], ADD, mo, seen[ch])
                        hb["Om"].append(seen[ch])
                        banks.give(i, seen[ch])
                    yield 1
                for i in range(3):
                    mslots.free[i] = banks.free[2 * i] + banks.free[2 * i + 1]
                hb["scan_end"] = [mo, ms] + [g["Sm"] for _, g in gs]

            def finish_head(h, hb, pair):
                sq, aux, c, z = pair[0]["X"], pair[1]["X"], pair[0]["Y"], pair[1]["Y"]
                lm = load(f"dz{h % 2}", z[:], pj[28 + h], hb["scan_end"])
                a = actf(sq[:], hb["O"][:], ACT.Square, hb["Om"], hb["scan_end"])
                s, p, fr = slots.take()
                for half in range(2):
                    cc = slice(half * 512, half * 512 + 512)
                    m = mm(p[:, cc], ONES, sq[:, cc], True, True, a, fr)
                yield
                za = actf(z[:], z[:], ACT.Silu, lm)
                a, r = neg2_rsqrt(sq[:], aux[:], p, 1.0 / 128, "eps", EPS, m)
                slots.give(s, a)
                yield
                m = stt(c[:], hb["O"][:], NH("dnw"), sq[:], MUL, MUL, r)
                m2 = tt(pool, c[:], c[:], z[:], MUL, m, za)
                hb["last"] = [store(f"cvo{h % 2}", mixd[4 + h], c[:], m2), r, m, m2] + hb["scan_end"]
                yield

            def prepare(h):
                hb, pair = heads[h % 2], hds[2 * (h % 2):2 * (h % 2) + 2]
                yield from prep_head(h, hb, hb["last"])
                for d in range(2):
                    yield from prep_dir(h, d, hb, pair[d], hb["last"])
                yield from prep_intra(hb, pair)

            def main(h):
                hb, pair = heads[h % 2], hds[2 * (h % 2):2 * (h % 2) + 2]
                gs = [(d, pair[d]) for d in range(2)]
                for l in range(1, 6):
                    yield from level(l, gs)
                for d in range(2):
                    apply(pair[d], hb, h + 4 * d)
                    yield 1
                yield from scan(gs, hb)

            for hb in heads:
                hb["last"] = []
            for _ in prepare(0):
                pass
            for h in range(4):
                back = []
                if h > 0:
                    back.append(finish_head(h - 1, heads[(h - 1) % 2], hds[2 * ((h - 1) % 2):2 * ((h - 1) % 2) + 2]))
                if h < 3:
                    back.append(prepare(h + 1))
                for n in main(h):
                    for _ in range(n):
                        if back and next(back[0], "end") == "end":
                            back.pop(0)
                for b in back:
                    for _ in b:
                        pass
            for _ in finish_head(3, heads[1], hds[2:4]):
                pass
            fence()

    def phase_outproj(x, xready, src, st):
        with ExitStack() as s2:
            H, Lo = sb(s2, [128, KC, L], R), sb(s2, [128, KC, L], R)
            tmp = Ring([sb(s2, [128, L]) for _ in range(2)])
            ready = []
            for k in range(KC):
                i, b, f = tmp.take()
                m = load(f"op{i}", b[:], src[k], f)
                ready.append(split(H[:, k, :], Lo[:, k, :], b[:], m))
                tmp.give(i, *ready[k])
            for m in range(KC):
                s, p, done = linear_tile(H, Lo, ready)
                xready[m] = tt(dve, x[:, m, :], x[:, m, :], p, ADD, done, xready[m])
                slots.give(s, xready[m])
            fence()
        return xready

    def phase_ffn(x, wname, xready):
        with ExitStack() as st:
            H, Lo = sb(st, [128, KC, L], R), sb(st, [128, KC, L], R)
            with ExitStack() as s2:
                ready = norm_split(x, wname, xready, H, Lo, s2)
                fence()
            AB = Ring([(sb(st, [128, L], R), sb(st, [128, L], R)) for _ in range(5)])
            sg = Ring([sb(st, [128, L]) for _ in range(1)])
            ab = Ring([sb(st, [128, L]) for _ in range(2)])
            tiles = []

            def gate_up():
                s1, pg, mg = linear_tile(H, Lo, ready)
                s2_, pu, mu = linear_tile(H, Lo, ready)
                i, g, f = sg.take()
                a = actf(g[:], pg, ACT.Silu, mg, f)
                slots.give(s1, a)
                k, b, f = ab.take()
                m = tt(dve, b[:], pu, g[:], MUL, mu, a, f)
                slots.give(s2_, m)
                sg.give(i, m)
                n, (ah, al), f = AB.take()
                marks = split(ah[:], al[:], b[:], m, f)
                ab.give(k, *marks)
                tiles.append((n, ah, al, marks))

            def down(nk):
                grp = tiles[:nk]
                del tiles[:nk]
                for mp in range(4):
                    wh, wl, wm = W.get()
                    for m in range(2):
                        s, p, fr = slots.take()
                        for half in range(2):
                            c = slice(half * 512, half * 512 + 512)
                            for k, (n, ah, al, marks) in enumerate(grp):
                                a = slice((k * 2 + m) * 128, (k * 2 + m) * 128 + 128)
                                last = mm3(p[:, c], (wh[:, a], wl[:, a]), (ah[:, c], al[:, c]),
                                           k == 0, k == nk - 1, wm, fr, marks)
                        o = 2 * mp + m
                        xready[o] = stt(x[:, o, :], p, 0.5, x[:, o, :], MUL, ADD, last, xready[o])
                        slots.give(s, xready[o])
                    W.done(last)
                for n, _, _, _ in grp:
                    AB.give(n, last)

            for _ in range(GROUPS[0]):
                gate_up()
            for g, nk in enumerate(GROUPS):
                if g + 1 < len(GROUPS):
                    gate_up()
                down(nk)
                if g + 1 < len(GROUPS):
                    for _ in range(GROUPS[g + 1] - 1):
                        gate_up()
            fence()
        return xready

    def phase_mix2(x, xready):
        nonlocal slots_s
        with ExitStack() as st:
            UH, UL = sb(st, [128, 4, L], R), sb(st, [128, 4, L], R)
            qkv = sb(st, [128, 6, L])
            qm = [None] * 6
            um = [None] * 4
            with ExitStack() as s2:
                H, Lo = sb(s2, [128, KC, L], R), sb(s2, [128, KC, L], R)
                with ExitStack() as s3:
                    ready = norm_split_in(x, "mixn", xready, H, Lo, qkv)
                    fence()
                for m in range(10):
                    s, p, done = linear_tile(H, Lo, ready)
                    if m < 4:
                        um[m] = split(UH[:, m, :], UL[:, m, :], p, done, q=dve)
                        slots.give(s, *um[m])
                    else:
                        qm[m - 4] = copy(dve if m % 2 else act, qkv[:, m - 4, :], p, done)
                        slots.give(s, qm[m - 4])
                fence()
            for g in range(6):
                store(f"q2{g}", pj[g], qkv[:, g, :], qm[g])
            with ExitStack() as s2:
                TH, TL = sb(s2, [128, 8, 4, 256], R), sb(s2, [128, 8, 4, 256], R)
                wh, wl, wm = W.get()
                tm = []
                for t in range(8):
                    s, p, fr = slots.take()
                    c = slice(t * 128, t * 128 + 128)
                    for g in range(4):
                        m = mm3(p[:, g * 256:g * 256 + 256], (UH[:, g, c], UL[:, g, c]),
                                (wh[:, 0:256], wl[:, 0:256]), True, True, fr, wm, um[g])
                    marks = split(TH[:, t, :, :].rearrange("p g n -> p (g n)"),
                                  TL[:, t, :, :].rearrange("p g n -> p (g n)"), p, m, q=dve)
                    tm.append(marks)
                    slots.give(s, *marks)
                W.done(m)
                alt = sb(s2, [128, 2], R)
                y5 = sb(s2, [128, 8])
                am = load("alt", y5[:, 0:2], A["alt"])
                am = actf(alt[:], y5[:, 0:2], ACT.Copy, am)
                s, p, fr = slots.take()
                for g in range(4):
                    for t in range(8):
                        mm(p[:, 2 * g:2 * g + 2], TH[:, t, g, 0:128], alt[:], t == 0, False, tm[t], am, fr)
                        m = mm(p[:, 2 * g:2 * g + 2], TL[:, t, g, 0:128], alt[:], False, t == 7)
                y5m = actf(y5[:], p[:, 0:8], ACT.Copy, m, am, scale=float(1.0 / np.sqrt(L * 128.0)))
                slots.give(s, y5m)
                taken = [slots.take() for _ in range(4)]
                for t in range(8):
                    wh, wl, wm = W.get()
                    for g in range(4):
                        s, p, fr = taken[g]
                        for d in range(2):
                            a, b = slice(d * 128, d * 128 + 128), slice(d * 512, d * 512 + 512)
                            m = mm3(p[:, b], (TH[:, t, g, a], TL[:, t, g, a]), (wh[:, b], wl[:, b]),
                                    t == 0, t == 7, fr, wm, tm[t])
                    W.done(m)
                wh, wl, wm = W.get()
                cs = Ring([sb(s2, [128, 512]) for _ in range(2)])
                yb = Ring([sb(s2, [128, L]) for _ in range(2)])
                ym = []
                for g in range(4):
                    s, p, _ = taken[g]
                    i, b, f = cs.take()
                    a = copy(act, b[:], p[:, 0:512], m, f)
                    k, y, f = yb.take()
                    a1 = tt(dve, y[:, 0:512], b[:], p[:, 512:1024], SUB, a, f)
                    a2 = tt(dve, y[:, 1023:512:-1], b[:, 1:512], p[:, 513:1024], ADD, a, f)
                    a3 = copy(dve, y[:, 512:513], y5[:, 2 * g:2 * g + 1], y5m, f)
                    slots.give(s, a1, a2)
                    cs.give(i, a1, a2)
                    ym.append(split(UH[:, g, :], UL[:, g, :], y[:], a1, a2, a3, m))
                    yb.give(k, *ym[g])
                for g in range(4):
                    s, p, fr = slots.take()
                    for half in range(2):
                        c = slice(half * 512, half * 512 + 512)
                        a = slice(g * 128, g * 128 + 128)
                        m = mm3(p[:, c], (wh[:, a], wl[:, a]), (UH[:, g, c], UL[:, g, c]), True, True,
                                fr, wm, ym[g])
                    k, y, f = yb.take()
                    a = ts(dve, y[:], p, C("fb", g), None, ADD, None, m, f)
                    slots.give(s, a)
                    yb.give(k, store(f"yb{k}", mixd2[g], y[:], a))
                W.done(m)
                fence()
        with ExitStack() as st:
            slots_s = Ring([slot(0), slot(1)])
            cs_ = sb(st, [128, 2, L])
            rp = sb(st, [128, 128])
            rm = [load("cs", cs_[:], A["rope"]), load("rp", rp[:], A["rperm"])]
            big = Ring([sb(st, [128, L]) for _ in range(3)])
            raws = Ring([sb(st, [128, L]) for _ in range(1)])
            KV = [sb(st, [128, L], R) for _ in range(2)]
            VH, VL = (sb(st, [128, 8, 2, 128], R) for _ in range(2))
            Q = Ring([tuple(sb(st, [128, L], R) for _ in range(2)) for _ in range(2)])
            outs = Ring([sb(st, [128, L]) for _ in range(1)])
            one, zero = (b[:, 0:512].rearrange("p (a n) -> p a n", a=8) for b in big.bufs[0:2])
            om = [memset(dve, one, 1.0), memset(dve, zero, 0.0)]
            vi = value_ones(VH, VL, one, zero, om)
            big.free = [list(vi), list(vi), []]
            rope = (cs_[:, 0, :], cs_[:, 1, :], rp[:])

            def fetch(row):
                i, b, f = raws.take()
                return i, b, load(f"gq{i}", b[:], pj[row], f)

            i, b, lm = fetch(0)
            km, g1 = [], []
            done = lambda marks, last: (km.extend(marks), g1.append(last))
            for _ in head_norm(big, b[:], "kn", "eps", 1.0 / 64, [lm] + rm, KV[0], KV[1], None, done, rope):
                pass
            raws.give(i, *g1)
            i, b, lm = fetch(1)
            vm = value_tiles(b, lm, VH, VL, None)
            raws.give(i, *vm)
            chunks = {}

            def prep(c):
                i, b, lm = fetch(2 + c)
                qi, (qh, ql), f = Q.take()
                ready = []

                def done(marks, last):
                    raws.give(i, last)
                    ready.extend(marks)
                yield from head_norm(big, b[:], "qn", "eps64", 1.0, lm, qh, ql, f, done, rope)
                chunks[c] = dict(qi=qi, q=(qh, ql), ready=ready + km + vm + vi)

            units = [dict(c=c, j=j, t=t, nk=1024, k0=0, base=0) for c in range(4) for j in range(2) for t in range(8)]
            state = {}

            def bind(c):
                ch = chunks[c]
                for u in units[16 * c:16 * c + 16]:
                    j = u["j"]
                    u["q"], u["k"], u["v"], u["bias"] = ch["q"], tuple(KV), (VH, VL), None
                    u["ready"] = lambda ch=ch: ch["ready"]
                    u["last_scores"] = (lambda m, ch=ch: Q.give(ch["qi"], m)) if (u["t"] == 7 and j == 1) else None

                    def out(j=j):
                        if j == 0:
                            state["out"] = outs.take()
                        return state["out"][1], state["out"][2]
                    u["out"] = out

                    def finish(z, m, j=j, c=c):
                        if j == 0:
                            state["z0"] = z
                            return
                        oi, ob, _ = state["out"]
                        outs.give(oi, store(f"gqo{oi}", mixd2[4 + c], ob[:], z, state["z0"]))
                    u["finish"] = finish

            background = [prep(0)]

            def drain():
                while background:
                    for _ in background.pop(0):
                        pass
            prep_at = {0: lambda: (drain(), bind(0))}
            for c in range(1, 4):
                prep_at[16 * c - 13] = lambda c=c: background.append(prep(c))
                prep_at[16 * c] = lambda c=c: (drain(), bind(c))
            attention(units, st, prep_at, background, 8)
            fence()
        return xready

    def norm_split_in(x, wname, xready, H, Lo, space):
        class Fake:
            pass
        bufs = [space[:, i, :] for i in range(6)]
        sq = Ring(bufs[0:2])
        rs = bufs[2]
        tmp = Ring(bufs[3:5])
        s, p, free = slots.take()
        for k in range(KC):
            i, b, f = sq.take()
            a = actf(b, x[:, k, :], ACT.Square, xready[k], f)
            for half in range(2):
                c = slice(half * 512, half * 512 + 512)
                m = mm(p[:, c], ONES, b[:, c], k == 0, k == KC - 1, a, free)
            sq.give(i, m)
        a, r = neg2_rsqrt(rs, bufs[5], p, 1.0 / D, "eps", EPS, m)
        slots.give(s, a)
        ready = []
        for k in range(KC):
            i, b, f = tmp.take()
            m = stt(b, x[:, k, :], NH(wname, k), rs, MUL, MUL, r, xready[k], f)
            ready.append(split(H[:, k, :], Lo[:, k, :], b, m))
            tmp.give(i, *ready[k])
        return ready

    phase_inproj()
    phase_na()
    phase_delta()
    with ExitStack() as st:
        W.open(st, A["wts"].shape[0])
        x = sb(st, [128, KC, L])
        xr = [load(f"x{k}", x[:, k, :], A["xT"][k]) for k in range(KC)]
        xr = phase_outproj(x, xr, mixd, st)
        xr = phase_ffn(x, "ffn1", xr)
        xr = phase_mix2(x, xr)
        xr = phase_outproj(x, xr, mixd2, st)
        xr = phase_ffn(x, "ffn2", xr)
        with ExitStack() as s2:
            def sink(k, b, m):
                return [store(f"fo{k % 2}", A["out"][k], b[:], m)]
            rmsnorm(x, "fin", xr, sink, s2)
            fence()
    if "dbg" in A:
        for n, (dst, src) in enumerate(((A["dbg"][0], pj), (A["dbg"][1], mixd), (A["dbg"][2], mixd2))):
            store(f"dbg{n}", dst, src)
    assert W.next == A["wts"].shape[0], (W.next, A["wts"].shape)
    sp.items.append((flat(out_marks), None, Mark(sp)))

    for q in engines + [sp]:
        q.number()
    with top:
        block = top.enter_context(nc.Block())

        @block.sync
        def _(e):
            sp.emit(e)

        @block.scalar
        def _(e):
            act.emit(e)

        @block.vector
        def _(e):
            dve.emit(e)

        @block.gpsimd
        def _(e):
            pool.emit(e)

        @block.tensor
        def _(e):
            pe.emit(e)


def _tiles(w, pad_to=None):
    K, M = w.shape
    return np.ascontiguousarray(w.reshape(K // 128, 128, M // 128, 128).transpose(2, 1, 0, 3)).reshape(M // 128, 128, K)


def _layout(inputs):
    f = np.float32
    I = {k: np.asarray(v) for k, v in inputs.items()}
    cols, ncst = const_columns()
    cst = np.zeros((128, ncst), f)

    def put(name, a):
        at, n = cols[name]
        cst[:, at:at + n] = a
    for name, src in (("norm1", I["norm_w"][0]), ("ffn1", I["ffn1_norm_2"]), ("mixn", I["mix_norm_2"]),
                      ("ffn2", I["ffn2_norm_2"]), ("fin", I["final_norm_2"])):
        put(name, src.reshape(8, 128).T)
    two = lambda a: np.concatenate([a, a])[:, None]
    put("gq", two(I["qk_gain_q"][0]))
    put("gk", two(I["qk_gain_k"][0]))
    put("qn", two(I["q_norm_2"]))
    put("kn", two(I["k_norm_2"]))
    put("conv", I["conv_w"][0].reshape(5, 12, 128).transpose(2, 1, 0).reshape(128, 60))
    cst[32:40, cols["alog"][0]] = I["a_log"][0].reshape(8)
    cst[32:40, cols["dtb"][0]] = I["dt_bias"][0].reshape(8)
    put("dnw", I["dn_norm_w"][0][:, None])
    put("fb", I["fnet_b_2"].T)
    put("eps", EPS)
    put("eps64", 64 * EPS)
    put("eps128", 128 * EPS)
    put("one", 1.0)
    put("ident", np.eye(128, dtype=f))
    put("ones", 1.0)
    blk = np.arange(128) // 64
    put("bones", (blk[:, None] == blk[None, :]).astype(f))

    w_in = I["w_in"][0]
    gates = np.zeros((D, 128), f)
    g16 = w_in[:, 4096:4112]
    gates[:, 0:4], gates[:, 4:8] = g16[:, 0:4], g16[:, 8:12]
    gates[:, 32:36], gates[:, 36:40] = g16[:, 4:8], g16[:, 12:16]
    parts = [_tiles(w_in[:, :4096]), _tiles(gates), _tiles(I["w_out"][0])]

    def ffn(g, u, d):
        pad = lambda a: np.concatenate([a, np.zeros((D, FT * 128 - FF), f)], 1)
        tg, tu = _tiles(pad(g)), _tiles(pad(u))
        dp = np.concatenate([d, np.zeros((FT * 128 - FF, D), f)], 0).reshape(FT, 128, 4, 256)
        out = []
        at = 0

        def gu(n):
            for _ in range(n):
                i = sum(1 for o in out if o[1] == "g")
                out.append((tg[i:i + 1], "g"))
                out.append((tu[i:i + 1], "u"))
        gu(GROUPS[0])
        for g_, nk in enumerate(GROUPS):
            if g_ + 1 < len(GROUPS):
                gu(1)
            for mp in range(4):
                t = np.zeros((1, 128, 1024), f)
                t[0, :, :nk * 256] = dp[at:at + nk, :, mp, :].transpose(1, 0, 2).reshape(128, nk * 256)
                out.append((t, "d"))
            at += nk
            if g_ + 1 < len(GROUPS):
                gu(GROUPS[g_ + 1] - 1)
        return [o[0] for o in out]

    parts += ffn(I["ffn1_w_gate_2"], I["ffn1_w_up_2"], I["ffn1_w_down_2"])
    w2 = I["w_in_2"]
    wf, wq, wk, wv = w2[:, :512], w2[:, 512:1024], w2[:, 1024:1152], w2[:, 1152:1280]
    heads = np.array([[c, c + 4] for c in range(4)]).reshape(-1)
    wq = wq.reshape(D, 8, 64)[:, heads].reshape(D, 512)
    parts += [_tiles(wf), _tiles(wk), _tiles(wv), _tiles(wq)]
    n = np.arange(128)
    ang = 2 * np.pi * ((n[:, None] * n[None, :]) % 128) / 128
    x1 = np.zeros((1, 128, 1024), f)
    x1[0, :, 0:128], x1[0, :, 128:256] = np.cos(ang), np.sin(ang)
    t, s = np.arange(L), np.arange(512)
    ang = 2 * np.pi * ((t[:, None] * s[None, :]) % L) / L
    sc = 1.0 / np.sqrt(L * 128.0)
    tab = np.concatenate([np.cos(ang) * sc, np.sin(ang) * sc], 1).astype(f).reshape(8, 128, 1024)
    x2 = np.zeros((1, 128, 1024), f)
    x2[0, :, 0:512] = I["fnet_w_2"].transpose(1, 0, 2).reshape(128, 512)
    wo2 = I["w_out_2"]
    wo2 = np.concatenate([wo2[:512], wo2[512:].reshape(8, 64, D)[heads].reshape(512, D)], 0)
    parts += [x1, tab, x2, _tiles(wo2)]
    parts += ffn(I["ffn2_w_gate_2"], I["ffn2_w_up_2"], I["ffn2_w_down_2"])
    wts = np.concatenate(parts, 0)

    rpb = I["rpb"][0]
    c, kc = np.arange(64), np.arange(64)
    lo = np.clip(c - 8, 0, 48)
    ok = (kc[None, :] >= lo[:, None]) & (kc[None, :] < lo[:, None] + 16)
    dc = np.clip(kc[None, :] - c[:, None] + 15, 0, 30)
    full = rpb[:, :, dc]
    tabs = np.full((8, 128, 23, 64), NEG, f)
    for half in range(2):
        r = slice(64 * half, 64 * half + 64)
        for i in range(14):
            tabs[:, r, i, :] = np.where(ok[None], full[:, i + 1 - half], f(NEG))
        for i in range(9):
            dr = i + 3 - half
            if 3 <= dr <= 10:
                tabs[:, r, 14 + i, :] = np.where(ok[None], full[:, dr], f(NEG))
    i = np.arange(128)
    same = blk[:, None] == blk[None, :]
    dm = np.zeros((128, 14, 128), f)
    dm[:, 0] = same & (i[:, None] <= i[None, :])
    dm[:, 1] = same & (i[:, None] >= i[None, :])
    for l in range(6):
        b = 1 << l
        low = (i[:, None] // (2 * b) == i[None, :] // (2 * b)) & (i[:, None] % (2 * b) >= b) & (i[None, :] % (2 * b) < b)
        dm[:, 2 + l] = low
        dm[:, 8 + l] = low.T
    inv = (np.float32(10000.0) ** (-np.arange(0, 32, 2, dtype=f) / np.float32(32))).astype(f)
    tok = np.arange(L)
    ar = (tok // 64).astype(f)[None, :] * inv[:, None]
    ac = (tok % 64).astype(f)[None, :] * inv[:, None]
    ang = np.concatenate([ar, ar, ac, ac] * 2, 0)
    rope = np.stack([np.cos(ang), np.sin(ang)], 1).astype(f)
    rp = np.zeros((128, 128), f)
    for p in range(128):
        if p % 32 < 16:
            rp[p + 16, p] = -1.0
        else:
            rp[p - 16, p] = 1.0
    alt = np.zeros((128, 2), f)
    alt[:] = (1.0 - 2.0 * (i % 2))[:, None]
    return dict(xT=np.ascontiguousarray(I["x"][0].T).reshape(8, 128, L), cst=cst, wts=wts,
                rpb=tabs.reshape(8, 128, 23 * 64), dmask=dm, rope=rope, rperm=rp, alt=alt)


DBG = False


def kernel(**inputs):
    import concourse.bacc as _bacc
    from concourse import mybir as _mybir
    from concourse.bass_utils import run_bass_kernel_spmd as _run

    nc = _bacc.Bacc("TRN2", target_bir_lowering=False, num_devices=1)
    arrays, A = {}, {}
    for name, a in _layout(inputs).items():
        a = np.ascontiguousarray(a)
        arrays[f"in_{name}_dram"] = a
        A[name] = nc.dram_tensor(f"in_{name}_dram", a.shape, _mybir.dt.from_np(a.dtype), kind="ExternalInput").ap()
    A["out"] = nc.dram_tensor("out_0_dram", (8, 128, L), _mybir.dt.float32, kind="ExternalOutput").ap()
    if DBG:
        A["dbg"] = [nc.dram_tensor(f"dbg{i}", (n, 128, L), _mybir.dt.float32, kind="ExternalOutput").ap()
                    for i, n in enumerate((33, 8, 8))]
    build(nc, A)
    r = _run(nc, [arrays], core_ids=[0])
    out = np.ascontiguousarray(np.asarray(r.results[0]["out_0_dram"]).reshape(D, L).T).reshape(1, L, D)
    if DBG:
        return tuple([out] + [np.asarray(r.results[0][f"dbg{i}"]) for i in range(3)])
    return out
```

```python
import numpy as np
from contextlib import ExitStack

L = 1024
D = 1024
KC = D // 128
FF = 2752
FT = 22
GROUPS = [4, 4, 4, 4, 3, 3]
EPS = 1e-6
N_INPROJ = 33
NEG = -1.0e30
IN_ORDER = [32]
for _c in range(4):
    IN_ORDER += [16 + _c, 12 + _c, 20 + _c, 8 + _c, 24 + _c, _c, 4 + _c, 28 + _c]


def const_columns():
    cols = {}
    at = 0
    for name, n in [("norm1", 8), ("ffn1", 8), ("mixn", 8), ("ffn2", 8), ("fin", 8), ("gq", 1), ("gk", 1),
                    ("qn", 1), ("kn", 1), ("dnw", 1), ("one", 1), ("conv", 60), ("alog", 1), ("dtb", 1), ("fb", 4),
                    ("eps", 1), ("eps64", 1), ("eps128", 1),
                    ("ident", 128), ("ones", 128), ("bones", 128), ("tri", 256)]:
        cols[name] = (at, n)
        at += n
    return cols, at


class Mark:
    __slots__ = ("q", "need", "sem", "val")

    def __init__(self, q=None, sem=None, val=0):
        self.q, self.need, self.sem, self.val = q, False, sem, val


class Queue:
    def __init__(self, sem):
        self.sem, self.items = sem, []

    def __call__(self, fn, *after):
        m = Mark(self)
        self.items.append((flat(after), fn, m))
        return m

    def last(self):
        for _, fn, m in reversed(self.items):
            if fn is not None and m.q is not None:
                return m
        return None

    def number(self):
        n = 0
        for _, _, m in self.items:
            if m.q is not None and m.need:
                n += 1
                m.sem, m.val = self.sem, n

    def emit(self, eng):
        seen = {}
        for after, fn, m in self.items:
            want = {}
            for a in after:
                k = id(a.sem)
                if a.val > seen.get(k, 0) and a.val > want.get(k, (0, None))[0]:
                    want[k] = (a.val, a.sem)
            for k, (v, s) in want.items():
                eng.wait_ge(s, v)
                seen[k] = v
            if fn is None:
                continue
            ins = fn(eng)
            if m.q is None:
                ins.then_inc(m.sem, 16)
            elif m.need:
                ins.then_inc(self.sem, 1)


def flat(after):
    out = []
    for a in after:
        if a is None:
            continue
        if isinstance(a, (list, tuple)):
            out += flat(a)
        else:
            a.need = True
            out.append(a)
    return out


class DmaSem:

    def __init__(self, sem):
        self.sem, self.n = sem, 0

    def start(self, q, fn, *after):
        self.n += 16
        m = Mark(None, self.sem, self.n)
        q.items.append((flat(after), fn, m))
        return m


class Ring:

    def __init__(self, bufs):
        self.bufs, self.free, self.busy, self.i = bufs, [[] for _ in bufs], [False] * len(bufs), 0

    def take(self):
        i = self.i
        assert not self.busy[i], "taken before it was given back"
        self.i = (i + 1) % len(self.bufs)
        self.busy[i] = True
        return i, self.bufs[i], self.free[i]

    def give(self, i, *marks):
        assert self.busy[i]
        self.busy[i], self.free[i] = False, list(marks)


def build(nc, A):
    import concourse.bass as bass
    from concourse import mybir

    F = mybir.dt.float32
    R = mybir.dt.float32r
    ACT = mybir.ActivationFunctionType
    ALU = mybir.AluOpType
    AX = mybir.AxisListType.X
    MUL, ADD, SUB = ALU.mult, ALU.add, ALU.subtract

    cols, ncst = const_columns()
    top = ExitStack()
    sem = lambda n: top.enter_context(nc.semaphore(n))
    pe, act, dve, pool, sp = (Queue(sem("s_" + n)) for n in ("pe", "act", "dve", "pool", "sp"))
    engines = [pe, act, dve, pool]
    dsems = {}

    def dsem(name):
        if name not in dsems:
            dsems[name] = DmaSem(sem("d_" + name))
        return dsems[name]

    out_marks = []
    phase_dmas = []

    def load(name, dst, src, *after):
        m = dsem(name).start(sp, lambda e: e.dma_start(dst, src), *after)
        phase_dmas.append(m)
        return m

    def store(name, dst, src, *after):
        m = load(name, dst, src, *after)
        out_marks.append(m)
        return m

    def fence(writers_only=False):
        marks = [q.last() for q in engines] + list(phase_dmas)
        phase_dmas.clear()
        for q in ([act, dve, pool] if writers_only else engines) + [sp]:
            q.items.append((flat(marks), None, Mark(q)))

    names = [0]

    def sb(stack, shape, dt=F):
        names[0] += 1
        return stack.enter_context(nc.sbuf_tensor(f"t{names[0]}", shape, dt))

    scr = lambda n, shape: nc.dram_tensor(n, shape, F, kind="Internal").ap()
    pj = scr("pj", (N_INPROJ, 128, L))
    kt_d = scr("kt_d", (4, 128, L))
    mixd2 = scr("mixd2", (4, 128, L))

    ps = top.enter_context(nc.psum_tensor("ps", [128, 8, 512], F))
    slot = lambda s: ps[:, 2 * s:2 * s + 2, :].rearrange("p a n -> p (a n)")
    slots = Ring([slot(s) for s in range(4)])

    cst = sb(top, [128, ncst])
    cm = load("cst", cst[:], A["cst"])
    C = lambda n, i=0, w=1: cst[:, cols[n][0] + i:cols[n][0] + i + w]
    nh = sb(top, [128, 46])
    NH = lambda n, i=0: nh[:, cols[n][0] + i:cols[n][0] + i + 1]
    IDENT = C("ident", 0, 128)
    ONES = C("ones", 0, 128)
    BONES = C("bones", 0, 128)
    for q in engines:
        q.items.append((flat([cm]), None, Mark(q)))
    hm = dve(lambda e: e.tensor_scalar(nh[:], cst[:, 0:46], -0.5, None, MUL))
    for q in (act, dve):
        q.items.append((flat([hm]), None, Mark(q)))

    def mm(out, lhsT, rhs, start, stop, *after):
        return pe(lambda e: e.matmul(out, lhsT, rhs, start=start, stop=stop), *after)

    def tr(out, in_, *after, n=128, ident=None):
        idn = IDENT[0:n, 0:n] if ident is None else ident
        return pe(lambda e: e.transpose(out, in_, idn), *after)

    def mm3(out, A_, B_, start, stop, *after):
        (ah, al), (bh, bl) = A_, B_
        mm(out, ah, bh, start, False, *after)
        mm(out, ah, bl, False, False)
        return mm(out, al, bh, False, stop)

    table = [None]

    def actf(out, in_, fn, *after, scale=1.0, bias=None, accum=None):
        if fn in (ACT.Exp, ACT.Ln) and table[0] != "lnexp":
            table[0] = "lnexp"
            act(lambda e: e.preload_act_table_set("natural_log_exp_and_others"))
        elif fn == ACT.Silu:
            table[0] = "silu"
        kw = {}
        if bias is not None:
            kw["bias"] = bias
        if accum is not None:
            kw["accum_out"] = accum
        return act(lambda e: e.activation(out, in_, fn, scale=scale, **kw), *after)

    def tt(q, out, a, b, op, *after):
        return q(lambda e: e.tensor_tensor(out, a, b, op), *after)

    def ts(q, out, a, s1, s2, op0, op1, *after):
        if op1 is None:
            return q(lambda e: e.tensor_scalar(out, a, s1, None, op0), *after)
        return q(lambda e: e.tensor_scalar(out, a, s1, s2, op0, op1), *after)

    def stt(out, a, s, b, op0, op1, *after):
        return dve(lambda e: e.scalar_tensor_tensor(out, a, s, b, op0, op1), *after)

    def recip(out, a, *after):
        return dve(lambda e: e.reciprocal(out, a), *after)

    def copy(q, out, a, *after):
        if q is act:
            return actf(out, a, ACT.Copy, *after)
        return q(lambda e: e.tensor_copy(out, a), *after)

    def memset(q, out, v, *after):
        return q(lambda e: e.memset(out, v), *after)

    def split(hi, lo, src, *after, q=pool):
        a = actf(hi, src, ACT.Copy, *after)
        b = tt(q, lo, src, hi.bitcast(F), SUB, a, *after)
        return [a, b]

    def split_psum(parts, *after):
        for hi, lo, src in parts:
            a = actf(hi, src, ACT.Copy, *after)
        for hi, lo, src in parts:
            b = tt(dve, lo, src, hi.bitcast(F), SUB, a, *after)
        return [a, b]

    def neg2_rsqrt(out, aux, p, scale, epsname, eps, *after):
        a = actf(aux, p, ACT.Ln, *after, scale=scale, bias=C(epsname))
        a = actf(out, aux, ACT.Exp, a, scale=-0.5)
        a = actf(aux, out, ACT.Square, a, scale=float(np.sqrt(scale)))
        d = stt(aux, p, eps / scale, aux, ADD, MUL, a)
        return d, stt(out, aux, -3.0, out, ADD, MUL, d)

    class Weights:
        NR, NS, AHEAD = 4, 3, 2

        def __init__(self):
            self.next = self.raws = self.splits = 0

        def open(self, stack, limit):
            self.limit = limit
            self.raw = Ring([sb(stack, [128, 1024]) for _ in range(self.NR)])
            self.sp = Ring([(sb(stack, [128, 1024], R), sb(stack, [128, 1024], R)) for _ in range(self.NS)])
            self.rawq, self.spq = [], []
            self.pump()

        def pump(self):
            while self.raws < min(self.next + self.NR, self.limit) and self.raws < self.splits + self.NR:
                n = self.raws
                i, buf, free = self.raw.take()
                m = dsem(f"w{i}").start(sp, lambda e, b=buf, n=n: e.dma_start(b[:], A["wts"][n]), *free)
                self.rawq.append((i, buf, m))
                self.raws += 1

        def split_one(self):
            i, buf, m = self.rawq.pop(0)
            k, (hi, lo), free = self.sp.take()
            marks = split(hi[:], lo[:], buf[:], m, free)
            self.raw.give(i, *marks)
            self.spq.append((k, hi, lo, marks))
            self.splits += 1
            self.pump()

        def get(self):
            while self.splits <= min(self.next + self.AHEAD, self.limit - 1):
                self.split_one()
            k, hi, lo, marks = self.spq.pop(0)
            self.next += 1
            self.k = k
            return hi, lo, marks

        def done(self, m):
            self.sp.give(self.k, m)

    W = Weights()

    def linear_tile(H, Lo, hready, slots=slots, tick=lambda: None, order=tuple(range(KC))):
        wh, wl, wm = W.get()
        s, p, free = slots.take()
        for half in range(2):
            o = p[:, half * 512:half * 512 + 512]
            b = slice(half * 512, half * 512 + 512)
            for n, k in enumerate(order):
                a = slice(k * 128, k * 128 + 128)
                last = mm3(o, (wh[:, a], wl[:, a]), (H[:, k, b], Lo[:, k, b]), n == 0, n == KC - 1,
                           wm, free, hready[k])
            tick()
        W.done(last)
        return s, p, last

    X = sb(top, [128, KC, L])
    gates = ExitStack()
    beta, G, eg, ed, bg = (sb(gates, [128, 8, 8]) for _ in range(5))
    gt = sb(gates, [128, 8, 64])
    TRI = [C("tri", 0, 128), C("tri", 128, 128)]
    gate_ready = []

    pre = ExitStack()
    na_raw = tuple(sb(pre, [128, L]) for _ in range(4))
    na_tab = sb(pre, [128, 23 * 64])
    stored = {}
    early = []

    def phase_inproj():
        with ExitStack() as st:
            W.open(st, N_INPROJ)
            H, Lo = sb(st, [128, KC, L], R), sb(st, [128, KC, L], R)
            x = X
            ev = Ring([sb(st, [128, L + 4]) for _ in range(4)])
            t1, t2, t3 = (sb(st, [128, L]) for _ in range(3))
            rs = sb(st, [128, L])
            xm = [load(f"x{k}", x[:, k, :], A["xT"][k]) for k in range(KC)]
            for _ in range(W.AHEAD + 1):
                W.split_one()
            ready, sqf, accm = [], [], []
            for k in range(KC):
                w = NH("norm1", k)
                a = actf(H[:, k, :], x[:, k, :], ACT.Copy, xm[k], scale=w)
                ready.append([a, stt(Lo[:, k, :], x[:, k, :], w, H[:, k, :].bitcast(F), MUL, SUB, a)])
                if k == 0:
                    accm = actf(t2[:], x[:, k, :], ACT.Square, xm[k])
                else:
                    a = actf(t1[:], x[:, k, :], ACT.Square, xm[k], sqf)
                    accm = tt(dve if k % 2 else pool, t2[:], t2[:], t1[:], ADD, a, accm)
                    sqf = [accm]
            edge = [memset(dve, b[:, c:c + 2], 0.0) for b in ev.bufs for c in (0, L + 2)]
            dense, aside = Ring([slot(0), slot(1), slot(2)]), Ring([slot(3)])
            tf = [[]]
            rm = []

            def factor():
                s, p, fr = aside.take()
                for half in range(2):
                    c = slice(half * 512, half * 512 + 512)
                    m = mm(p[:, c], ONES, t2[:, c], True, True, accm, fr)
                a, r = neg2_rsqrt(rs[:], t3[:], p, 1.0 / D, "eps", EPS, m)
                aside.give(s, a)
                tf[0] = [r, m]
                rm.append(r)

            def keep(i, row, buf, *marks):
                stored[row] = store(f"ev{i}", pj[row], buf, *marks)
                return stored[row]

            def square_sum(buf, ones, mark):
                a = actf(t1[:], buf, ACT.Square, mark, tf[0])
                yield
                s, p, fr = aside.take()
                for half in range(2):
                    c = slice(half * 512, half * 512 + 512)
                    m = mm(p[:, c], ones, t1[:, c], True, True, a, fr)
                d = copy(dve, t3[:], p, m, tf[0])
                aside.give(s, d)
                yield
                return d

            def rsqrt_steps(d, scale, epsname, eps):
                a = actf(t2[:], t3[:], ACT.Ln, d, tf[0], scale=scale, bias=C(epsname))
                yield
                a = actf(t1[:], t2[:], ACT.Exp, a, scale=-0.5)
                yield
                a = actf(t2[:], t1[:], ACT.Square, a, scale=float(np.sqrt(scale)))
                yield
                d = stt(t2[:], t3[:], eps / scale, t2[:], ADD, MUL, a)
                yield
                d = stt(t1[:], t2[:], -3.0, t1[:], ADD, MUL, d)
                yield
                return d

            def post_qk(i, b, c, row, gain, scale, epsname, eps):
                d = yield from square_sum(b[:, 2:L + 2], BONES, c)
                d = yield from rsqrt_steps(d, scale, epsname, eps)
                m = stt(b[:, 2:L + 2], b[:, 2:L + 2], NH(gain), t1[:], MUL, MUL, d)
                tf[0] = [m]
                ev.give(i, keep(i, row, b[:, 2:L + 2], m))
                yield

            def to_tokens(src, mark):
                s, p, fr = aside.take()
                for t in range(8):
                    m = tr(p[:, t * 128:t * 128 + 128], src[:, t * 128:t * 128 + 128], mark, fr)
                c = copy(act, t3[:], p, m, tf[0])
                aside.give(s, c)
                return m, c

            def post_v(i, b, c, row):
                m, a = to_tokens(b[:, 2:L + 2], c)
                stored[row] = store("tok", pj[row], t3[:], a)
                tf[0] = [stored[row]]
                ev.give(i, m)
                yield

            def post_conv(i, b, c, row):
                wi = row - 16
                m = ts(dve, t1[:], b[:, 0:L], C("conv", wi * 5), None, MUL, None, c, tf[0])
                yield
                for tap in range(1, 5):
                    m = stt(t1[:], b[:, tap:tap + L], C("conv", wi * 5 + tap), t1[:], MUL, ADD, m)
                    yield
                y = b[:, 2:L + 2]
                m = actf(y, t1[:], ACT.Silu, m)
                tf[0] = tf[0] + [m]
                yield
                if row < 24:
                    d = yield from square_sum(y, ONES, m)
                    scale, epsname = (128.0, "eps128") if row < 20 else (1.0, "eps")
                    d = yield from rsqrt_steps(d, scale, epsname, scale * EPS)
                    m = stt(y, y, -0.5, t1[:], MUL, MUL, d)
                    tf[0] = [m]
                    yield
                marks = []
                if row < 24:
                    marks.append(keep(i, row, y, m))
                if row >= 20:
                    mt, a = to_tokens(y, m)
                    tf[0] = [store("tok", pj[row] if row >= 24 else kt_d[row - 20], t3[:], a)]
                    marks.append(mt)
                ev.give(i, *marks)
                yield

            def post_gates(i, b, c):
                gr, w1, w2, w3 = b[0:64, 2:L + 2], t1[0:64, :], t2[0:64, :], t3[0:64, :]
                b_, a_ = slice(0, 32), slice(32, 64)
                f = tf[0]
                y0 = ts(dve, w1[a_, :], gr[a_, :], C("dtb")[a_, :], None, ADD, None, c, f)
                yield
                x1 = actf(w1[b_, :], gr[b_, :], ACT.Exp, c, f, scale=-1.0)
                y1 = actf(w2[a_, :], w1[a_, :], ACT.Abs, y0, f)
                yield
                y1 = actf(w2[a_, :], w2[a_, :], ACT.Exp, y1, scale=-1.0)
                x1 = ts(dve, w1[b_, :], w1[b_, :], 1.0, None, ADD, None, x1)
                yield
                y1 = actf(w2[a_, :], w2[a_, :], ACT.Ln, y1, bias=C("one")[a_, :])
                x1 = recip(gr[b_, :], w1[b_, :], x1)
                yield
                y2 = ts(dve, w3[a_, :], w1[a_, :], 0.0, None, ALU.max, None, y0, f)
                y3 = tt(dve, w3[a_, :], w3[a_, :], w2[a_, :], ADD, y1, y2)
                n1 = actf(nA[a_, :], C("alog")[a_, :], ACT.Exp)
                yield
                y4 = ts(dve, gr[a_, :], w3[a_, :], nA[a_, :], -1.0, MUL, MUL, y3, n1, y0)
                tf[0] = [x1, y4]
                yield
                s, p, fr = aside.take()
                for t in range(8):
                    m = tr(p[:, t * 64:t * 64 + 64], gr[:, t * 128:t * 128 + 128], x1, y4, fr, n=64)
                c1 = copy(dve, gt[:], p[:, 0:512].rearrange("p (t f) -> p t f", t=8), m)
                aside.give(s, c1)
                ev.give(i, m)
                c2 = copy(dve, beta[:], gt[:, :, 0:8], c1)
                yield
                s, p, fr = aside.take()
                pg = p.rearrange("p (a n) -> p a n", a=2)
                for d in range(2):
                    m = mm(pg[:, 0, 32 * d:32 * d + 32], TRI[d], gt[:, :, 32 + 4 * d:36 + 4 * d], True, True,
                           c1, fr)
                m2 = mm(pg[:, 1, 0:64], BONES, gt[:, :, 32:40], True, True, c1, fr)
                gs = []
                for d in range(2):
                    gs.append(copy(dve, G[:, :, 4 * d:4 * d + 4],
                                   pg[:, 0, 32 * d:32 * d + 32].rearrange("p (t h) -> p t h", t=8), m2))
                c3 = tt(dve, ed[:], pg[:, 1, 0:64].rearrange("p (t h) -> p t h", t=8), G[:], SUB, gs)
                aside.give(s, c3)
                yield
                e1 = actf(ed[:], ed[:], ACT.Exp, c3)
                e2 = actf(eg[:], G[:], ACT.Exp, gs)
                e3 = tt(dve, bg[:], eg[:], beta[:], MUL, e2, c2)
                gate_ready.extend([c1, c2, e1, e2, e3] + gs)
                yield

            nA = sb(st, [64, 1])
            work = []

            def tick():
                if not rm:
                    factor()
                for _ in range(6):
                    if work and next(work[0], "end") == "end":
                        work.pop(0)

            for row in IN_ORDER:
                s, p, done = linear_tile(H, Lo, ready, dense, tick)
                while ev.busy[ev.i]:
                    if next(work[0], "end") == "end":
                        work.pop(0)
                i, b, f = ev.take()
                y = b[:, 2:L + 2]
                c = tt(dve, y, p, rs[:], MUL, done, f, edge, rm)
                dense.give(s, c)
                if row in range(12, 16) or row >= 28 and row < 32:
                    c = actf(y, y, ACT.Silu, c)
                if row < 8:
                    q = row < 4
                    work.append(post_qk(i, b, c, row, "gq" if q else "gk", 1.0 if q else 1.0 / 64,
                                        "eps64" if q else "eps", 64 * EPS if q else EPS))
                elif row < 12:
                    work.append(post_v(i, b, c, row))
                elif 16 <= row < 28:
                    work.append(post_conv(i, b, c, row))
                elif row == 32:
                    work.append(post_gates(i, b, c))
                else:
                    ev.give(i, keep(i, row, y, c))
                if row == IN_ORDER[20]:
                    early.extend(load(f"na0{n}", na_raw[n][:], pj[4 * n], stored[4 * n]) for n in range(4))
                    early.append(load("tab0", na_tab[:], A["rpb"][0]))
            for g in work:
                for _ in g:
                    pass
            fence()

    def head_norm(big, raw, gain, epsname, scale, mraw, hi, lo, free, done, rope=None):
        (i1, sqb, f1), (i2, var, f2), (i3, qn, f3) = big.take(), big.take(), big.take()
        a = actf(sqb[:], raw, ACT.Square, mraw, f1)
        yield
        s, p, fr = slots_s.take()
        for half in range(2):
            c = slice(half * 512, half * 512 + 512)
            m = mm(p[:, c], BONES, sqb[:, c], True, True, a, fr)
        d = copy(dve, var[:], p, m, f2)
        slots_s.give(s, d)
        yield
        a = actf(qn[:], var[:], ACT.Ln, d, f3, scale=scale, bias=C(epsname))
        yield
        a = actf(sqb[:], qn[:], ACT.Exp, a, m, scale=-0.5)
        yield
        a = actf(qn[:], sqb[:], ACT.Square, a, scale=float(np.sqrt(scale)))
        yield
        d = stt(qn[:], var[:], {"eps": EPS, "eps64": 64 * EPS}[epsname] / scale, qn[:], ADD, MUL, a)
        yield
        d = stt(sqb[:], qn[:], -3.0, sqb[:], ADD, MUL, d)
        yield
        m = stt(qn[:], raw, NH(gain), sqb[:], MUL, MUL, d)
        last = m
        yield
        if rope is not None:
            cos, sin, rp = rope
            s, p, fr = slots_s.take()
            for half in range(2):
                c = slice(half * 512, half * 512 + 512)
                m2 = mm(p[:, c], rp, qn[:, c], True, True, m, fr)
            a1 = tt(dve, sqb[:], p, sin, MUL, m2)
            slots_s.give(s, a1)
            a2 = tt(pool, var[:], qn[:], cos, MUL, m)
            yield
            m = tt(dve, qn[:], var[:], sqb[:], ADD, a1, a2, m2)
            yield
        marks = split(hi[:], lo[:], qn[:], m, free)
        big.give(i1, m)
        big.give(i2, m)
        big.give(i3, *marks)
        done(marks, last)
        yield

    slots_s = None

    def value_tiles(vraw, vm, VH, VL, free):
        s, p, fr = slots_s.take()
        for t in range(8):
            m = tr(p[:, t * 128:t * 128 + 128], vraw[:, t * 128:t * 128 + 128], vm, fr)
        pv = p.rearrange("p (t f) -> p t f", t=8)
        cs = [slice(64 * j, 64 * j + 64) for j in range(2)]
        marks = split_psum([(VH[:, :, j, cs[j]], VL[:, :, j, cs[j]], pv[:, :, cs[j]]) for j in range(2)], m, free)
        slots_s.give(s, *marks)
        return marks

    def value_ones(VH, VL, one, zero, ready):
        marks = []
        for j in range(2):
            c = slice(64 * (1 - j), 64 * (1 - j) + 64)
            marks.append(copy(act, VH[:, :, j, c], one, ready))
            marks.append(copy(act, VL[:, :, j, c], zero, ready))
        return marks

    def attention(units, st, prep_at, background, pair_keys):
        P = Ring([sb(st, [128, L]) for _ in range(2)])
        PT = Ring([(sb(st, [128, pair_keys, 256], R), sb(st, [128, pair_keys, 256], R)) for _ in range(2)])
        nmx = Ring([sb(st, [128, 2]) for _ in range(4)])
        rec, rec2 = sb(st, [128, L]), sb(st, [128, L])
        tslot, oslot = Ring([ps[:, 4, :], ps[:, 5, :]]), Ring([ps[:, 6, :], ps[:, 7, :]])
        state = {}
        ending = []

        def end_steps():
            if ending and next(ending[0], "end") == "end":
                ending.pop(0)

        def finish(u, s, o, m):
            j, hf = u["j"], u["t"] // 4
            a, b = slice(64 * j, 64 * j + 64), slice(64 - 64 * j, 128 - 64 * j)
            c = slice(512 * hf, 512 * hf + 512)
            r = actf(rec[a, c], o[b, :], ACT.Ln, m, state.get(("rec", j, hf)))
            yield
            r = actf(rec[a, c], rec[a, c], ACT.Exp, r, scale=-1.0)
            yield
            r = tt(dve, rec2[a, c], o[b, :], rec[a, c], MUL, r)
            yield
            r = stt(rec[a, c], rec2[a, c], -2.0, rec[a, c], ADD, MUL, r)
            out, f = u["out"](hf)
            yield
            z = stt(out[a, c], o[a, :], -1.0, rec[a, c], MUL, MUL, r, f)
            state["rec", j, hf] = z
            oslot.give(s, z)
            if hf == 0:
                state["z"] = z
            else:
                u["finish"]([state["z"], z], m)

        def scores(u):
            s, p, fr = slots_s.take()
            j, t, nk, k0 = u["j"], u["t"], u["nk"], u["k0"]
            r = slice(64 * j, 64 * j + 64)
            qh, ql = u["q"]
            kh, kl = u["k"]
            for c in range(0, nk, 512):
                w = min(512, nk - c)
                m = mm3(p[:, c:c + w], (qh[r, t * 128:t * 128 + 128], ql[r, t * 128:t * 128 + 128]),
                        (kh[r, k0 + c:k0 + c + w], kl[r, k0 + c:k0 + c + w]), True, True, fr, u["ready"]())
            i, pb, f = P.take()
            n, mx, fn_ = nmx.take()
            u["S"] = (s, p, i, pb)
            if u["bias"] is not None:
                b, bm = u["bias"]
                a = dve(lambda e: e.tensor_tensor_reduce(pb[:, 0:nk], p[:, 0:nk], b, 1.0, NEG, ADD, ALU.max,
                                                         mx[:, 1:2]), m, f, fn_, bm)
                a2 = ts(dve, mx[:, 0:1], mx[:, 1:2], -1.0, None, MUL, None, a)
                slots_s.give(s, a)
                u["bias_done"](a)
            else:
                a2 = dve(lambda e: e.tensor_reduce(mx[:, 0:1], p[:, 0:nk], AX, ALU.max, negate=True), m, fn_)
            u["max"] = (n, mx, a2, f)
            if u["last_scores"]:
                u["last_scores"](m)

        def exps(u):
            s, p, i, pb = u["S"]
            n, mx, a2, f = u["max"]
            nk = u["nk"]
            if u["bias"] is not None:
                e_ = actf(pb[:, 0:nk], pb[:, 0:nk], ACT.Exp, a2, bias=mx[:, 0:1])
            else:
                e_ = actf(pb[:, 0:nk], p[:, 0:nk], ACT.Exp, a2, f, bias=mx[:, 0:1])
                slots_s.give(s, e_)
            nmx.give(n, e_)
            u["P"] = (i, pb, e_)

        def transposes(u):
            i, pb, e_ = u["P"]
            nk = u["nk"]
            if u["t"] % 2 == 0:
                state["PT"] = PT.take()
                state["marks"] = []
            k, (ph, pl), f = state["PT"]
            o = 128 * (u["t"] % 2)
            at = (u["k0"] - u["base"]) // 128
            banks = []
            for c0 in range(0, nk, 512):
                s, p, fr = tslot.take()
                for c in range(c0, min(nk, c0 + 512), 128):
                    w = min(128, nk - c)
                    m = tr(p[0:w, c - c0:c - c0 + 128], pb[:, c:c + w], e_, fr)
                n = (min(nk, c0 + 512) - c0) // 128
                kk = at + c0 // 128
                if n:
                    w, src = 128, p[:, 0:n * 128].rearrange("p (k n) -> p k n", k=n)
                    hi, lo = ph[:, kk:kk + n, o:o + 128], pl[:, kk:kk + n, o:o + 128]
                else:
                    src, hi, lo = p[0:64, 0:128], ph[0:64, kk, o:o + 128], pl[0:64, kk, o:o + 128]
                banks.append((s, m, hi, lo, src))
            P.give(i, m)
            his = [actf(hi, src, ACT.Copy, m, f) for s, m, hi, lo, src in banks]
            for (s, m, hi, lo, src), a in zip(banks, his):
                b = tt(dve, lo, src, hi.bitcast(F), SUB, a)
                tslot.give(s, a, b)
                state["marks"] += [a, b]
            u["PT"] = (k, ph, pl, state["marks"])

        def values(u):
            k, ph, pl, marks = u["PT"]
            j, t, nk, base = u["j"], u["t"], u["nk"], u["base"]
            if t % 4 == 1:
                while oslot.busy[oslot.i]:
                    end_steps()
                state["o"] = oslot.take()
            s, o, fr = state["o"]
            VH, VL = u["v"]
            if nk % 128 == 0:
                steps = [(i, 128, 0, 256) for i in range(nk // 128)]
            else:
                steps = [(1, 128, 0, 256), (2, 128, 0, 256), (3, 128, 0, 256), (0, 128, 0, 128), (4, 64, 0, 128),
                         (4, 128, 128, 256), (5, 64, 128, 256)]
            q0 = (t % 4 - 1) * 128
            for n_, (i, w, a, b) in enumerate(steps):
                kt = base // 128 + i
                m = mm3(o[:, q0 + a:q0 + b], (VH[0:w, kt, j, :], VL[0:w, kt, j, :]),
                        (ph[0:w, i, a:b], pl[0:w, i, a:b]), n_ == 0, n_ == len(steps) - 1, marks, fr, u["ready"]())
            PT.give(k, m)
            if t % 4 == 3:
                ending.append(finish(u, s, o, m))

        n = len(units)
        for i in range(n + 2):
            if i in prep_at:
                prep_at[i]()
            if i < n:
                scores(units[i])
            end_steps()
            if 1 <= i <= n:
                transposes(units[i - 1])
            if i < n:
                exps(units[i])
            if i >= 2 and i % 2 == 1:
                values(units[i - 2])
            end_steps()
            for _ in range(2):
                if background:
                    if next(background[0], "end") == "end":
                        background.pop(0)
        while ending:
            end_steps()

    def phase_na():
        nonlocal slots_s
        slots_s = Ring([slot(0), slot(1)])
        with ExitStack() as st:
            raws = Ring([na_raw, tuple(sb(st, [128, L]) for _ in range(4))])
            QK = Ring([tuple(sb(st, [128, L], R) for _ in range(4)) for _ in range(2)])
            V = Ring([tuple(sb(st, [128, 8, 2, 128], R) for _ in range(2)) for _ in range(2)])
            tab = Ring([na_tab, sb(st, [128, 23 * 64])])
            one, zero = sb(st, [128, 8, 64]), sb(st, [128, 8, 64])
            om = [memset(dve, one[:], 1.0), memset(dve, zero[:], 0.0)]
            vinit = [value_ones(VH, VL, one[:], zero[:], om) for VH, VL in V.bufs]
            loads, chunks, tabs = {}, {}, {}

            def fetch(c):
                i, bufs, f = raws.take()
                ms = [load(f"na{i}{n}", bufs[n][:], pj[4 * n + c], f) for n in range(4)]
                loads[c] = (i, bufs, ms)

            def fetch_tab(h):
                i, b, f = tab.take()
                tabs[h] = (i, b, load(f"tab{i}", b[:], A["rpb"][h], f))

            def prep(c):
                i, (q, k, v, z), ms = loads[c]
                qi, (qh, ql, kh, kl), f = QK.take()
                vi, (VH, VL), fv = V.take()
                m1 = split(qh[:], ql[:], q[:], ms[0], f)
                yield
                m1 += split(kh[:], kl[:], k[:], ms[1], f)
                yield
                v4 = v[:].rearrange("p (t j n) -> p t j n", t=8, j=2)
                two = lambda V_: V_[:].rearrange("p t j (h n) -> p t (j h) n", h=2)[:, :, 0:4:3, :]
                m1 += split(two(VH), two(VL), v4, ms[2], fv)
                chunks[c] = dict(i=i, z=z, zm=ms[3], qi=qi, vi=vi, q=(qh, ql), k=(kh, kl), v=(VH, VL),
                                 ready=m1 + vinit[vi])
                yield

            units = []
            state = {}
            for c in range(4):
                for j in range(2):
                    h = 2 * c + j
                    for t in range(8):
                        if t < 2:
                            nk, k0, b0 = 512, 0, (7 - 2 * t - 1) * 64
                        elif t >= 6:
                            nk, k0, b0 = 512, 512, (8 - 2 * t + 7 - 1) * 64
                        else:
                            nk, k0, b0 = 576, (2 * t - 4) * 64, 14 * 64
                        u = dict(c=c, j=j, h=h, t=t, nk=nk, k0=k0, base=[0, 0, 256, 512][t // 2])
                        units.append(u)

                        class Late:
                            pass
                        u["b0"] = b0

            def bind(c, j):
                ch = chunks[c]
                i, b, bm = tabs[2 * c + j]
                for u in units[(2 * c + j) * 8:(2 * c + j) * 8 + 8]:
                    u["q"], u["k"], u["v"] = ch["q"], ch["k"], ch["v"]
                    u["ready"] = lambda ch=ch: ch["ready"]
                    u["bias"] = (b[:, u["b0"]:u["b0"] + u["nk"]], bm)
                    u["bias_done"] = (lambda a, i=i: tab.give(i, a)) if u["t"] == 7 else (lambda a: None)
                    u["last_scores"] = (lambda m, ch=ch: QK.give(ch["qi"], m)) if (u["t"] == 7 and j == 1) else None

                    u["out"] = lambda hf, c=c: (X[:, c, :], [])

                    def finish(z, m, ch=ch, j=j, c=c):
                        if j == 0:
                            state["z0"] = z
                            return
                        g = tt(pool, X[:, c, :], X[:, c, :], ch["z"][:], MUL, z, state["z0"], ch["zm"])
                        V.give(ch["vi"], m)
                        raws.give(ch["i"], g)
                    u["finish"] = finish

            i, bufs, _ = raws.take()
            loads[0] = (i, bufs, early[0:4])
            i, b, _ = tab.take()
            tabs[0] = (i, b, early[4])
            fetch(1)
            prep_at = {}

            def at(i, *fns):
                old = prep_at.get(i)

                def run():
                    if old:
                        old()
                    for f in fns:
                        f()
                prep_at[i] = run
            background = []

            def drain():
                while background:
                    for _ in background.pop(0):
                        pass
            at(0, lambda: background.append(prep(0)), drain)
            for c in range(4):
                for j in range(2):
                    h = 2 * c + j
                    if j == 0:
                        at(8 * h, drain)
                    at(8 * h, lambda c=c, j=j: bind(c, j))
                    if h < 7:
                        at(8 * h + 1, lambda h=h: fetch_tab(h + 1))
            for c in range(1, 4):
                at(16 * (c - 1) + 7, lambda c=c: background.append(prep(c)))
                if c + 1 < 4:
                    at(16 * c + 6, lambda c=c: fetch(c + 1))
            attention(units, st, prep_at, background, 6)
            fence()

    def phase_delta():
        with ExitStack() as st:
            dm = sb(st, [128, 12, 128])
            dmm = load("dm", dm[:], A["dmask"])
            LEV = [[dm[:, d * 6 + l, :] for l in range(6)] for d in range(2)]
            for q in (dve, pool):
                q.items.append((flat([dmm]), None, Mark(q)))

            bc8 = lambda a: a.unsqueeze(1).to_broadcast([128, 8, 128])
            bcl = lambda a: a.unsqueeze(2).to_broadcast([128, 8, 128])
            v8 = lambda a: a.rearrange("p (t f) -> p t f", t=8)

            heads = [dict(q=sb(st, [128, L]), k=sb(st, [128, L]), kt=sb(st, [128, L]), vt=sb(st, [128, L]))
                     for _ in range(2)]
            hds = [dict(D=sb(st, [128, L]), MT=sb(st, [128, L]), X=sb(st, [128, L]), Y=sb(st, [128, L]),
                        vb=sb(st, [128, L]), kb=sb(st, [128, L]), qg=sb(st, [128, L]), egl=sb(st, [128, 16]))
                   for _ in range(4)]
            for d in range(2):
                hds[d]["S"] = hds[2 + d]["S"] = sb(st, [128, 128])
                hds[d]["vn"] = hds[2 + d]["vn"] = sb(st, [128, 128])
            scanned = []
            EB = Ring([sb(st, [128, L]) for _ in range(2)])
            P1 = Ring([sb(st, [128, L]) for _ in range(2)])
            mslots = Ring([slot(i) for i in range(3)])
            slots = Ring([slot(i) for i in range(4)])

            def prep_head(h, hb, last):
                for n, (name, src) in enumerate((("q", pj[16 + h]), ("k", pj[20 + h]), ("kt", kt_d[h]),
                                                 ("vt", pj[24 + h]))):
                    hb[name + "m"] = load(f"h{h % 2}{name}", hb[name][:], src, last)
                yield

            def gate_rows(g, src, col, rhs):
                s, p, fr = slots.take()
                for t in range(8):
                    m = mm(p[:, t * 128:t * 128 + 128], src[:, t, col:col + 1].to_broadcast([128, 128]), rhs,
                           True, True, fr, gate_ready)
                return s, p, m

            def prep_dir(h, d, hb, g, last, q=pool):
                hd = h + 4 * d
                s, p, m = gate_rows(g, gt, 32 + hd, TRI[d])
                ei, E, ef = EB.take()
                x = actf(E[:], p, ACT.Exp, m, ef)
                for t in range(8):
                    c = slice(t * 128, t * 128 + 128)
                    y = ts(dve, g["D"][:, c], p[:, c], G[:, t, hd:hd + 1], 0.0, SUB, ALU.min, m, x, last)
                slots.give(s, x, y)
                yield
                y = actf(g["D"][:], g["D"][:], ACT.Exp, y)
                y = tt(q, v8(g["D"][:]), v8(g["D"][:]), bc8(TRI[d]), MUL, y)
                g["eglm"] = copy(dve, g["egl"][:], E[:, (63 if d == 0 else 0)::64], x, last)
                g["qgm"] = tt(pool, g["qg"][:], hb["q"][:], E[:], MUL, x, hb["qm"], last)
                EB.give(ei, g["eglm"], g["qgm"])
                yield
                s, p, m = gate_rows(g, gt, hd, IDENT)
                ei, kbT, ef = EB.take()
                b = tt(dve, kbT[:], hb["k"][:], p, MUL, m, hb["km"], ef)
                slots.give(s, b)
                yield
                s, p, fr = slots.take()
                for t in range(8):
                    c = slice(t * 128, t * 128 + 128)
                    m = mm(p[:, c], hb["k"][:, c], kbT[:, c], True, True, b, fr)
                EB.give(ei, m)
                mt = tt(dve, g["MT"][:], p, g["D"][:], MUL, m, y, last)
                slots.give(s, mt)
                yield
                g["Dm"] = y
                g["MTm"] = mt
                m1 = LEV[1 - d][0]
                a = tt(q, v8(g["Y"][:]), v8(g["MT"][:]), bc8(m1), MUL, mt, last)
                yield
                a = tt(dve, v8(g["Y"][:]), bc8(IDENT), v8(g["Y"][:]), SUB, a)
                g["Ym"] = a
                s, p, fr = slots.take()
                for t in range(8):
                    c = slice(t * 128, t * 128 + 128)
                    m = tr(p[:, c], g["Y"][:, c], a, fr)
                g["Xm"] = copy(act, g["X"][:], p, m, last)
                slots.give(s, g["Xm"])
                yield
                g["vbm"] = tt(pool, v8(g["vb"][:]), v8(hb["vt"][:]), bcl(beta[:, :, hd]), MUL, hb["vtm"], last)
                g["kbm"] = tt(pool, v8(g["kb"][:]), v8(hb["kt"][:]), bcl(bg[:, :, hd]), MUL, hb["ktm"], last)
                yield

            def prep_intra(hb, pair):
                s, p, fr = slots.take()
                for t in range(8):
                    c = slice(t * 128, t * 128 + 128)
                    m = mm(p[:, c], hb["k"][:, c], hb["q"][:, c], True, True, fr, hb["qm"], hb["km"])
                for g in pair:
                    g["Im"] = tt(dve, g["D"][:], p, g["D"][:], MUL, m, g["Dm"], g["MTm"])
                slots.give(s, *[g["Im"] for g in pair])
                yield

            def level(l, gs):
                todo = []
                for d, g in gs:
                    s, p, fr = mslots.take()
                    for t in range(8):
                        c = slice(t * 128, t * 128 + 128)
                        m = mm(p[:, c], g["MT"][:, c], g["X"][:, c], True, True, g["MTm"], g["Xm"], fr)
                    i, b, f = P1.take()
                    a = tt(dve, v8(b[:]), v8(p), bc8(LEV[d][l]), MUL, m, f)
                    mslots.give(s, a)
                    todo.append((i, b, a))
                yield 2
                for (d, g), (i, b, a) in zip(gs, todo):
                    m2 = None
                    if l < 5:
                        s2, p2, fr2 = mslots.take()
                        for t in range(8):
                            c = slice(t * 128, t * 128 + 128)
                            m2 = mm(p2[:, c], g["Y"][:, c], b[:, c], True, True, a, g["Ym"], fr2)
                        g["Xm"] = tt(dve, g["X"][:], g["X"][:], p2, SUB, m2)
                        mslots.give(s2, g["Xm"])
                    s, p, fr = mslots.take()
                    for t in range(8):
                        c = slice(t * 128, t * 128 + 128)
                        m = mm(p[:, c], b[:, c], g["Y"][:, c], True, True, a, g["Ym"], fr)
                    g["Ym"] = tt(dve, g["Y"][:], g["Y"][:], p, SUB, m)
                    P1.give(i, m)
                    mslots.give(s, g["Ym"])
                    yield 1

            def apply(g, hb, hd):
                s, p, fr = mslots.take()
                for t in range(8):
                    c = slice(t * 128, t * 128 + 128)
                    m = mm(p[:, c], g["Y"][:, c], g["vb"][:, c], True, True, g["Ym"], g["vbm"], fr)
                g["um"] = copy(act, g["vb"][:], p, m)
                mslots.give(s, g["um"])
                s, p, fr = mslots.take()
                for t in range(8):
                    c = slice(t * 128, t * 128 + 128)
                    m = mm(p[:, c], g["kb"][:, c], g["Y"][:, c], True, True, g["kbm"], fr)
                g["wm"] = copy(dve, g["kb"][:], p, m)
                mslots.give(s, g["wm"])
                g["kdm"] = tt(pool, v8(g["MT"][:]), v8(hb["kt"][:]), bcl(ed[:, :, hd]), MUL, g["Ym"], hb["ktm"])

            def scan(gs, hb):
                banks = Ring([ps[:, i, :] for i in range(6)])
                for i in range(6):
                    banks.free[i] = list(mslots.free[i // 2])
                for _, g in gs:
                    g["Sm"] = memset(dve, g["S"][:], 0.0, hb["last"], list(scanned))
                    g["vfree"] = hb["last"] + scanned
                seen = {}
                hb["Om"] = []
                for n in range(16):
                    work = []
                    for d, g in gs:
                        ch = n if d == 0 else 15 - n
                        t, j = ch // 2, ch % 2
                        r, c, cc = slice(64 * j, 64 * j + 64), slice(64 * ch, 64 * ch + 64), slice(128 * t, 128 * t + 128)
                        i, p, fr = banks.take()
                        m = mm(p[r, 0:128], g["kb"][:, c], g["S"][:], True, True, g["wm"], g["Sm"], fr)
                        v = tt(dve, g["vn"][r, :], g["vb"][r, cc], p[r, 0:128], SUB, m, g["um"], g["vfree"])
                        banks.give(i, v)
                        work.append((d, g, ch, r, c, cc, v))
                    outs = []
                    for d, g, ch, r, c, cc, v in work:
                        i, p, fr = banks.take()
                        mm(p[:, 0:64], g["S"][:], g["qg"][:, c], True, False, g["qgm"], fr)
                        outs.append((i, p))
                    for (d, g, ch, r, c, cc, v), (i, p) in zip(work, outs):
                        i2, p2, fr2 = banks.take()
                        ms = mm(p2[:, 0:128], g["MT"][r, cc], g["vn"][r, :], True, True, v, g["kdm"], fr2)
                        mo = mm(p[:, 0:64], g["vn"][r, :], g["D"][r, c], False, True, v, g["Im"])
                        g["vfree"] = mo
                        g["Sm"] = stt(g["S"][:], g["S"][:], g["egl"][:, ch:ch + 1], p2[:, 0:128], MUL, ADD, ms,
                                      g["eglm"], g["Sm"])
                        banks.give(i2, g["Sm"])
                        if ch not in seen:
                            seen[ch] = copy(act, hb["O"][:, c], p[:, 0:64], mo, hb["last"])
                        else:
                            seen[ch] = tt(dve, hb["O"][:, c], hb["O"][:, c], p[:, 0:64], ADD, mo, seen[ch])
                        hb["Om"].append(seen[ch])
                        banks.give(i, seen[ch])
                    yield 1
                for i in range(3):
                    mslots.free[i] = banks.free[2 * i] + banks.free[2 * i + 1]
                hb["scan_end"] = [mo, ms] + [g["Sm"] for _, g in gs]
                scanned[:] = hb["scan_end"]

            def finish_head(h, hb, pair):
                sq, aux, c, z = pair[0]["X"], pair[1]["X"], pair[0]["Y"], pair[1]["Y"]
                lm = load(f"dz{h % 2}", z[:], pj[28 + h], hb["scan_end"])
                a = actf(sq[:], hb["O"], ACT.Square, hb["Om"], hb["scan_end"])
                s, p, fr = slots.take()
                for half in range(2):
                    cc = slice(half * 512, half * 512 + 512)
                    m = mm(p[:, cc], ONES, sq[:, cc], True, True, a, fr)
                yield
                a, r = neg2_rsqrt(sq[:], aux[:], p, 1.0 / 128, "eps", EPS, m)
                slots.give(s, a)
                yield
                m = stt(c[:], hb["O"], NH("dnw"), sq[:], MUL, MUL, r)
                m2 = tt(pool, X[:, 4 + h, :], c[:], z[:], MUL, m, lm)
                hb["last"] = [r, m, m2] + hb["scan_end"]
                yield

            def prepare(h):
                hb, pair = heads[h % 2], hds[2 * (h % 2):2 * (h % 2) + 2]
                yield from prep_head(h, hb, hb["last"])
                for d in range(2):
                    yield from prep_dir(h, d, hb, pair[d], hb["last"])
                yield from prep_intra(hb, pair)

            def main(h):
                hb, pair = heads[h % 2], hds[2 * (h % 2):2 * (h % 2) + 2]
                gs = [(d, pair[d]) for d in range(2)]
                for l in range(1, 6):
                    yield from level(l, gs)
                for d in range(2):
                    apply(pair[d], hb, h + 4 * d)
                    yield 1
                hb["O"] = X[:, 4 + h, :]
                yield from scan(gs, hb)

            for hb in heads:
                hb["last"] = []
            for _ in prep_head(0, heads[0], []):
                pass
            two = [prep_dir(0, d, heads[0], hds[d], [], dve) for d in range(2)]
            while two:
                two = [g for g in two if next(g, "end") != "end"]
            for _ in prep_intra(heads[0], hds[0:2]):
                pass
            for i in range(3):
                mslots.free[i] = slots.free[i]
            old = slots.free[3]
            slots = Ring([slot(3)])
            slots.free[0] = old
            for h in range(4):
                back = []
                if h > 0:
                    back.append(finish_head(h - 1, heads[(h - 1) % 2], hds[2 * ((h - 1) % 2):2 * ((h - 1) % 2) + 2]))
                if h < 3:
                    back.append(prepare(h + 1))
                for n in main(h):
                    for _ in range(n):
                        if back and next(back[0], "end") == "end":
                            back.pop(0)
                for b in back:
                    for _ in b:
                        pass
            for _ in finish_head(3, heads[1], hds[2:4]):
                pass
            fence()

    class Backbone:

        def __init__(self, st):
            self.x = X
            self.acc, self.sq, self.rs = (sb(st, [128, L]) for _ in range(3))
            self.accf, self.sqf, self.rsf = [], [], []
            self.xm = [[] for _ in range(KC)]
            self.ready = [[] for _ in range(KC)]

        def open(self):
            self.pair = ExitStack()
            self.H, self.Lo = sb(self.pair, [128, KC, L], R), sb(self.pair, [128, KC, L], R)

        def squares(self, k):
            if k == 0:
                self.accm = actf(self.acc[:], self.x[:, k, :], ACT.Square, self.xm[k], self.accf)
                return
            a = actf(self.sq[:], self.x[:, k, :], ACT.Square, self.xm[k], self.sqf)
            self.accm = tt(pool, self.acc[:], self.acc[:], self.sq[:], ADD, a, self.accm)
            self.sqf = [self.accm]

        def operand(self, k, wname, free):
            w = NH(wname, k)
            a = actf(self.H[:, k, :], self.x[:, k, :], ACT.Copy, self.xm[k], free, scale=w)
            b = stt(self.Lo[:, k, :], self.x[:, k, :], w, self.H[:, k, :].bitcast(F), MUL, SUB, a)
            self.ready[k] = [a, b]

        def factor(self):
            s, p, free = slots.take()
            for half in range(2):
                c = slice(half * 512, half * 512 + 512)
                m = mm(p[:, c], ONES, self.acc[:, c], True, True, self.accm, free)
            self.accf = [m]
            a, self.rm = neg2_rsqrt(self.rs[:], self.sq[:], p, 1.0 / D, "eps", EPS, m, self.sqf, self.rsf)
            self.sqf, self.rsf = [self.rm], []
            slots.give(s, a)

        def tile(self, first):
            todo = [self.factor] if first else []
            return linear_tile(self.H, self.Lo, self.ready, tick=lambda: todo and todo.pop()(), order=self.order)

        def scaled(self, out, p, *after):
            m = tt(dve, out, p, self.rs[:], MUL, self.rm, *after)
            self.rsf = [m]
            return m

    def phase_outproj(B, load_src, wname, order=tuple(range(KC))):
        B.order = order
        for k in order:
            b, m, give = load_src(k)
            B.ready[k] = split(B.H[:, k, :], B.Lo[:, k, :], b, m, q=dve if k % 2 else pool)
            give(*B.ready[k])
            if k == 1 and not W.spq:
                W.split_one()
        for m in range(KC):
            s, p, done = B.tile(False)
            B.xm[m] = tt(dve, B.x[:, m, :], B.x[:, m, :], p, ADD, done, B.xm[m])
            slots.give(s, B.xm[m])
            B.squares(m)
        B.order = tuple(range(KC))
        for k in range(KC):
            B.operand(k, wname, done)

    def phase_ffn(B, after, spare=None):
        x, H, Lo, ready, xready = B.x, B.H, B.Lo, B.ready, B.xm
        with ExitStack() as st:
            AB = Ring([(sb(st, [128, L], R), sb(st, [128, L], R)) for _ in range(5)])
            bufs = spare or [sb(st, [128, L]) for _ in range(3)]
            sg, ab = Ring(bufs[0:1]), Ring(bufs[1:3])
            tiles, count, gated = [], [], []

            def gate_up():
                s1, pg, mg = B.tile(not count)
                count.append(1)
                s2_, pu, mu = linear_tile(H, Lo, ready)
                i, g, f = sg.take()
                a = B.scaled(g[:], pg, mg, f)
                slots.give(s1, a)
                a = actf(g[:], g[:], ACT.Silu, a)
                gated.append(mu)
                k, b, f = ab.take()
                m = B.scaled(b[:], pu, mu, f)
                slots.give(s2_, m)
                m = tt(dve, b[:], b[:], g[:], MUL, m, a)
                sg.give(i, m)
                n, (ah, al), f = AB.take()
                marks = split(ah[:], al[:], b[:], m, f)
                ab.give(k, *marks)
                tiles.append((n, ah, al, marks))

            def down(nk, final):
                grp = tiles[:nk]
                del tiles[:nk]
                for mp in range(4):
                    wh, wl, wm = W.get()
                    for m in range(2):
                        s, p, fr = slots.take()
                        for half in range(2):
                            c = slice(half * 512, half * 512 + 512)
                            for k, (n, ah, al, marks) in enumerate(grp):
                                a = slice((k * 2 + m) * 128, (k * 2 + m) * 128 + 128)
                                last = mm3(p[:, c], (wh[:, a], wl[:, a]), (ah[:, c], al[:, c]),
                                           k == 0, k == nk - 1, wm, fr, marks)
                        o = 2 * mp + m
                        xready[o] = stt(x[:, o, :], p, 0.5, x[:, o, :], MUL, ADD, last, xready[o])
                        slots.give(s, xready[o])
                        if final:
                            B.squares(o)
                            if after:
                                B.operand(o, after, gated[-1])
                    W.done(last)
                for n, _, _, _ in grp:
                    AB.give(n, last)

            for _ in range(GROUPS[0]):
                gate_up()
            for g, nk in enumerate(GROUPS):
                if g + 1 < len(GROUPS):
                    gate_up()
                down(nk, g + 1 == len(GROUPS))
                if g + 1 < len(GROUPS):
                    for _ in range(GROUPS[g + 1] - 1):
                        gate_up()
            fence(writers_only=True)

    def phase_mix2(B, outer):
        nonlocal slots_s
        with ExitStack() as st:
            UH, UL = sb(st, [128, 4, L], R), sb(st, [128, 4, L], R)
            um = [None] * 4
            with ExitStack() as s2:
                tmp = Ring([sb(s2, [128, L]) for _ in range(3)])
                for m in range(10):
                    s, p, hdone = B.tile(m == 0)
                    i, b, f = tmp.take()
                    a = B.scaled(b[:], p, hdone, f)
                    slots.give(s, a)
                    if m < 4:
                        um[m] = split(UH[:, m, :], UL[:, m, :], b[:], a, q=dve)
                        tmp.give(i, *um[m])
                    else:
                        tmp.give(i, store(f"q2{i}", pj[m - 4], b[:], a))
                fence(writers_only=True)
            with ExitStack() as s2:
                alt = sb(s2, [128, 2], R)
                y5 = sb(s2, [128, 8])
                am = load("alt", y5[:, 0:2], A["alt"])
                TH, TL = (b[:].rearrange("p t (g n) -> p t g n", g=4) for b in (B.H, B.Lo))
                wh, wl, wm = W.get()
                tm = []
                for t in range(8):
                    s, p, fr = slots.take()
                    c = slice(t * 128, t * 128 + 128)
                    for g in range(4):
                        m = mm3(p[:, g * 256:g * 256 + 256], (UH[:, g, c], UL[:, g, c]),
                                (wh[:, 0:256], wl[:, 0:256]), True, True, fr, wm, um[g])
                    marks = split(TH[:, t, :, :].rearrange("p g n -> p (g n)"),
                                  TL[:, t, :, :].rearrange("p g n -> p (g n)"), p, m, hdone, q=dve)
                    tm.append(marks)
                    slots.give(s, *marks)
                W.done(m)
                am = actf(alt[:], y5[:, 0:2], ACT.Copy, am)
                s, p, fr = slots.take()
                for g in range(4):
                    for t in range(8):
                        mm(p[:, 2 * g:2 * g + 2], TH[:, t, g, 0:128], alt[:], t == 0, False, tm[t], am, fr)
                        m = mm(p[:, 2 * g:2 * g + 2], TL[:, t, g, 0:128], alt[:], False, t == 7)
                y5m = actf(y5[:], p[:, 0:8], ACT.Copy, m, am, scale=float(1.0 / np.sqrt(L * 128.0)))
                slots.give(s, y5m)
                taken = [slots.take() for _ in range(4)]
                for t in range(8):
                    wh, wl, wm = W.get()
                    for g in range(4):
                        s, p, fr = taken[g]
                        for d in range(2):
                            a, b = slice(d * 128, d * 128 + 128), slice(d * 512, d * 512 + 512)
                            m = mm3(p[:, b], (TH[:, t, g, a], TL[:, t, g, a]), (wh[:, b], wl[:, b]),
                                    t == 0, t == 7, fr, wm, tm[t])
                    W.done(m)
                wh, wl, wm = W.get()
                cs = Ring([sb(s2, [128, 512]) for _ in range(2)])
                yb = Ring([sb(s2, [128, L]) for _ in range(2)])
                ym = []
                for g in range(4):
                    s, p, _ = taken[g]
                    i, b, f = cs.take()
                    a = copy(act, b[:], p[:, 0:512], m, f)
                    k, y, f = yb.take()
                    a1 = tt(dve, y[:, 0:512], b[:], p[:, 512:1024], SUB, a, f)
                    a2 = tt(dve, y[:, 1023:512:-1], b[:, 1:512], p[:, 513:1024], ADD, a, f)
                    a3 = copy(dve, y[:, 512:513], y5[:, 2 * g:2 * g + 1], y5m, f)
                    slots.give(s, a1, a2)
                    cs.give(i, a1, a2)
                    ym.append(split(UH[:, g, :], UL[:, g, :], y[:], a1, a2, a3, m))
                    yb.give(k, *ym[g])
                for g in range(4):
                    s, p, fr = slots.take()
                    for half in range(2):
                        c = slice(half * 512, half * 512 + 512)
                        a = slice(g * 128, g * 128 + 128)
                        m = mm3(p[:, c], (wh[:, a], wl[:, a]), (UH[:, g, c], UL[:, g, c]), True, True,
                                fr, wm, ym[g])
                    k, y, f = yb.take()
                    a = ts(dve, y[:], p, C("fb", g), None, ADD, None, m, f)
                    slots.give(s, a)
                    yb.give(k, store(f"yb{k}", mixd2[g], y[:], a))
                W.done(m)
                fence()
        B.pair.close()
        gq = sb(outer, [128, 4, L])
        with ExitStack() as st:
            slots_s = Ring([slot(0), slot(1)])
            cs_ = sb(st, [128, 2, L])
            rp = sb(st, [128, 128])
            rm = []
            big = Ring([B.acc, B.sq, B.rs])
            raws = Ring([sb(st, [128, L]) for _ in range(1)])
            KV = [sb(st, [128, L], R) for _ in range(2)]
            VH, VL = (sb(st, [128, 8, 2, 128], R) for _ in range(2))
            Q = Ring([tuple(sb(st, [128, L], R) for _ in range(2)) for _ in range(2)])
            one, zero = (b[:, 0:512].rearrange("p (a n) -> p a n", a=8) for b in big.bufs[0:2])
            om = [memset(dve, one, 1.0), memset(dve, zero, 0.0)]
            vi = value_ones(VH, VL, one, zero, om)
            big.free = [list(vi), list(vi), []]
            rope = (cs_[:, 0, :], cs_[:, 1, :], rp[:])

            def fetch(row):
                i, b, f = raws.take()
                return i, b, load(f"gq{i}", b[:], pj[row], f)

            chunks = {}

            def prep(c):
                i, b, lm = fetch(2 + c)
                qi, (qh, ql), f = Q.take()
                ready = []

                def done(marks, last):
                    raws.give(i, last)
                    ready.extend(marks)
                yield from head_norm(big, b[:], "qn", "eps64", 1.0, lm, qh, ql, f, done, rope)
                chunks[c] = dict(qi=qi, q=(qh, ql), ready=ready + km + vm + vi)

            km = []
            with ExitStack() as s3:
                big0 = Ring([sb(s3, [128, L]) for _ in range(3)])
                first = [sb(s3, [128, L]) for _ in range(3)]
                lms = [load(f"gf{n}", first[n][:], pj[n]) for n in range(3)]
                rm.extend([load("rp", rp[:], A["rperm"]), load("cs", cs_[:], A["rope"])])
                qi, (qh, ql), f = Q.take()
                q0 = []
                kgen = head_norm(big0, first[0][:], "kn", "eps", 1.0 / 64, [lms[0]] + rm, KV[0], KV[1], None,
                                 lambda marks, last: km.extend(marks), rope)
                qgen = head_norm(big, first[2][:], "qn", "eps64", 1.0, [lms[2]] + rm, qh, ql, f,
                                 lambda marks, last: q0.extend(marks), rope)
                next(kgen)
                next(qgen)
                vm = value_tiles(first[1], lms[1], VH, VL, None)
                two = [kgen, qgen]
                while two:
                    two = [g for g in two if next(g, "end") != "end"]
                chunks[0] = dict(qi=qi, q=(qh, ql), ready=q0 + km + vm + vi)
                fence(writers_only=True)

            units = [dict(c=c, j=j, t=t, nk=1024, k0=0, base=0) for c in range(4) for j in range(2) for t in range(8)]
            state = {}

            def bind(c):
                ch = chunks[c]
                for u in units[16 * c:16 * c + 16]:
                    j = u["j"]
                    u["q"], u["k"], u["v"], u["bias"] = ch["q"], tuple(KV), (VH, VL), None
                    u["ready"] = lambda ch=ch: ch["ready"]
                    u["last_scores"] = (lambda m, ch=ch: Q.give(ch["qi"], m)) if (u["t"] == 7 and j == 1) else None

                    u["out"] = lambda hf, c=c: (gq[:, c, :], [])
                    u["finish"] = lambda z, m: None

            background = []

            def drain():
                while background:
                    for _ in background.pop(0):
                        pass
            prep_at = {0: lambda: (drain(), bind(0))}
            for c in range(1, 4):
                prep_at[16 * c - 13] = lambda c=c: background.append(prep(c))
                prep_at[16 * c] = lambda c=c: (drain(), bind(c))
            attention(units, st, prep_at, background, 8)
            fence()
        return gq

    def fetch(ring, src, k):
        i, b, f = ring.take()
        m = load(f"op{i}", b[:], src[k], f)
        return b[:], m, lambda *marks: ring.give(i, *marks)

    phase_inproj()
    phase_na()
    pre.close()
    phase_delta()
    gates.close()
    with ExitStack() as st:
        W.open(st, A["wts"].shape[0])
        B = Backbone(st)
        B.open()
        def reload(k):
            def give(*marks):
                B.xm[k] = load(f"x{k}", X[:, k, :], A["xT"][k], *marks)
            return X[:, k, :], [], give
        phase_outproj(B, reload, "ffn1")
        phase_ffn(B, "mixn")
        gq = phase_mix2(B, st)
        B.open()
        with ExitStack() as s2:
            tmp = Ring([sb(s2, [128, L]) for _ in range(4)])
            srcs = [fetch(tmp, mixd2, k) for k in range(4)]
            srcs += [(gq[:, c, :], [], lambda *marks: None) for c in range(4)]
            phase_outproj(B, lambda k: srcs[k], "ffn2", (4, 5, 6, 7, 0, 1, 2, 3))
            fence(writers_only=True)
        phase_ffn(B, None, [gq[:, c, :] for c in range(3)])
        B.pair.close()
        with ExitStack() as s2:
            B.factor()
            ring = Ring([sb(s2, [128, L]) for _ in range(4)])
            for k in range(KC):
                i, b, f = ring.take()
                m = stt(b[:], B.x[:, k, :], NH("fin", k), B.rs[:], MUL, MUL, B.rm, B.xm[k], f)
                ring.give(i, store(f"fo{i}", A["out"][k], b[:], m))
            fence()
    if "dbg" in A:
        for n, (dst, src) in enumerate(((A["dbg"][0], pj), (A["dbg"][2], mixd2))):
            store(f"dbg{n}", dst, src)
    assert W.next == A["wts"].shape[0], (W.next, A["wts"].shape)
    sp.items.append((flat(out_marks), None, Mark(sp)))

    for q in engines + [sp]:
        q.number()
    with top:
        block = top.enter_context(nc.Block())

        @block.sync
        def _(e):
            sp.emit(e)

        @block.scalar
        def _(e):
            act.emit(e)

        @block.vector
        def _(e):
            dve.emit(e)

        @block.gpsimd
        def _(e):
            pool.emit(e)

        @block.tensor
        def _(e):
            pe.emit(e)


def _tiles(w, pad_to=None):
    K, M = w.shape
    return np.ascontiguousarray(w.reshape(K // 128, 128, M // 128, 128).transpose(2, 1, 0, 3)).reshape(M // 128, 128, K)


def _layout(inputs):
    f = np.float32
    I = {k: np.asarray(v) for k, v in inputs.items()}
    cols, ncst = const_columns()
    cst = np.zeros((128, ncst), f)

    def put(name, a):
        at, n = cols[name]
        cst[:, at:at + n] = a
    for name, src in (("norm1", I["norm_w"][0]), ("ffn1", I["ffn1_norm_2"]), ("mixn", I["mix_norm_2"]),
                      ("ffn2", I["ffn2_norm_2"]), ("fin", I["final_norm_2"])):
        put(name, src.reshape(8, 128).T)
    two = lambda a: np.concatenate([a, a])[:, None]
    put("gq", two(I["qk_gain_q"][0]))
    put("gk", two(I["qk_gain_k"][0]))
    put("qn", two(I["q_norm_2"]))
    put("kn", two(I["k_norm_2"]))
    put("conv", I["conv_w"][0].reshape(5, 12, 128).transpose(2, 1, 0).reshape(128, 60))
    cst[32:40, cols["alog"][0]] = I["a_log"][0].reshape(8)
    cst[32:40, cols["dtb"][0]] = I["dt_bias"][0].reshape(8)
    put("dnw", I["dn_norm_w"][0][:, None])
    put("fb", I["fnet_b_2"].T)
    put("eps", EPS)
    put("eps64", 64 * EPS)
    put("eps128", 128 * EPS)
    put("one", 1.0)
    put("ident", np.eye(128, dtype=f))
    put("ones", 1.0)
    blk = np.arange(128) // 64
    same = blk[:, None] == blk[None, :]
    put("bones", same.astype(f))
    i = np.arange(128)
    put("tri", np.concatenate([same & (i[:, None] <= i[None, :]), same & (i[:, None] >= i[None, :])], 1).astype(f))

    w_in = I["w_in"][0]
    gates = np.zeros((D, 128), f)
    g16 = w_in[:, 4096:4112]
    gates[:, 0:4], gates[:, 4:8] = g16[:, 0:4], g16[:, 8:12]
    gates[:, 32:36], gates[:, 36:40] = g16[:, 4:8], g16[:, 12:16]
    parts = [_tiles(np.concatenate([w_in[:, :4096], gates], 1))[IN_ORDER], _tiles(I["w_out"][0])]

    def ffn(g, u, d):
        pad = lambda a: np.concatenate([a, np.zeros((D, FT * 128 - FF), f)], 1)
        tg, tu = _tiles(pad(g)), _tiles(pad(u))
        dp = np.concatenate([d, np.zeros((FT * 128 - FF, D), f)], 0).reshape(FT, 128, 4, 256)
        out = []
        at = 0

        def gu(n):
            for _ in range(n):
                i = sum(1 for o in out if o[1] == "g")
                out.append((tg[i:i + 1], "g"))
                out.append((tu[i:i + 1], "u"))
        gu(GROUPS[0])
        for g_, nk in enumerate(GROUPS):
            if g_ + 1 < len(GROUPS):
                gu(1)
            for mp in range(4):
                t = np.zeros((1, 128, 1024), f)
                t[0, :, :nk * 256] = dp[at:at + nk, :, mp, :].transpose(1, 0, 2).reshape(128, nk * 256)
                out.append((t, "d"))
            at += nk
            if g_ + 1 < len(GROUPS):
                gu(GROUPS[g_ + 1] - 1)
        return [o[0] for o in out]

    parts += ffn(I["ffn1_w_gate_2"], I["ffn1_w_up_2"], I["ffn1_w_down_2"])
    w2 = I["w_in_2"]
    wf, wq, wk, wv = w2[:, :512], w2[:, 512:1024], w2[:, 1024:1152], w2[:, 1152:1280]
    heads = np.array([[c, c + 4] for c in range(4)]).reshape(-1)
    wq = wq.reshape(D, 8, 64)[:, heads].reshape(D, 512)
    parts += [_tiles(wf), _tiles(wk), _tiles(wv), _tiles(wq)]
    n = np.arange(128)
    ang = 2 * np.pi * ((n[:, None] * n[None, :]) % 128) / 128
    x1 = np.zeros((1, 128, 1024), f)
    x1[0, :, 0:128], x1[0, :, 128:256] = np.cos(ang), np.sin(ang)
    t, s = np.arange(L), np.arange(512)
    ang = 2 * np.pi * ((t[:, None] * s[None, :]) % L) / L
    sc = 1.0 / np.sqrt(L * 128.0)
    tab = np.concatenate([np.cos(ang) * sc, np.sin(ang) * sc], 1).astype(f).reshape(8, 128, 1024)
    x2 = np.zeros((1, 128, 1024), f)
    x2[0, :, 0:512] = I["fnet_w_2"].transpose(1, 0, 2).reshape(128, 512)
    wo2 = I["w_out_2"]
    wo2 = np.concatenate([wo2[:512], wo2[512:].reshape(8, 64, D)[heads].reshape(512, D)], 0)
    parts += [x1, tab, x2, _tiles(wo2)]
    parts += ffn(I["ffn2_w_gate_2"], I["ffn2_w_up_2"], I["ffn2_w_down_2"])
    wts = np.concatenate(parts, 0)

    rpb = I["rpb"][0]
    c, kc = np.arange(64), np.arange(64)
    lo = np.clip(c - 8, 0, 48)
    ok = (kc[None, :] >= lo[:, None]) & (kc[None, :] < lo[:, None] + 16)
    dc = np.clip(kc[None, :] - c[:, None] + 15, 0, 30)
    full = rpb[:, :, dc]
    tabs = np.full((8, 128, 23, 64), NEG, f)
    for half in range(2):
        r = slice(64 * half, 64 * half + 64)
        for i in range(14):
            tabs[:, r, i, :] = np.where(ok[None], full[:, i + 1 - half], f(NEG))
        for i in range(9):
            dr = i + 3 - half
            if 3 <= dr <= 10:
                tabs[:, r, 14 + i, :] = np.where(ok[None], full[:, dr], f(NEG))
    i = np.arange(128)
    dm = np.zeros((128, 12, 128), f)
    for l in range(6):
        b = 1 << l
        low = (i[:, None] // (2 * b) == i[None, :] // (2 * b)) & (i[:, None] % (2 * b) >= b) & (i[None, :] % (2 * b) < b)
        dm[:, l] = low
        dm[:, 6 + l] = low.T
    inv = (np.float32(10000.0) ** (-np.arange(0, 32, 2, dtype=f) / np.float32(32))).astype(f)
    tok = np.arange(L)
    ar = (tok // 64).astype(f)[None, :] * inv[:, None]
    ac = (tok % 64).astype(f)[None, :] * inv[:, None]
    ang = np.concatenate([ar, ar, ac, ac] * 2, 0)
    rope = np.stack([np.cos(ang), np.sin(ang)], 1).astype(f)
    rp = np.zeros((128, 128), f)
    for p in range(128):
        if p % 32 < 16:
            rp[p + 16, p] = -1.0
        else:
            rp[p - 16, p] = 1.0
    alt = np.zeros((128, 2), f)
    alt[:] = (1.0 - 2.0 * (i % 2))[:, None]
    return dict(xT=np.ascontiguousarray(I["x"][0].T).reshape(8, 128, L), cst=cst, wts=wts,
                rpb=tabs.reshape(8, 128, 23 * 64), dmask=dm, rope=rope, rperm=rp, alt=alt)


DBG = False


def kernel(**inputs):
    import concourse.bacc as _bacc
    from concourse import mybir as _mybir
    from concourse.bass_utils import run_bass_kernel_spmd as _run

    nc = _bacc.Bacc("TRN2", target_bir_lowering=False, num_devices=1)
    arrays, A = {}, {}
    for name, a in _layout(inputs).items():
        a = np.ascontiguousarray(a)
        arrays[f"in_{name}_dram"] = a
        A[name] = nc.dram_tensor(f"in_{name}_dram", a.shape, _mybir.dt.from_np(a.dtype), kind="ExternalInput").ap()
    A["out"] = nc.dram_tensor("out_0_dram", (8, 128, L), _mybir.dt.float32, kind="ExternalOutput").ap()
    if DBG:
        A["dbg"] = [nc.dram_tensor(f"dbg{i}", (n, 128, L), _mybir.dt.float32, kind="ExternalOutput").ap()
                    for i, n in enumerate((33, 8, 8))]
    build(nc, A)
    r = _run(nc, [arrays], core_ids=[0])
    out = np.ascontiguousarray(np.asarray(r.results[0]["out_0_dram"]).reshape(D, L).T).reshape(1, L, D)
    if DBG:
        return tuple([out] + [np.asarray(r.results[0][f"dbg{i}"]) for i in range(3)])
    return out
```
